# Optimizing a Trainium2 kernel written in Bass

```python
import math
import jax, jax.numpy as jnp
from jax import lax
import numpy as np

D_MODEL = 1024
BATCH = 1
SEQ = 128
DEPTH = 2
DEC_BATCH = 1
DEC_SEQ = 2048
PAST_LEN = 128

GRID_W = 64
D_MIX = D_MODEL
BRANCH_W = D_MIX // 4
Q_BLOCK = 128
ROPE_THETA = 10000.0
EPS = 1e-6

MLA_V = 64
MLA_HEADS = BRANCH_W // MLA_V
MLA_NOPE = 64
MLA_ROPE = 32
MLA_QK = MLA_NOPE + MLA_ROPE
MLA_Q_RANK = 192
MLA_KV_RANK = 128
MLA_W = MLA_HEADS * MLA_V

SSD_P = 64
SSD_HEADS = BRANCH_W // SSD_P
SSD_W = SSD_HEADS * SSD_P
SSD_GROUPS = 2
SSD_N = 64
SSD_CONV = 3
SSD_CHUNK = 128
SSD_CONV_CH = SSD_W + 2 * SSD_GROUPS * SSD_N

CF_W = BRANCH_W
CF_K = 31

GQA_HD = 64
GQA_HEADS = BRANCH_W // GQA_HD
GQA_KV_HEADS = 2
GQA_W = GQA_HEADS * GQA_HD

SPLITS = (MLA_Q_RANK, MLA_KV_RANK, MLA_ROPE, MLA_W,
          SSD_CONV_CH, 2 * SSD_HEADS, SSD_W,
          CF_W, CF_W, CF_W,
          GQA_W, GQA_KV_HEADS * GQA_HD, GQA_KV_HEADS * GQA_HD, GQA_W)
IN_W = sum(SPLITS)

kernel_name = 'hybrid_diffusion_mla_ssd_conformer_gqa'

def split_proj(u):
    outs = []
    o = 0
    for s in SPLITS:
        outs.append(u[..., o:o + s])
        o += s
    return outs

def rms_norm(x, g):
    xf = x.astype(jnp.float32)
    y = xf * lax.rsqrt(jnp.mean(xf * xf, axis=-1, keepdims=True) + EPS)
    return (y * g.astype(jnp.float32)).astype(x.dtype)

def layer_norm(x, g, b):
    xf = x.astype(jnp.float32)
    mu = jnp.mean(xf, axis=-1, keepdims=True)
    var = jnp.mean(jnp.square(xf - mu), axis=-1, keepdims=True)
    y = (xf - mu) * lax.rsqrt(var + EPS)
    return (y * g.astype(jnp.float32) + b.astype(jnp.float32)).astype(x.dtype)

def dwconv(x, w, b):
    k = w.shape[0]
    y = lax.conv_general_dilated(x, w[:, None, :], window_strides=(1,),
                                 padding=[(k // 2, k // 2)],
                                 dimension_numbers=('NWC', 'WIO', 'NWC'),
                                 feature_group_count=x.shape[-1])
    return y + b

def axial_rope_tables(n_tokens, dim):
    n_rows = n_tokens // GRID_W
    row = jnp.repeat(jnp.arange(n_rows), GRID_W).astype(jnp.float32)
    col = jnp.tile(jnp.arange(GRID_W), n_rows).astype(jnp.float32)
    quarter = dim // 4
    inv = ROPE_THETA ** (-jnp.arange(quarter, dtype=jnp.float32) / quarter)
    ar = row[:, None] * inv
    ac = col[:, None] * inv
    ang = jnp.concatenate([ar, ar, ac, ac], axis=-1)
    return jnp.cos(ang), jnp.sin(ang)

def apply_axial_rope(x, cos, sin):
    q = x.shape[-1] // 4
    x1, x2, x3, x4 = x[..., :q], x[..., q:2 * q], x[..., 2 * q:3 * q], x[..., 3 * q:]
    xrot = jnp.concatenate([-x2, x1, -x4, x3], axis=-1)
    return x * cos[:, None, :].astype(x.dtype) + xrot * sin[:, None, :].astype(x.dtype)

def block_attention(q, k, v, scale):
    b, sq, h, dk = q.shape
    hk = k.shape[2]
    rep = h // hk
    dv = v.shape[-1]
    nb = sq // Q_BLOCK
    qb = jnp.moveaxis(q.reshape(b, nb, Q_BLOCK, hk, rep, dk), 1, 0)

    def one_block(qblk):
        s = jnp.einsum('bqgrd,bkgd->bgrqk', qblk, k).astype(jnp.float32) * scale
        p = jax.nn.softmax(s, axis=-1).astype(v.dtype)
        return jnp.einsum('bgrqk,bkgd->bqgrd', p, v)

    o = lax.map(one_block, qb)
    return jnp.moveaxis(o, 0, 1).reshape(b, sq, h, dv)

def mla_queries(q_lat, q_norm_g, w_uq, q_head_g, rope):
    b, L, _ = q_lat.shape
    q = (rms_norm(q_lat, q_norm_g) @ w_uq).reshape(b, L, MLA_HEADS, MLA_QK)
    q = rms_norm(q, q_head_g)
    if rope is not None:
        q = jnp.concatenate([q[..., :MLA_NOPE], apply_axial_rope(q[..., MLA_NOPE:], *rope)], axis=-1)
    return q

def mla_keys(ckv, krope, w_ukv, k_head_g, rope):
    b, L, _ = ckv.shape
    kv = (ckv @ w_ukv).reshape(b, L, MLA_HEADS, MLA_NOPE + MLA_V)
    k_nope, v = kv[..., :MLA_NOPE], kv[..., MLA_NOPE:]
    k = jnp.concatenate([k_nope, jnp.broadcast_to(krope[:, :, None, :], (b, L, MLA_HEADS, MLA_ROPE))], axis=-1)
    k = rms_norm(k, k_head_g)
    if rope is not None:
        k = jnp.concatenate([k[..., :MLA_NOPE], apply_axial_rope(k[..., MLA_NOPE:], *rope)], axis=-1)
    return k, v

def ssd_scan(x, dt, a, bm, cm, s0):
    b, L, H, P = x.shape
    N = bm.shape[-1]
    Q = SSD_CHUNK
    nc = L // Q
    xc = x.reshape(b, nc, Q, H, P)
    dtc = dt.reshape(b, nc, Q, H)
    bc = bm.reshape(b, nc, Q, H, N)
    cc = cm.reshape(b, nc, Q, H, N)
    acum = jnp.cumsum(dtc * a, axis=2)
    seg = acum[:, :, :, None, :] - acum[:, :, None, :, :]
    causal = jnp.tril(jnp.ones((Q, Q), dtype=bool))[None, None, :, :, None]
    decay = jnp.exp(jnp.where(causal, seg, -jnp.inf))
    xdt = xc * dtc[..., None]
    scores = jnp.einsum('bcihn,bcjhn->bcijh', cc, bc) * decay
    y_diag = jnp.einsum('bcijh,bcjhp->bcihp', scores, xdt)
    tail = jnp.exp(acum[:, :, -1:, :] - acum)
    chunk_states = jnp.einsum('bcjhn,bcjh,bcjhp->bchpn', bc, tail, xdt)
    chunk_decay = jnp.exp(acum[:, :, -1, :])

    def step(s, inp):
        dcy, st = inp
        return (dcy[:, :, None, None] * s + st).astype(s.dtype), s

    s_final, s_prev = lax.scan(step, s0.astype(chunk_states.dtype),
                               (jnp.moveaxis(chunk_decay, 1, 0), jnp.moveaxis(chunk_states, 1, 0)))
    y_off = jnp.einsum('bcihn,cbhpn->bcihp', cc * jnp.exp(acum)[..., None], s_prev)
    return (y_diag + y_off).reshape(b, L, H, P), s_final

def ssd_mixer(xbc, dt_raw, z, conv_w, conv_b, dt_bias, a_log, d_skip, norm_g, s_init):
    b, L, _ = xbc.shape
    xbc = jax.nn.silu(dwconv(xbc, conv_w, conv_b))
    xs = xbc[..., :SSD_W].reshape(b, L, SSD_HEADS, SSD_P)
    rep = SSD_HEADS // SSD_GROUPS
    bm = jnp.repeat(xbc[..., SSD_W:SSD_W + SSD_GROUPS * SSD_N].reshape(b, L, SSD_GROUPS, SSD_N), rep, axis=2)
    cm = jnp.repeat(xbc[..., SSD_W + SSD_GROUPS * SSD_N:].reshape(b, L, SSD_GROUPS, SSD_N), rep, axis=2)
    ys = []
    states = []
    for d in range(2):
        dt = jax.nn.softplus(dt_raw[..., d * SSD_HEADS:(d + 1) * SSD_HEADS] + dt_bias[d])
        a = -jnp.exp(a_log[d])
        if d == 0:
            y, s = ssd_scan(xs, dt, a, bm, cm, s_init[:, d])
        else:
            y, s = ssd_scan(xs[:, ::-1], dt[:, ::-1], a, bm[:, ::-1], cm[:, ::-1], s_init[:, d])
            y = y[:, ::-1]
        ys.append(y)
        states.append(s)
    y = ys[0] + ys[1] + d_skip[:, None] * xs
    y = rms_norm(y.reshape(b, L, SSD_W) * jax.nn.silu(z), norm_g)
    return y, jnp.stack(states, axis=1)

def conformer_mixer(val, glu_gate, gate, conv_w, conv_b, ln_g, ln_b):
    g = val * jax.nn.sigmoid(glu_gate)
    y = layer_norm(dwconv(g, conv_w, conv_b), ln_g, ln_b)
    return jax.nn.silu(y) * jax.nn.silu(gate)

def trunk_layer(x, mod, l, prm, ctx, ropes):
    b, L, _ = x.shape
    latent = ctx is not None
    rope_a, rope_d = ropes
    shift, scale, gate = jnp.split(mod, 3, axis=-1)
    h = rms_norm(x, prm['norm_g'][l]) * (1.0 + scale) + shift
    u = h @ prm['w_in'][l]
    (a_q, a_kv, a_r, a_g, b_xbc, b_dt, b_z, c_v, c_gl, c_g, d_q, d_k, d_v, d_g) = split_proj(u)

    ckv = rms_norm(a_kv, prm['mla_kv_norm_g'][l])
    q_a = mla_queries(a_q, prm['mla_q_norm_g'][l], prm['mla_w_uq'][l], prm['mla_q_head_g'][l], rope_a)
    k_a, v_a = mla_keys(ckv, a_r, prm['mla_w_ukv'][l], prm['mla_k_head_g'][l], rope_a)
    if latent:
        k_c, v_c = mla_keys(ctx[0], ctx[1], prm['mla_w_ukv'][l], prm['mla_k_head_g'][l], None)
        k_a = jnp.concatenate([k_c, k_a], axis=1)
        v_a = jnp.concatenate([v_c, v_a], axis=1)
    o_a = block_attention(q_a, k_a, v_a, MLA_QK ** -0.5).reshape(b, L, MLA_W) * jax.nn.silu(a_g)

    s_init = ctx[4] if latent else jnp.zeros((b, 2, SSD_HEADS, SSD_P, SSD_N), x.dtype)
    o_b, s_fin = ssd_mixer(b_xbc, b_dt, b_z, prm['ssd_conv_w'][l], prm['ssd_conv_b'][l],
                           prm['ssd_dt_bias'][l], prm['ssd_a_log'][l], prm['ssd_d'][l],
                           prm['ssd_norm_g'][l], s_init)

    o_c = conformer_mixer(c_v, c_gl, c_g, prm['cf_conv_w'][l], prm['cf_conv_b'][l],
                          prm['cf_ln_g'][l], prm['cf_ln_b'][l])

    q_d = rms_norm(d_q.reshape(b, L, GQA_HEADS, GQA_HD), prm['gqa_q_g'][l])
    k_d = rms_norm(d_k.reshape(b, L, GQA_KV_HEADS, GQA_HD), prm['gqa_k_g'][l])
    v_d = d_v.reshape(b, L, GQA_KV_HEADS, GQA_HD)
    if latent:
        q_att = apply_axial_rope(q_d, *rope_d)
        k_att = jnp.concatenate([ctx[2], apply_axial_rope(k_d, *rope_d)], axis=1)
        v_att = jnp.concatenate([ctx[3], v_d], axis=1)
    else:
        q_att, k_att, v_att = q_d, k_d, v_d
    o_d = block_attention(q_att, k_att, v_att, GQA_HD ** -0.5).reshape(b, L, GQA_W) * jax.nn.silu(d_g)

    out = jnp.concatenate([o_a, o_b, o_c, o_d], axis=-1) @ prm['w_out'][l]
    x = x + gate * out
    new_ctx = None if latent else (ckv, a_r, k_d, v_d, s_fin)
    return x, new_ctx

def setup_inputs(seed: int = 0) -> dict:
    key = jax.random.key(seed)
    ks = jax.random.split(key, 32)
    f32 = jnp.float32

    def nrm(k, shape, s=1.0):
        return s * jax.random.normal(k, shape, f32)

    def gain(k, shape):
        return 1.0 + 0.02 * jax.random.normal(k, shape, f32)

    dt0 = jnp.exp(jax.random.uniform(ks[22], (DEPTH, 2, SSD_HEADS), f32, math.log(1e-3), math.log(1e-1)))
    dt_bias = dt0 + jnp.log(-jnp.expm1(-dt0))
    a_log = jnp.log(jax.random.uniform(ks[23], (DEPTH, 2, SSD_HEADS), f32, 1.0, 16.0))
    return {
        'x_prompt': nrm(ks[0], (BATCH, SEQ, D_MODEL)),
        'x_sample': nrm(ks[1], (DEC_BATCH, DEC_SEQ, D_MODEL)),
        'cache_mla_ckv': nrm(ks[2], (DEC_BATCH, DEPTH, PAST_LEN, MLA_KV_RANK)),
        'cache_mla_krope': nrm(ks[3], (DEC_BATCH, DEPTH, PAST_LEN, MLA_ROPE)),
        'cache_gqa_k': nrm(ks[4], (DEC_BATCH, DEPTH, PAST_LEN, GQA_KV_HEADS, GQA_HD)),
        'cache_gqa_v': nrm(ks[5], (DEC_BATCH, DEPTH, PAST_LEN, GQA_KV_HEADS, GQA_HD)),
        'state_ssd': nrm(ks[6], (DEC_BATCH, DEPTH, 2, SSD_HEADS, SSD_P, SSD_N), 0.1),
        'c': nrm(ks[7], (DEC_BATCH, D_MODEL)),
        'c_ctx': nrm(ks[8], (D_MODEL,)),
        'w_mod': nrm(ks[9], (DEPTH, D_MODEL, 3 * D_MODEL), D_MODEL ** -0.5),
        'b_mod': nrm(ks[10], (DEPTH, 3 * D_MODEL), 0.02),
        'norm_g': gain(ks[11], (DEPTH, D_MODEL)),
        'w_in': nrm(ks[12], (DEPTH, D_MODEL, IN_W), D_MODEL ** -0.5),
        'w_out': nrm(ks[13], (DEPTH, D_MIX, D_MODEL), D_MIX ** -0.5),
        'mla_q_norm_g': gain(ks[14], (DEPTH, MLA_Q_RANK)),
        'mla_w_uq': nrm(ks[15], (DEPTH, MLA_Q_RANK, MLA_HEADS * MLA_QK), MLA_Q_RANK ** -0.5),
        'mla_kv_norm_g': gain(ks[16], (DEPTH, MLA_KV_RANK)),
        'mla_w_ukv': nrm(ks[17], (DEPTH, MLA_KV_RANK, MLA_HEADS * (MLA_NOPE + MLA_V)), MLA_KV_RANK ** -0.5),
        'mla_q_head_g': gain(ks[18], (DEPTH, MLA_QK)),
        'mla_k_head_g': gain(ks[19], (DEPTH, MLA_QK)),
        'ssd_conv_w': nrm(ks[20], (DEPTH, SSD_CONV, SSD_CONV_CH), SSD_CONV ** -0.5),
        'ssd_conv_b': nrm(ks[21], (DEPTH, SSD_CONV_CH), 0.02),
        'ssd_dt_bias': dt_bias,
        'ssd_a_log': a_log,
        'ssd_d': gain(ks[24], (DEPTH, SSD_HEADS)),
        'ssd_norm_g': gain(ks[25], (DEPTH, SSD_W)),
        'cf_conv_w': nrm(ks[26], (DEPTH, CF_K, CF_W), CF_K ** -0.5),
        'cf_conv_b': nrm(ks[27], (DEPTH, CF_W), 0.02),
        'cf_ln_g': gain(ks[28], (DEPTH, CF_W)),
        'cf_ln_b': nrm(ks[29], (DEPTH, CF_W), 0.02),
        'gqa_q_g': gain(ks[30], (DEPTH, GQA_HD)),
        'gqa_k_g': gain(ks[31], (DEPTH, GQA_HD)),
    }

def reference(x_prompt, x_sample, cache_mla_ckv, cache_mla_krope, cache_gqa_k, cache_gqa_v, state_ssd,
              c, c_ctx, w_mod, b_mod, norm_g, w_in, w_out,
              mla_q_norm_g, mla_w_uq, mla_kv_norm_g, mla_w_ukv, mla_q_head_g, mla_k_head_g,
              ssd_conv_w, ssd_conv_b, ssd_dt_bias, ssd_a_log, ssd_d, ssd_norm_g,
              cf_conv_w, cf_conv_b, cf_ln_g, cf_ln_b, gqa_q_g, gqa_k_g):
    prm = dict(norm_g=norm_g, w_in=w_in, w_out=w_out,
               mla_q_norm_g=mla_q_norm_g, mla_w_uq=mla_w_uq, mla_kv_norm_g=mla_kv_norm_g,
               mla_w_ukv=mla_w_ukv, mla_q_head_g=mla_q_head_g, mla_k_head_g=mla_k_head_g,
               ssd_conv_w=ssd_conv_w, ssd_conv_b=ssd_conv_b, ssd_dt_bias=ssd_dt_bias,
               ssd_a_log=ssd_a_log, ssd_d=ssd_d, ssd_norm_g=ssd_norm_g,
               cf_conv_w=cf_conv_w, cf_conv_b=cf_conv_b, cf_ln_g=cf_ln_g, cf_ln_b=cf_ln_b,
               gqa_q_g=gqa_q_g, gqa_k_g=gqa_k_g)

    y = x_prompt
    ctx_out = []
    for l in range(DEPTH):
        mod = (jax.nn.silu(c_ctx) @ w_mod[l] + b_mod[l])[None, None, :]
        y, new_ctx = trunk_layer(y, mod, l, prm, None, (None, None))
        ctx_out.append(new_ctx)
    new_mla_ckv = jnp.stack([t[0] for t in ctx_out], axis=1)
    new_mla_krope = jnp.stack([t[1] for t in ctx_out], axis=1)
    new_gqa_k = jnp.stack([t[2] for t in ctx_out], axis=1)
    new_gqa_v = jnp.stack([t[3] for t in ctx_out], axis=1)
    new_state_ssd = jnp.stack([t[4] for t in ctx_out], axis=1)

    n_lat = x_sample.shape[1]
    ropes = (axial_rope_tables(n_lat, MLA_ROPE), axial_rope_tables(n_lat, GQA_HD))
    z = x_sample
    for l in range(DEPTH):
        mod = (jax.nn.silu(c) @ w_mod[l] + b_mod[l])[:, None, :]
        ctx = (cache_mla_ckv[:, l], cache_mla_krope[:, l], cache_gqa_k[:, l], cache_gqa_v[:, l], state_ssd[:, l])
        z, _ = trunk_layer(z, mod, l, prm, ctx, ropes)

    return (y, z, new_mla_ckv, new_mla_krope, new_gqa_k, new_gqa_v, new_state_ssd)


_drawn_inputs = setup_inputs


def setup_inputs(seed=0):
    import zlib

    import numpy as np

    out = dict(_drawn_inputs(seed))
    spreads = {}
    factors = {'cache_mla_ckv': 8.0,
     'cache_mla_krope': 8.0,
     'cache_gqa_k': 8.0,
     'cache_gqa_v': 8.0,
     'state_ssd': 3.277,
     'mla_q_norm_g': 8.0,
     'mla_kv_norm_g': 2.772,
     'mla_q_head_g': 8.0,
     'mla_k_head_g': 8.0,
     'ssd_d': 8.0,
     'ssd_norm_g': 6.951,
     'cf_conv_b': 8.0,
     'cf_ln_g': 8.0,
     'cf_ln_b': 8.0,
     'gqa_q_g': 8.0,
     'gqa_k_g': 2.702}
    for name, (base, spread) in spreads.items():
        noise = np.random.default_rng([zlib.crc32(name.encode()), seed]).standard_normal(out[name].shape)
        drawn = base * np.exp(spread * noise) if base else spread * noise
        out[name] = __import__('jax').numpy.asarray(drawn.astype(out[name].dtype))
    for name, factor in factors.items():
        out[name] = (out[name] * factor).astype(out[name].dtype)
    return out
```

```python
from contextlib import ExitStack

import numpy as np
import concourse.bass as bass
from concourse import mybir

F32 = mybir.dt.float32
F32R = mybir.dt.float32r
I32 = mybir.dt.int32
ALU = mybir.AluOpType
ACT = mybir.ActivationFunctionType
AX = mybir.AxisListType

P = 128
D = 1024
DC = D // P
DEPTH = 2
LAT = 2048
NLAT = LAT // P
NT = NLAT + 1
CTX = NT - 1
NSLOT = NT + 1
EPS = 1e-6
GRID_W = 64
THETA = 10000.0
A_Q, A_KV, A_R, A_G = 0, 192, 320, 352
B_XBC, B_DT, B_Z = 608, 1120, 1128
C_V, C_GL, C_G = 1384, 1640, 1896
D_Q, D_K, D_V, D_G = 2152, 2408, 2536, 2664
IN_W = 2920
QR, KVR, ROPE, NOPE, QK, HD = 192, 128, 32, 64, 96, 64
NH = 8
KW = 31


def rope_table():
    def tab(dim):
        quarter = dim // 4
        inv = np.float32(THETA) ** (-np.arange(quarter, dtype=np.float32) / np.float32(quarter))
        row = np.repeat(np.arange(LAT // GRID_W), GRID_W).astype(np.float32)
        col = np.tile(np.arange(GRID_W), LAT // GRID_W).astype(np.float32)
        ar, ac = row[:, None] * inv, col[:, None] * inv
        ang = np.concatenate([ar, ar, ac, ac], -1).astype(np.float64)
        sign = np.repeat(np.array([-1.0, 1.0, -1.0, 1.0]), quarter)
        return np.cos(ang), np.sin(ang) * sign
    c1, s1 = tab(ROPE)
    c2, s2 = tab(HD)
    lat = np.concatenate([c1, s1, c2, s2], 1)
    ctx = np.concatenate([np.ones((P, ROPE)), np.zeros((P, ROPE)), np.ones((P, HD)), np.zeros((P, HD))], 1)
    return np.concatenate([lat, ctx], 0).astype(np.float32)


RT = 2 * ROPE + 2 * HD
START = 1


class Chain:

    def __init__(self, eng, sem, per=0, n=0):
        self.eng, self.sem, self.base, self.per, self.k = eng, sem, n * per if per else 0, per, 0

    def __call__(self, ins):
        self.k += 1
        ins.then_inc(self.sem, 1)
        self.eng.wait_ge(self.sem, self.base + self.k + START)

    def tile(self, n):
        assert self.k in (0, self.per), (self.sem, self.k)
        self.base, self.k = n * self.per, 0

    def end(self):
        assert self.k in (0, self.per), (self.sem, self.k)


def emit(ins, sem, eng, value):
    ins.then_inc(sem, 1)
    eng.wait_ge(sem, value + START)


def rsqrt_steps(dve, step, y, v, t):
    step(dve.tensor_scalar(y.bitcast(I32), v.bitcast(I32), -0.5, 1597463007.0, ALU.mult, ALU.add))
    for _ in range(3):
        step(dve.scalar_tensor_tensor(t, y, -0.5, y, ALU.mult, ALU.mult))
        step(dve.tensor_tensor(t, t, v, ALU.mult))
        step(dve.scalar_tensor_tensor(y, t, 1.5, y, ALU.add, ALU.mult))


RSQRT = 10


class Scope:

    def __init__(self, nc, x, tag):
        self.nc, self.x, self.tag, self.sems = nc, x, tag, []

    def sb(self, name, shape, dt=F32):
        return self.x.enter_context(self.nc.sbuf_tensor(f"{self.tag}_{name}", shape, dt))

    def ps(self, name, shape):
        return self.x.enter_context(self.nc.psum_tensor(f"{self.tag}_{name}", shape, F32))

    def sem(self, name):
        self.sems.append(self.x.enter_context(self.nc.semaphore(f"{self.tag}_{name}")))
        return self.sems[-1]

    def block(self):
        for sem in self.sems:
            self.nc.gpsimd.sem_clear(sem)
            self.nc.gpsimd.sem_inc(sem, START)
        self.nc.all_engine_barrier()
        return self.x.enter_context(self.nc.Block())


def constants_phase(nc, K, S):
    with ExitStack() as x:
        s = Scope(nc, x, "const")
        made, stored = s.sem("made"), s.sem("stored")
        zeros = s.sb("zeros", [32, 2304])
        block = s.block()

        @block.gpsimd
        def _(pool):
            step = Chain(pool, made)
            step(pool.memset(K.ident[:, :], 0.0))
            step(pool.affine_select(out=K.ident[:, :], in_=K.ident[:, :], compare_op=ALU.not_equal, fill=1.0,
                                    base=0, pattern=[[-1, P]], channel_multiplier=1))
            step(pool.memset(K.ident2[:, :], 0.0))
            for base in (0, -HD):
                step(pool.affine_select(out=K.ident2[:, :], in_=K.ident2[:, :], compare_op=ALU.not_equal,
                                        fill=1.0, base=base, pattern=[[-1, HD]], channel_multiplier=1))
            step(pool.memset(K.ones[:, :], 1.0))
            for m, (cm, pat, base) in enumerate([(1, -1, -1), (-1, 1, -1), (-1, 1, 0), (1, -1, 0)]):
                step(pool.affine_select(out=K.tri[:, m, :], in_=K.ones[:, :], compare_op=ALU.is_ge, fill=0.0,
                                        base=base, pattern=[[pat, P]], channel_multiplier=cm))
            step(pool.memset(zeros[:, :], 0.0))

        @block.sync
        def _(sp):
            sp.wait_ge(made, 11 + START)
            for h in range(4, NH):
                sp.dma_start(S.QT[h, HD:QK, :], zeros[:, 0:NT * P]).then_inc(stored, 16)
                sp.dma_start(S.KT[h, HD:QK, :], zeros[:, 0:NSLOT * P]).then_inc(stored, 16)
            sp.wait_ge(stored, 16 * 8 + START)


def modulation_phase(nc, A, K, S, l):
    with ExitStack() as x:
        s = Scope(nc, x, f"mod{l}")
        w = s.sb("w", [P, DC, 3 * D])
        cc = s.sb("cc", [P, 2, DC])
        th = s.sb("th", [P, 2, DC])
        sc = s.sb("sc", [P, 2, DC])
        scb = s.sb("scb", [P, 2, DC, P])
        bm = s.sb("bm", [P, 2 * DC])
        ng = s.sb("ng", [P, DC])
        gb = s.sb("gb", [P, D])
        out = s.sb("out", [P, 2, 2 * DC])
        pm = s.ps("pm", [P, 2 * DC, 2])
        pg = [s.ps(f"pg{i}", [P, 512]) for i in range(4)]
        small, wl, tanhed, silued, mods, gates, dch, kept, stored = (
            s.sem(n) for n in ("small", "wl", "tanhed", "silued", "mods", "gates", "dch", "kept", "stored"))
        block = s.block()

        @block.sync
        def _(sp):
            with nc.allow_non_contiguous_dma(reason="small vectors, channels on partitions"):
                sp.dma_start(cc[:, 0, :], A["c"][0].rearrange("(c p) -> p c", p=P)).then_inc(small, 16)
                sp.dma_start(cc[:, 1, :], A["c_ctx"].rearrange("(c p) -> p c", p=P)).then_inc(small, 16)
                sp.dma_start(bm[:, :], A["b_mod"][l, 0:2 * D].rearrange("(c p) -> p c", p=P)).then_inc(small, 16)
                sp.dma_start(ng[:, :], A["norm_g"][l].rearrange("(c p) -> p c", p=P)).then_inc(small, 16)
                sp.dma_start(gb[:, :], A["b_mod"][l, 2 * D:3 * D].partition_broadcast(P)).then_inc(small, 16)
                for c in range(DC):
                    sp.dma_start(w[:, c, :], A["w_mod"][l, c * P:(c + 1) * P, :]).then_inc(wl, 16)
                sp.wait_ge(kept, 1 + START)
                for n in range(NT):
                    sp.dma_start(S.MOD[n], out[:, 1 if n == CTX else 0, :]).then_inc(stored, 16)
                sp.wait_ge(stored, 16 * NT + START)

        @block.scalar
        def _(act):
            act.wait_ge(small, 80 + START)
            act.activation(th[:, :, :], cc[:, :, :], ACT.Tanh, scale=0.5).then_inc(tanhed, 1)

        @block.vector
        def _(dve):
            step = Chain(dve, dch)
            dve.wait_ge(tanhed, 1 + START)
            step(dve.scalar_tensor_tensor(sc[:, :, :], th[:, :, :], 1.0, cc[:, :, :], ALU.add, ALU.mult))
            step(dve.tensor_scalar(sc[:, :, :], sc[:, :, :], 0.5, None, ALU.mult))
            for k in range(2):
                ins = dve.tensor_copy(scb[:, k, :, :], sc[:, k, :].unsqueeze(2).broadcast_to([P, DC, P]))
                emit(ins, silued, dve, k + 1)
            dve.wait_ge(mods, 1 + START)
            for k in range(2):
                step(dve.tensor_tensor(out[:, k, DC:2 * DC], pm[:, 0:DC, k], bm[:, 0:DC], ALU.add))
                step(dve.tensor_tensor(out[:, k, 0:DC], pm[:, DC:2 * DC, k], bm[:, DC:2 * DC], ALU.add))
                step(dve.scalar_tensor_tensor(out[:, k, 0:DC], out[:, k, 0:DC], 1.0, ng[:, :], ALU.add, ALU.mult))
            dve.wait_ge(gates, 1 + START)
            for k in range(2):
                for j in range(2):
                    cols = slice(512 * j, 512 * (j + 1))
                    step(dve.tensor_tensor(K.gate[:, k, cols], pg[2 * k + j][:, :], gb[:, cols], ALU.add))
            dve.nop().then_inc(kept, 1)

        @block.tensor
        def _(pe):
            pe.wait_ge(silued, 2 + START)
            pe.wait_ge(wl, 16 * DC + START)
            for m in range(2 * DC):
                for c in range(DC):
                    mm = pe.matmul(pm[:, m, :], w[:, c, m * P:(m + 1) * P], sc[:, :, c],
                                   start=(c == 0), stop=(c == DC - 1))
            mm.then_inc(mods, 1)
            for k in range(2):
                for j in range(2):
                    for c in range(DC):
                        mm = pe.matmul(pg[2 * k + j][:, :], scb[:, k, c, :],
                                       w[:, c, 2 * D + 512 * j:2 * D + 512 * (j + 1)],
                                       start=(c == 0), stop=(c == DC - 1))
            mm.then_inc(gates, 1)


def halves(ap, b):
    q = ap.shape[-1] // 4
    return ap.rearrange("p h (a b q) -> p h a b q", a=2, b=2, q=q)[:, :, :, b, :]


def rope_steps(pool, step, t1, t2, src, cos, sin):
    h = src.shape[1]

    def over_heads(tab):
        return tab.unsqueeze(1).broadcast_to([P, h, tab.shape[-1]])

    step(pool.tensor_tensor(t1, src, over_heads(cos), ALU.mult))
    q = src.shape[-1] // 4
    for b in range(2):
        sb = sin.rearrange("p (a b q) -> p a b q", a=2, b=2, q=q)[:, :, b, :]
        step(pool.tensor_tensor(halves(t2, b), halves(src, 1 - b), sb.unsqueeze(1).broadcast_to([P, h, 2, q]),
                                ALU.mult))


def projection_phase(nc, A, K, S, l, xin):
    with ExitStack() as x:
        s = Scope(nc, x, f"proj{l}")
        w = s.sb("w", [P, DC, IN_W])
        wuq = s.sb("wuq", [QK, 2, 4 * QK])
        wukv = s.sb("wukv", [P, 4 * P])
        gq = s.sb("gq", [P, QR])
        gkv = s.sb("gkv", [P, KVR])
        qkg = s.sb("qkg", [P, 8, QK])
        gg = s.sb("gg", [P, 6, HD])
        xt = [s.sb(f"xt{i}", [P, D]) for i in range(2)]
        md = [s.sb(f"md{i}", [P, 2 * DC]) for i in range(2)]
        rp = s.sb("rp", [P, RT])
        xn = s.sb("xn", [P, D])
        hT = [s.sb(f"hT{i}", [P, DC, P]) for i in range(2)]
        junk = s.sb("junk", [P, D])
        pss, pv, pr, ptmp = (s.sb(n, [P, 1]) for n in ("pss", "pv", "pr", "ptmp"))
        E0 = s.sb("E0", [P, 360])
        ss0, v0, r0, tmp0 = (s.sb(n, [P, 2]) for n in ("ss0", "v0", "r0", "tmp0"))
        krss = s.sb("krss", [P, 1])
        ql = s.sb("ql", [P, QR])
        ck = s.sb("ck", [P, KVR])
        LT = s.sb("LT", [P, 3, P])
        qsq = s.sb("qsq", [P, 4, QK])
        KV = s.sb("KV", [P, 4, P])
        ksq = s.sb("ksq", [P, 4, NOPE])
        ssh, vh, rh, tmph = (s.sb(n, [P, 8]) for n in ("ssh", "vh", "rh", "tmph"))
        QKt = s.sb("QKt", [P, 8, QK])
        E3 = s.sb("E3", [P, 8, HD])
        gsq = s.sb("gsq", [P, 6, HD])
        ssg, vg, rg, tmpg = (s.sb(n, [P, 6]) for n in ("ssg", "vg", "rg", "tmpg"))
        GN = s.sb("GN", [P, 6, HD])
        GR = s.sb("GR", [P, 6, HD])
        t1 = s.sb("t1", [P, 6, HD])
        t2 = s.sb("t2", [P, 6, HD])
        m1 = s.sb("m1", [P, 8, ROPE])
        m2 = s.sb("m2", [P, 8, ROPE])
        TH = [s.sb(f"TH{i}", [P, 512]) for i in range(2)]
        TG = s.sb("TG", [P, 256])
        GT = s.sb("GT", [P, D])
        FB = s.sb("FB", [P, 4, P])
        FG = s.sb("FG", [P, 2, P])
        QST = s.sb("QST", [QK, 4, P])
        KST = s.sb("KST", [QK, 4, P])
        GST = s.sb("GST", [P, 3, P])
        b = [s.ps(f"b{i}", [P, 512]) for i in range(8)]
        names = ("w_loaded small x_loaded md_loaded rp_loaded gains ss_ready r_ready xn_ready xT_done ht_act ht_dve "
                 "t0_done t1_done t2_done t3_done s1_done s2_done s3_done s5_done f0_done f1_done e0_ready e3_ready "
                 "th1_ready th2_ready th3_ready qlck_ready lt_ready sq_ready qk_ready qkr_ready gn_ready gr_ready "
                 "gate1_ready gates_ready fb_ready fg_ready qst_ready kst_ready gst_ready "
                 "st_dt st_v3 st_v st_q st_k st_g st_gd st_fb st_fg st_out act_steps act_pre dve_steps dve_pre "
                 "pool_steps").split()
        q = {n: s.sem(n) for n in names}
        block = s.block()

        @block.sync
        def _(sp):
            with nc.allow_non_contiguous_dma(reason="broadcast gains"):
                sp.dma_start(wuq[:, :, :], A["mla_w_uq"][l].rearrange("(a p) n -> p a n", a=2)).then_inc(q["small"], 16)
                sp.dma_start(wukv[:, :], A["mla_w_ukv"][l]).then_inc(q["small"], 16)
                sp.dma_start(gq[:, :], A["mla_q_norm_g"][l].partition_broadcast(P)).then_inc(q["small"], 16)
                sp.dma_start(gkv[:, :], A["mla_kv_norm_g"][l].partition_broadcast(P)).then_inc(q["small"], 16)
                for h in range(8):
                    g = A["mla_q_head_g" if h < 4 else "mla_k_head_g"]
                    sp.dma_start(qkg[:, h, :], g[l].partition_broadcast(P)).then_inc(q["small"], 16)
                for h in range(6):
                    g = A["gqa_q_g" if h < 4 else "gqa_k_g"]
                    sp.dma_start(gg[:, h, :], g[l].partition_broadcast(P)).then_inc(q["small"], 16)

            def load_x(m, par):
                if not (isinstance(m, int) and m == 0):
                    sp.wait_ge(q["xn_ready"], m + START)
                    sp.wait_ge(q["ht_act"], m + START)
                    sp.wait_ge(q["ht_dve"], m + START)
                sp.dma_start(xt[par][:, :], xin[bass.ds(m * P, P), :]).then_inc(q["x_loaded"], 16)
                sp.dma_start(md[par][:, :], S.MODR[bass.ds(m * P, P), :]).then_inc(q["md_loaded"], 16)

            load_x(0, 0)
            sp.dma_start(rp[:, :], A["rope"][0:P, :]).then_inc(q["rp_loaded"], 16)
            for c in range(DC):
                sp.dma_start(w[:, c, :], A["w_in"][l, c * P:(c + 1) * P, :]).then_inc(q["w_loaded"], 16)

            def tile(n, par, last):
                if not last:
                    load_x(n + 1, 1 - par)
                sp.wait_ge(q["e0_ready"], n + 1 + START)
                sp.dma_start(S.DT[bass.ds(n * P, P), :], E0[:, 352:360]).then_inc(q["st_dt"], 16)
                if last:
                    sp.dma_start(A["new_mla_krope"][0, l], E0[:, A_R:A_R + ROPE]).then_inc(q["st_out"], 16)
                    sp.wait_ge(q["qlck_ready"], n + 1 + START)
                    sp.dma_start(A["new_mla_ckv"][0, l], ck[:, :]).then_inc(q["st_out"], 16)
                sp.wait_ge(q["e3_ready"], n + 1 + START)
                for r in range(2):
                    sp.dma_start(S.V[4 + r:NH:2, :, bass.ds(n + 1, 1), :].rearrange("h p s d -> p h (s d)"),
                                 E3[:, 6:8, :]).then_inc(q["st_v3"], 16)
                if last:
                    sp.dma_start(A["new_gqa_v"][0, l], E3[:, 6:8, :]).then_inc(q["st_out"], 16)
                    sp.wait_ge(q["gn_ready"], n + 1 + START)
                    sp.dma_start(A["new_gqa_k"][0, l], GN[:, 4:6, :]).then_inc(q["st_out"], 16)
                sp.wait_ge(q["gates_ready"], n + 1 + START)
                sp.dma_start(S.G[bass.ds(n * P, P), :], GT[:, :]).then_inc(q["st_gd"], 16)
                if not last:
                    sp.wait_ge(q["qkr_ready"], n + 1 + START)
                    sp.dma_start(rp[:, :], A["rope"][bass.ds((n + 1) * P, P), :]).then_inc(q["rp_loaded"], 16)
            with sp.Fori(0, NLAT // 2) as j:
                for u in range(2):
                    tile(j * 2 + u, u, False)
            tile(CTX, 0, True)
            for n, per in (("st_dt", 16), ("st_v3", 32), ("st_v", 16), ("st_q", 16), ("st_k", 16), ("st_g", 96),
                           ("st_gd", 16), ("st_fb", 16), ("st_fg", 16)):
                sp.wait_ge(q[n], per * NT + START)
            sp.wait_ge(q["st_out"], 64 + START)

        @block.scalar
        def _(act):
            step = Chain(act, q["act_steps"], 18)

            def pre(m, par):
                act.wait_ge(q["x_loaded"], (m + 1) * 16 + START)
                emit(act.activation(junk[:, :], xt[par][:, :], ACT.Square, accum_out=pss[:, :]), q["ss_ready"], act, m + 1)
                act.wait_ge(q["r_ready"], m + 1 + START)
                act.wait_ge(q["xT_done"], m + START)
                emit(act.activation(xn[:, :], xt[par][:, :], ACT.Copy, scale=pr[:, :]), q["xn_ready"], act, m + 1)

            def evac_hT(m, par):
                act.wait_ge(q["xT_done"], m + 1 + START)
                act.wait_ge(q["md_loaded"], (m + 1) * 16 + START)
                pst = Chain(act, q["act_pre"], 3, m)
                for c in range(4):
                    ins = act.activation(hT[par][:, c, :], b[0][:, c * P:(c + 1) * P], ACT.Identity,
                                         scale=md[par][:, c:c + 1], bias=md[par][:, DC + c:DC + c + 1])
                    if c < 3:
                        pst(ins)
                    else:
                        emit(ins, q["ht_act"], act, m + 1)

            def tile(n, par, last):
                step.tile(n)
                act.wait_ge(q["t0_done"], n + 1 + START)
                act.wait_ge(q["st_dt"], n * 16 + START)
                step(act.activation(E0[:, :], b[2][:, 0:360], ACT.Copy))
                step(act.activation(junk[:, 0:QR], E0[:, 0:QR], ACT.Square, accum_out=ss0[:, 0:1]))
                step(act.activation(junk[:, 0:KVR], E0[:, A_KV:A_R], ACT.Square, accum_out=ss0[:, 1:2]))
                emit(act.activation(junk[:, 0:ROPE], E0[:, A_R:A_G], ACT.Square, accum_out=krss[:, :]),
                     q["e0_ready"], act, n + 1)
                if not last:
                    pre(n + 1, 1 - par)
                act.wait_ge(q["t3_done"], n + 1 + START)
                act.wait_ge(q["st_v3"], n * 32 + START)
                step(act.activation(E3[:, :, :], b[5][:, :], ACT.Copy))
                emit(act.activation(gsq[:, :, :], E3[:, 0:6, :], ACT.Square), q["e3_ready"], act, n + 1)
                act.wait_ge(q["t1_done"], n + 1 + START)
                emit(act.activation(TH[0][:, :], b[3][:, :], ACT.Tanh, scale=0.5), q["th1_ready"], act, n + 1)
                act.wait_ge(q["s1_done"], n + 1 + START)
                step(act.activation(LT[0:QK, 0:2, :], b[7][0:QK, 0:2 * P], ACT.Copy))
                emit(act.activation(LT[:, 2, :], b[7][:, 2 * P:3 * P], ACT.Copy), q["lt_ready"], act, n + 1)
                act.wait_ge(q["t2_done"], n + 1 + START)
                emit(act.activation(TH[1][:, :], b[4][:, :], ACT.Tanh, scale=0.5), q["th2_ready"], act, n + 1)
                act.wait_ge(q["s2_done"], n + 1 + START)
                step(act.activation(qsq[:, :, :], b[2][:, 0:4 * QK], ACT.Square))
                act.wait_ge(q["st_v"], n * 16 + START)
                step(act.activation(KV[:, :, :], b[7][:, :], ACT.Copy))
                emit(act.activation(ksq[:, :, :], KV[:, :, 0:NOPE], ACT.Square), q["sq_ready"], act, n + 1)
                act.dma_start(S.V[0:4, :, bass.ds(n + 1, 1), :].rearrange("h p s d -> p h (s d)"),
                             KV[:, :, NOPE:P]).then_inc(q["st_v"], 16)
                act.wait_ge(q["f0_done"], n + 1 + START)
                act.wait_ge(q["st_fb"], n * 16 + START)
                emit(act.activation(FB[:, :, :], b[6][:, :], ACT.Copy), q["fb_ready"], act, n + 1)
                act.dma_start(S.XBC[:, :, bass.ds(n * P, P)].rearrange("f p t -> p f t"), FB[:, :, :]).then_inc(q["st_fb"], 16)
                act.wait_ge(q["s3_done"], n + 1 + START)
                act.wait_ge(q["st_q"], n * 16 + START)
                emit(act.activation(QST[:, :, :], b[2][0:QK, :], ACT.Copy), q["qst_ready"], act, n + 1)
                act.dma_start(S.QT[0:4, :, bass.ds(n * P, P)].rearrange("h r t -> r h t"), QST[:, :, :]).then_inc(q["st_q"], 16)
                act.wait_ge(q["st_k"], n * 16 + START)
                emit(act.activation(KST[:, :, :], b[7][0:QK, :], ACT.Copy), q["kst_ready"], act, n + 1)
                act.dma_start(S.KT[0:4, :, bass.ds((n + 1) * P, P)].rearrange("h r t -> r h t"), KST[:, :, :]).then_inc(q["st_k"], 16)
                if not last:
                    evac_hT(n + 1, 1 - par)
                act.wait_ge(q["f1_done"], n + 1 + START)
                emit(act.activation(TG[:, :], b[6][:, 256:512], ACT.Tanh, scale=0.5), q["th3_ready"], act, n + 1)
                act.wait_ge(q["s5_done"], n + 1 + START)
                act.wait_ge(q["st_g"], n * 96 + START)
                emit(act.activation(GST[:, :, :], b[5][:, 0:3 * P], ACT.Copy), q["gst_ready"], act, n + 1)
                for o in range(2):
                    rows = slice(o * HD, (o + 1) * HD)
                    act.dma_start(S.QT[4 + o:NH:2, 0:HD, bass.ds(n * P, P)].rearrange("h r t -> r h t"),
                                 GST[rows, 0:2, :]).then_inc(q["st_g"], 16)
                    for h in (4 + 2 * o, 5 + 2 * o):
                        act.dma_start(S.KT[h, 0:HD, bass.ds((n + 1) * P, P)], GST[rows, 2, :]).then_inc(q["st_g"], 16)
                act.wait_ge(q["fg_ready"], n + 1 + START)
                act.dma_start(S.GLU[:, :, bass.ds(n * P, P)].rearrange("f p t -> p f t"), FG[:, :, :]).then_inc(q["st_fg"], 16)
                step.end()

            step.per = 7
            act.wait_ge(q["small"], 16 * 18 + START)
            pre0 = act
            pre0.wait_ge(q["x_loaded"], 16 + START)
            emit(act.activation(junk[:, :], xt[0][:, :], ACT.Square, accum_out=pss[:, :]), q["ss_ready"], act, 1)
            act.wait_ge(q["r_ready"], 1 + START)
            emit(act.activation(xn[:, :], xt[0][:, :], ACT.Copy, scale=pr[:, :]), q["xn_ready"], act, 1)
            evac_hT(0, 0)
            with act.Fori(0, NLAT // 2) as j:
                for u in range(2):
                    tile(j * 2 + u, u, False)
            tile(CTX, 0, True)

        @block.vector
        def _(dve):
            setup = Chain(dve, q["gains"])
            dve.wait_ge(q["small"], 16 * 18 + START)
            setup(dve.tensor_scalar(qkg[:, 0:4, :], qkg[:, 0:4, :], float(QK) ** -0.5, None, ALU.mult))
            setup(dve.tensor_scalar(gg[:, 0:4, :], gg[:, 0:4, :], float(HD) ** -0.5, None, ALU.mult))
            step = Chain(dve, q["dve_steps"], RSQRT * 3 + 13)

            def pre(m, par):
                pst = Chain(dve, q["dve_pre"], RSQRT + 3, m)
                dve.wait_ge(q["ss_ready"], m + 1 + START)
                pst(dve.tensor_scalar(pv[:, :], pss[:, :], 1.0 / D, EPS, ALU.mult, ALU.add))
                rsqrt_steps(dve, lambda i: pst(i) if pst.k < RSQRT else emit(i, q["r_ready"], dve, m + 1),
                            pr[:, :], pv[:, :], ptmp[:, :])
                assert pst.k == RSQRT

            def evac_hT(m, par):
                pst = Chain(dve, q["dve_pre"], RSQRT + 3, m)
                pst.k = RSQRT
                dve.wait_ge(q["xT_done"], m + 1 + START)
                dve.wait_ge(q["md_loaded"], (m + 1) * 16 + START)
                for c in range(4, 8):
                    ins = dve.tensor_scalar(hT[par][:, c, :], b[1][:, (c - 4) * P:(c - 3) * P],
                                            md[par][:, c:c + 1], md[par][:, DC + c:DC + c + 1], ALU.mult, ALU.add)
                    if c < 7:
                        pst(ins)
                    else:
                        emit(ins, q["ht_dve"], dve, m + 1)
                pst.end()

            def tile(n, par, last):
                step.tile(n)
                dve.wait_ge(q["e0_ready"], n + 1 + START)
                step(dve.tensor_scalar(v0[:, 0:1], ss0[:, 0:1], 1.0 / QR, EPS, ALU.mult, ALU.add))
                step(dve.tensor_scalar(v0[:, 1:2], ss0[:, 1:2], 1.0 / KVR, EPS, ALU.mult, ALU.add))
                rsqrt_steps(dve, step, r0[:, :], v0[:, :], tmp0[:, :])
                step(dve.scalar_tensor_tensor(ql[:, :], E0[:, 0:QR], r0[:, 0:1], gq[:, :], ALU.mult, ALU.mult))
                emit(dve.scalar_tensor_tensor(ck[:, :], E0[:, A_KV:A_R], r0[:, 1:2], gkv[:, :], ALU.mult, ALU.mult),
                     q["qlck_ready"], dve, n + 1)
                if not last:
                    pre(n + 1, 1 - par)
                dve.wait_ge(q["e3_ready"], n + 1 + START)
                step(dve.tensor_reduce(ssg[:, :], gsq[:, :, :], AX.X, ALU.add))
                step(dve.tensor_scalar(vg[:, :], ssg[:, :], 1.0 / HD, EPS, ALU.mult, ALU.add))
                rsqrt_steps(dve, step, rg[:, :], vg[:, :], tmpg[:, :])
                step(dve.tensor_tensor(GN[:, :, :], E3[:, 0:6, :], rg[:, :].unsqueeze(2).broadcast_to([P, 6, HD]), ALU.mult))
                emit(dve.tensor_tensor(GN[:, :, :], GN[:, :, :], gg[:, :, :], ALU.mult), q["gn_ready"], dve, n + 1)
                dve.wait_ge(q["th1_ready"], n + 1 + START)
                dve.wait_ge(q["st_gd"], n * 16 + START)
                emit(dve.scalar_tensor_tensor(GT[:, 0:512], TH[0][:, :], 1.0, b[3][:, :], ALU.add, ALU.mult),
                     q["gate1_ready"], dve, n + 1)
                dve.wait_ge(q["th2_ready"], n + 1 + START)
                emit(dve.scalar_tensor_tensor(GT[:, 512:D], TH[1][:, :], 1.0, b[4][:, :], ALU.add, ALU.mult),
                     q["gates_ready"], dve, n + 1)
                dve.wait_ge(q["sq_ready"], n + 1 + START)
                step(dve.tensor_reduce(ssh[:, 0:4], qsq[:, :, :], AX.X, ALU.add))
                step(dve.tensor_reduce(ssh[:, 4:8], ksq[:, :, :], AX.X, ALU.add))
                step(dve.tensor_scalar(ssh[:, 4:8], ssh[:, 4:8], krss[:, 0:1], None, ALU.add))
                step(dve.tensor_scalar(vh[:, :], ssh[:, :], 1.0 / QK, EPS, ALU.mult, ALU.add))
                rsqrt_steps(dve, step, rh[:, :], vh[:, :], tmph[:, :])

                def rows(a, b_, w_):
                    return rh[:, a:b_].unsqueeze(2).broadcast_to([P, b_ - a, w_])

                step(dve.tensor_tensor(QKt[:, 0:4, :], b[2][:, 0:4 * QK].rearrange("p (h d) -> p h d", h=4),
                                       rows(0, 4, QK), ALU.mult))
                step(dve.tensor_tensor(QKt[:, 4:8, 0:NOPE], KV[:, :, 0:NOPE], rows(4, 8, NOPE), ALU.mult))
                step(dve.tensor_tensor(QKt[:, 4:8, NOPE:QK], E0[:, A_R:A_G].unsqueeze(1).broadcast_to([P, 4, ROPE]),
                                       rows(4, 8, ROPE), ALU.mult))
                emit(dve.tensor_tensor(QKt[:, :, :], QKt[:, :, :], qkg[:, :, :], ALU.mult), q["qk_ready"], dve, n + 1)
                if not last:
                    evac_hT(n + 1, 1 - par)
                dve.wait_ge(q["th3_ready"], n + 1 + START)
                dve.wait_ge(q["st_fg"], n * 16 + START)
                emit(dve.scalar_tensor_tensor(FG[:, :, :], TG[:, :].rearrange("p (f t) -> p f t", f=2), 1.0,
                                              b[6][:, 0:256].rearrange("p (f t) -> p f t", f=2), ALU.add, ALU.mult),
                     q["fg_ready"], dve, n + 1)
                step.end()

            step.per = 3 + RSQRT + 3 + RSQRT + 7 + RSQRT
            pre(0, 0)
            evac_hT(0, 0)
            with dve.Fori(0, NLAT // 2) as j:
                for u in range(2):
                    tile(j * 2 + u, u, False)
            tile(CTX, 0, True)

        @block.gpsimd
        def _(pool):
            step = Chain(pool, q["pool_steps"], 6)

            def tile(n, par, last):
                step.tile(n)
                pool.wait_ge(q["rp_loaded"], (n + 1) * 16 + START)
                pool.wait_ge(q["gn_ready"], n + 1 + START)
                rope_steps(pool, step, t1[:, :, :], t2[:, :, :], GN[:, :, :], rp[:, 64:128], rp[:, 128:192])
                emit(pool.tensor_tensor(GR[:, :, :], t1[:, :, :], t2[:, :, :], ALU.add), q["gr_ready"], pool, n + 1)
                pool.wait_ge(q["qk_ready"], n + 1 + START)
                rope_steps(pool, step, m1[:, :, :], m2[:, :, :], QKt[:, :, NOPE:QK], rp[:, 0:32], rp[:, 32:64])
                emit(pool.tensor_tensor(QKt[:, :, NOPE:QK], m1[:, :, :], m2[:, :, :], ALU.add), q["qkr_ready"], pool, n + 1)
                step.end()

            with pool.Fori(0, NLAT // 2) as j:
                for u in range(2):
                    tile(j * 2 + u, u, False)
            tile(CTX, 0, True)

        @block.tensor
        def _(pe):
            def xT(m):
                pe.wait_ge(q["xn_ready"], m + 1 + START)
                pe.wait_ge(q["ht_act"], m + START)
                pe.wait_ge(q["ht_dve"], m + START)
                for c in range(DC):
                    mm = pe.transpose(b[c // 4][:, (c % 4) * P:(c % 4 + 1) * P], xn[:, c * P:(c + 1) * P], K.ident[:, :])
                mm.then_inc(q["xT_done"], 1)

            def tokens(par, bank, parts):
                at = 0
                for a, e in parts:
                    for c in range(DC):
                        mm = pe.matmul(b[bank][:, at:at + e - a], hT[par][:, c, :], w[:, c, a:e],
                                       start=(c == 0), stop=(c == DC - 1))
                    at += e - a
                return mm

            def channels(par, bank, cols):
                for f, a in enumerate(cols):
                    for c in range(DC):
                        mm = pe.matmul(b[bank][:, f * P:(f + 1) * P], w[:, c, a:a + P], hT[par][:, c, :],
                                       start=(c == 0), stop=(c == DC - 1))
                return mm

            def tile(n, par, last):
                pe.wait_ge(q["ht_act"], n + 1 + START)
                pe.wait_ge(q["ht_dve"], n + 1 + START)
                pe.wait_ge(q["qst_ready"], n + START)
                tokens(par, 2, [(A_Q, A_G), (B_DT, B_Z)]).then_inc(q["t0_done"], 1)
                pe.wait_ge(q["gst_ready"], n + START)
                tokens(par, 5, [(D_Q, D_G)]).then_inc(q["t3_done"], 1)
                pe.wait_ge(q["gate1_ready"], n + START)
                tokens(par, 3, [(A_G, B_XBC), (B_Z, C_V)]).then_inc(q["t1_done"], 1)
                pe.wait_ge(q["kst_ready"], n + START)
                pe.wait_ge(q["qlck_ready"], n + 1 + START)
                for a in range(2):
                    pe.transpose(b[7][0:QK, a * P:(a + 1) * P], ql[:, a * QK:(a + 1) * QK], K.ident[:, :])
                pe.transpose(b[7][:, 2 * P:3 * P], ck[:, :], K.ident[:, :]).then_inc(q["s1_done"], 1)
                pe.wait_ge(q["gates_ready"], n + START)
                tokens(par, 4, [(C_G, D_Q), (D_G, IN_W)]).then_inc(q["t2_done"], 1)
                pe.wait_ge(q["lt_ready"], n + 1 + START)
                for a in range(2):
                    pe.matmul(b[2][:, 0:4 * QK], LT[0:QK, a, :], wuq[:, a, :], start=(a == 0), stop=(a == 1))
                pe.matmul(b[7][:, :], LT[:, 2, :], wukv[:, :], start=True, stop=True).then_inc(q["s2_done"], 1)
                pe.wait_ge(q["fg_ready"], n + START)
                channels(par, 6, [B_XBC + P * f for f in range(4)]).then_inc(q["f0_done"], 1)
                pe.wait_ge(q["qkr_ready"], n + 1 + START)
                for h in range(8):
                    mm = pe.transpose(b[2 if h < 4 else 7][0:QK, (h % 4) * P:(h % 4 + 1) * P], QKt[:, h, :], K.ident[:, :])
                mm.then_inc(q["s3_done"], 1)
                if not last:
                    xT(n + 1)
                pe.wait_ge(q["fb_ready"], n + 1 + START)
                channels(par, 6, [C_V, C_V + P, C_GL, C_GL + P]).then_inc(q["f1_done"], 1)
                pe.wait_ge(q["gr_ready"], n + 1 + START)
                for pair in range(3):
                    mm = pe.transpose(b[5][:, pair * P:(pair + 1) * P],
                                      GR[:, 2 * pair:2 * pair + 2, :].rearrange("p h d -> p (h d)"), K.ident[:, :])
                mm.then_inc(q["s5_done"], 1)

            pe.wait_ge(q["xn_ready"], 1 + START)
            xT(0)
            pe.wait_ge(q["small"], 16 * 18 + START)
            pe.wait_ge(q["w_loaded"], 16 * DC + START)
            with pe.Fori(0, NLAT // 2) as j:
                for u in range(2):
                    tile(j * 2 + u, u, False)
            tile(CTX, 0, True)


def cache_phase(nc, A, K, S, l):
    with ExitStack() as x:
        s = Scope(nc, x, f"cache{l}")
        wukv = s.sb("wukv", [P, 4 * P])
        kg = s.sb("kg", [P, QK])
        ck = s.sb("ck", [P, KVR])
        kr = s.sb("kr", [P, ROPE])
        gk = s.sb("gk", [P, 2, HD])
        gv = s.sb("gv", [P, 2, HD])
        ckT = s.sb("ckT", [P, P])
        KV = s.sb("KV", [P, 4, P])
        sq = s.sb("sq", [P, 4, NOPE])
        sqr = s.sb("sqr", [P, ROPE])
        krss = s.sb("krss", [P, 1])
        ss, v, r, tmp = (s.sb(n, [P, 4]) for n in ("ss", "v", "r", "tmp"))
        KN = s.sb("KN", [P, 4, QK])
        KST = s.sb("KST", [QK, 4, P])
        GST = s.sb("GST", [HD, 2, P])
        pt, pkv, pk, pgk = (s.ps(n, [P, 512]) for n in ("pt", "pkv", "pk", "pgk"))
        loaded, turned, copied, kv_done, sq_ready, kn_ready, kt_done, st_ready, stored, ach, dch = (
            s.sem(n) for n in ("loaded", "turned", "copied", "kv_done", "sq_ready", "kn_ready", "kt_done",
                               "st_ready", "stored", "act_steps", "dve_steps"))
        block = s.block()

        @block.sync
        def _(sp):
            with nc.allow_non_contiguous_dma(reason="broadcast gain"):
                sp.dma_start(ck[:, :], A["cache_mla_ckv"][0, l]).then_inc(loaded, 16)
                sp.dma_start(kr[:, :], A["cache_mla_krope"][0, l]).then_inc(loaded, 16)
                sp.dma_start(gk[:, :, :], A["cache_gqa_k"][0, l]).then_inc(loaded, 16)
                sp.dma_start(gv[:, :, :], A["cache_gqa_v"][0, l]).then_inc(loaded, 16)
                sp.dma_start(wukv[:, :], A["mla_w_ukv"][l]).then_inc(loaded, 16)
                sp.dma_start(kg[:, :], A["mla_k_head_g"][l].partition_broadcast(P)).then_inc(loaded, 16)
            sp.wait_ge(loaded, 96 + START)
            for rep in range(2):
                sp.dma_start(S.V[4 + rep:NH:2, :, 0, :].rearrange("h p d -> p h d"), gv[:, :, :]).then_inc(stored, 16)
            sp.wait_ge(sq_ready, 1 + START)
            sp.dma_start(S.V[0:4, :, 0, :].rearrange("h p d -> p h d"), KV[:, :, NOPE:P]).then_inc(stored, 16)
            sp.wait_ge(st_ready, 1 + START)
            sp.dma_start(S.KT[0:4, :, 0:P].rearrange("h r t -> r h t"), KST[:, :, :]).then_inc(stored, 16)
            for rep in range(2):
                sp.dma_start(S.KT[4 + rep:NH:2, 0:HD, 0:P].rearrange("h r t -> r h t"), GST[:, :, :]).then_inc(stored, 16)
            sp.wait_ge(stored, 96 + START)

        @block.tensor
        def _(pe):
            pe.wait_ge(loaded, 96 + START)
            pe.transpose(pt[:, 0:P], ck[:, :], K.ident[:, :]).then_inc(turned, 1)
            pe.wait_ge(copied, 1 + START)
            pe.matmul(pkv[:, :], ckT[:, :], wukv[:, :], start=True, stop=True).then_inc(kv_done, 1)
            for h in range(2):
                pe.transpose(pgk[0:HD, h * P:(h + 1) * P], gk[:, h, :], K.ident[:, :])
            pe.wait_ge(kn_ready, 1 + START)
            for h in range(4):
                mm = pe.transpose(pk[0:QK, h * P:(h + 1) * P], KN[:, h, :], K.ident[:, :])
            mm.then_inc(kt_done, 1)

        @block.scalar
        def _(act):
            step = Chain(act, ach)
            act.wait_ge(loaded, 96 + START)
            act.wait_ge(turned, 1 + START)
            emit(act.activation(ckT[:, :], pt[:, 0:P], ACT.Copy), copied, act, 1)
            act.wait_ge(kv_done, 1 + START)
            step(act.activation(KV[:, :, :], pkv[:, :], ACT.Copy))
            step(act.activation(sqr[:, :], kr[:, :], ACT.Square, accum_out=krss[:, :]))
            emit(act.activation(sq[:, :, :], KV[:, :, 0:NOPE], ACT.Square), sq_ready, act, 1)
            act.wait_ge(kt_done, 1 + START)
            step(act.activation(KST[:, :, :], pk[0:QK, :], ACT.Copy))
            emit(act.activation(GST[:, :, :], pgk[0:HD, 0:2 * P], ACT.Copy), st_ready, act, 1)

        @block.vector
        def _(dve):
            step = Chain(dve, dch)
            dve.wait_ge(sq_ready, 1 + START)
            step(dve.tensor_reduce(ss[:, :], sq[:, :, :], AX.X, ALU.add))
            step(dve.tensor_scalar(ss[:, :], ss[:, :], krss[:, 0:1], None, ALU.add))
            step(dve.tensor_scalar(v[:, :], ss[:, :], 1.0 / QK, EPS, ALU.mult, ALU.add))
            rsqrt_steps(dve, step, r[:, :], v[:, :], tmp[:, :])
            step(dve.tensor_tensor(KN[:, :, 0:NOPE], KV[:, :, 0:NOPE], r[:, :].unsqueeze(2).broadcast_to([P, 4, NOPE]), ALU.mult))
            step(dve.tensor_tensor(KN[:, :, NOPE:QK], kr[:, :].unsqueeze(1).broadcast_to([P, 4, ROPE]),
                                   r[:, :].unsqueeze(2).broadcast_to([P, 4, ROPE]), ALU.mult))
            emit(dve.tensor_tensor(KN[:, :, :], KN[:, :, :], kg[:, :].unsqueeze(1).broadcast_to([P, 4, QK]), ALU.mult),
                 kn_ready, dve, 1)


def convolution_phase(nc, A, K, S, l):
    half = KW // 2
    with ExitStack() as x:
        s = Scope(nc, x, f"conv{l}")
        XB = [s.sb(f"XB{i}", [P, LAT + 2]) for i in range(2)]
        GB = [s.sb(f"GB{i}", [P, LAT + 2 * half]) for i in range(2)]
        Y = [s.sb(f"Y{i}", [P, LAT]) for i in range(2)]
        TH = s.sb("TH", [P, LAT])
        Z = [s.sb(f"Z{i}", [P, LAT]) for i in range(2)]
        cw = s.sb("cw", [P, 4, 3])
        cb = s.sb("cb", [P, 4])
        fw = s.sb("fw", [P, 2, KW])
        fb = s.sb("fb", [P, 2])
        small, x_loaded, g_loaded, padded, y_ready, th_ready, z_ready, stored, dch = (
            s.sem(n) for n in ("small", "x_loaded", "g_loaded", "padded", "y_ready", "th_ready", "z_ready",
                               "stored", "dve_steps"))
        seqs = [(0, LAT), (LAT, P)]
        xjobs = [(at, n, f) for at, n in seqs for f in range(4)]
        gjobs = [(at, n, f) for at, n in seqs for f in range(2)]
        block = s.block()

        @block.sync
        def _(sp):
            with nc.allow_non_contiguous_dma(reason="taps, channels on partitions"):
                for f in range(4):
                    sp.dma_start(cw[:, f, :], A["ssd_conv_w"][l][:, f * P:(f + 1) * P].rearrange("k p -> p k")).then_inc(small, 16)
                sp.dma_start(cb[:, :], A["ssd_conv_b"][l].rearrange("(f p) -> p f", p=P)).then_inc(small, 16)
                for f in range(2):
                    sp.dma_start(fw[:, f, :], A["cf_conv_w"][l][:, f * P:(f + 1) * P].rearrange("k p -> p k")).then_inc(small, 16)
                sp.dma_start(fb[:, :], A["cf_conv_b"][l].rearrange("(f p) -> p f", p=P)).then_inc(small, 16)

            def load_x(i):
                at, n, f = xjobs[i]
                sp.dma_start(XB[i % 2][:, 1:1 + n], S.XBC[f, :, at:at + n]).then_inc(x_loaded, 16)

            def load_g(i):
                at, n, f = gjobs[i]
                sp.dma_start(GB[i % 2][:, half:half + n], S.GLU[f, :, at:at + n]).then_inc(g_loaded, 16)

            load_x(0)
            for i, (at, n, f) in enumerate(xjobs):
                if i + 1 < len(xjobs):
                    sp.wait_ge(x_loaded, 16 * (i + 1) + START)
                    if i >= 1:
                        sp.wait_ge(y_ready, i + START)
                    load_x(i + 1)
                if i == 0:
                    load_g(0)
                sp.wait_ge(z_ready, i + 1 + START)
                sp.dma_start(S.XC[f, :, at:at + n], Z[i % 2][:, 0:n]).then_inc(stored, 16)
                sp.wait_ge(stored, 16 * (i + 1) + START)
            base = len(xjobs)
            for i, (at, n, f) in enumerate(gjobs):
                if i + 1 < len(gjobs):
                    sp.wait_ge(g_loaded, 16 * (i + 1) + START)
                    load_g(i + 1)
                sp.wait_ge(z_ready, base + i + 1 + START)
                sp.dma_start(S.YC[f, :, at:at + n], Z[i % 2][:, 0:n]).then_inc(stored, 16)
                sp.wait_ge(stored, 16 * (base + i + 1) + START)

        @block.scalar
        def _(act):
            for i, (at, n, f) in enumerate(xjobs):
                act.wait_ge(y_ready, i + 1 + START)
                if i >= 1:
                    act.wait_ge(z_ready, i + START)
                act.activation(TH[:, 0:n], Y[i % 2][:, 0:n], ACT.Tanh).then_inc(th_ready, 1)

        @block.gpsimd
        def _(pool):
            for i in range(2):
                pool.memset(XB[i][:, 0:1], 0.0)
                pool.memset(XB[i][:, LAT + 1:LAT + 2], 0.0)
                pool.memset(GB[i][:, 0:half], 0.0)
                ins = pool.memset(GB[i][:, LAT + half:LAT + 2 * half], 0.0)
            ins.then_inc(padded, 1)

        @block.vector
        def _(dve):
            step = Chain(dve, dch)
            dve.wait_ge(small, 16 * 8 + START)
            step(dve.tensor_scalar(cw[:, :, :], cw[:, :, :], 0.5, None, ALU.mult))
            step(dve.tensor_scalar(cb[:, :], cb[:, :], 0.5, None, ALU.mult))
            step(dve.tensor_scalar(fw[:, :, :], fw[:, :, :], 0.5, None, ALU.mult))
            dve.wait_ge(padded, 1 + START)

            def silu(i):
                at, n, f = xjobs[i]
                dve.wait_ge(th_ready, i + 1 + START)
                if i >= 2:
                    dve.wait_ge(stored, 16 * (i - 1) + START)
                emit(dve.scalar_tensor_tensor(Z[i % 2][:, 0:n], TH[:, 0:n], 1.0, Y[i % 2][:, 0:n], ALU.add, ALU.mult),
                     z_ready, dve, i + 1)

            for i, (at, n, f) in enumerate(xjobs):
                X, y = XB[i % 2], Y[i % 2]
                dve.wait_ge(x_loaded, 16 * (i + 1) + START)
                if n == P and i >= len(xjobs) - 2:
                    pass
                if n == P:
                    step(dve.memset(X[:, 1 + n:2 + n], 0.0))
                step(dve.tensor_scalar(y[:, 0:n], X[:, 1:1 + n], cw[:, f, 1:2], cb[:, f:f + 1], ALU.mult, ALU.add))
                step(dve.scalar_tensor_tensor(y[:, 0:n], X[:, 0:n], cw[:, f, 0:1], y[:, 0:n], ALU.mult, ALU.add))
                emit(dve.scalar_tensor_tensor(y[:, 0:n], X[:, 2:2 + n], cw[:, f, 2:3], y[:, 0:n], ALU.mult, ALU.add),
                     y_ready, dve, i + 1)
                if i >= 1:
                    silu(i - 1)
            silu(len(xjobs) - 1)
            base = len(xjobs)
            for i, (at, n, f) in enumerate(gjobs):
                X, z = GB[i % 2], Z[i % 2]
                dve.wait_ge(g_loaded, 16 * (i + 1) + START)
                dve.wait_ge(stored, 16 * (base + i - 1) + START)
                if n == P:
                    step(dve.memset(X[:, half + n:2 * half + n], 0.0))
                step(dve.tensor_scalar(z[:, 0:n], X[:, 0:n], fw[:, f, 0:1], fb[:, f:f + 1], ALU.mult, ALU.add))
                for k in range(1, KW):
                    ins = dve.scalar_tensor_tensor(z[:, 0:n], X[:, k:k + n], fw[:, f, k:k + 1], z[:, 0:n], ALU.mult, ALU.add)
                    if k < KW - 1:
                        step(ins)
                    else:
                        emit(ins, z_ready, dve, base + i + 1)


def scan_phase(nc, A, K, S, l):
    W4 = 4 * HD
    AFTER, BEFORE, UPTO, FROM = range(4)
    with ExitStack() as xs_:
        s = Scope(nc, xs_, f"scan{l}")
        dt = s.sb("dt", [P, NT, 8])
        dA = s.sb("dA", [P, NT, 8])
        Sb = [s.sb(f"Sb{i}", [P, W4]) for i in range(2)]
        Sp = [s.sb(f"Sp{i}", [P, 2 * W4]) for i in range(2)]
        Sc = s.sb("Sc", [P, W4])
        init = s.sb("init", [P, 2, W4])
        _scan_prepare(nc, A, K, S, l, dt, dA, Sb, Sp, init)
        _scan_backward(nc, A, K, S, l, dt, dA, Sb, Sc, init)
        _scan_forward(nc, A, K, S, l, dt, dA, Sp, Sc, init)


def _scan_prepare(nc, A, K, S, l, dt, dA, Sb, Sp, init):
    with ExitStack() as x:
        s = Scope(nc, x, f"prep{l}")
        n8 = [P, NT, 8]
        bias = s.sb("bias", [P, 8])
        al = s.sb("al", [P, 8])
        t, u, d, e, g = (s.sb(n, n8) for n in ("t", "u", "d", "e", "g"))
        si = s.sb("si", [P, 2, 2, P])
        pt = s.ps("pt", [P, 512])
        loaded, zeroed, s_loaded, t_ready, u_ready, ln_ready, turned, dch = (
            s.sem(n) for n in ("loaded", "zeroed", "s_loaded", "t_ready", "u_ready", "ln_ready", "turned", "dve_steps"))
        block = s.block()

        @block.sync
        def _(sp):
            with nc.allow_non_contiguous_dma(reason="narrow rows"):
                sp.dma_start(dt[:, :, :], S.DT.rearrange("(n p) c -> p n c", p=P)).then_inc(loaded, 16)
                sp.dma_start(bias[:, :], A["ssd_dt_bias"][l].rearrange("d h -> (d h)").partition_broadcast(P)).then_inc(loaded, 16)
                sp.dma_start(al[:, :], A["ssd_a_log"][l].rearrange("d h -> (d h)").partition_broadcast(P)).then_inc(loaded, 16)
                sp.wait_ge(zeroed, 1 + START)
                for dr in range(2):
                    for grp in range(2):
                        sp.dma_start(si[:, dr, grp, grp * HD:(grp + 1) * HD],
                                     A["state_ssd"][0, l, dr, 2 * grp:2 * grp + 2].rearrange("h p n -> (h p) n")).then_inc(s_loaded, 16)

        @block.gpsimd
        def _(pool):
            for i in range(2):
                pool.memset(Sb[i][:, :], 0.0)
                pool.memset(Sp[i][:, :], 0.0)
            pool.memset(si[:, :, :, :], 0.0).then_inc(zeroed, 1)

        @block.tensor
        def _(pe):
            pe.wait_ge(s_loaded, 64 + START)
            for i in range(4):
                mm = pe.transpose(pt[:, i * P:(i + 1) * P], si[:, i // 2, i % 2, :], K.ident[:, :])
            mm.then_inc(turned, 1)

        @block.scalar
        def _(act):
            act.wait_ge(t_ready, 1 + START)
            act.activation(t[:, :, :], t[:, :, :], ACT.Exp)
            act.activation(al[:, :], al[:, :], ACT.Exp).then_inc(u_ready, 1)
            act.wait_ge(t_ready, 2 + START)
            act.activation(g[:, :, :], u[:, :, :], ACT.Ln).then_inc(ln_ready, 1)

        @block.vector
        def _(dve):
            step = Chain(dve, dch)
            dve.wait_ge(loaded, 48 + START)
            step(dve.tensor_tensor(dt[:, :, :], dt[:, :, :], bias[:, :].unsqueeze(1).broadcast_to(n8), ALU.add))
            emit(dve.scalar_tensor_tensor(t[:, :, :], dt[:, :, :], -1.0, dt[:, :, :], ALU.mult, ALU.min), t_ready, dve, 1)
            dve.wait_ge(u_ready, 1 + START)
            emit(dve.tensor_scalar(u[:, :, :], t[:, :, :], 1.0, None, ALU.add), t_ready, dve, 2)
            step(dve.tensor_scalar(d[:, :, :], u[:, :, :], -1.0, None, ALU.add))
            step(dve.tensor_scalar(e[:, :, :], d[:, :, :], 0.0, None, ALU.is_equal))
            step(dve.tensor_tensor(d[:, :, :], d[:, :, :], e[:, :, :], ALU.add))
            step(dve.reciprocal(d[:, :, :], d[:, :, :]))
            dve.wait_ge(ln_ready, 1 + START)
            step(dve.tensor_tensor(g[:, :, :], g[:, :, :], e[:, :, :], ALU.add))
            step(dve.tensor_tensor(g[:, :, :], g[:, :, :], t[:, :, :], ALU.mult))
            step(dve.tensor_tensor(g[:, :, :], g[:, :, :], d[:, :, :], ALU.mult))
            step(dve.scalar_tensor_tensor(dt[:, :, :], dt[:, :, :], 0.0, g[:, :, :], ALU.max, ALU.add))
            step(dve.scalar_tensor_tensor(dA[:, :, :], dt[:, :, :], -1.0, al[:, :].unsqueeze(1).broadcast_to(n8),
                                          ALU.mult, ALU.mult))
            dve.wait_ge(turned, 1 + START)
            step(dve.tensor_copy(init[:, :, :], pt[:, :]))


def state_update(dve, step, last, new, old, decay, made):
    for g in range(2):
        rows, cols = slice(g * HD, (g + 1) * HD), slice(2 * g * HD, (2 * g + 2) * HD)
        dec = decay[rows, 2 * g:2 * g + 2].unsqueeze(2).broadcast_to([HD, 2, HD])

        def v(ap):
            return ap[rows, cols].rearrange("p (h d) -> p h d", h=2)

        step(dve.tensor_tensor(v(new), v(old), dec, ALU.mult))
        (last if g else step)(dve.tensor_tensor(v(new), v(new), v(made), ALU.add))


def _scan_backward(nc, A, K, S, l, dt, dA, Sb, Sc, init):
    W4 = 4 * HD
    AFTER, BEFORE, UPTO, FROM = range(4)
    with ExitStack() as x:
        s = Scope(nc, x, f"back{l}")
        X = [s.sb(f"X{i}", [P, 3, P]) for i in range(2)]
        XT = [s.sb(f"XT{i}", [P, 3 * P]) for i in range(2)]
        ex = [s.sb(f"ex{i}", [P, 8]) for i in range(2)]
        wt = s.sb("wt", [P, 4])
        xw = [s.sb(f"xw{i}", [P, 4, HD]) for i in range(2)]
        pt = [s.ps(f"pt{i}", [P, 512]) for i in range(2)]
        ps = [s.ps(f"ps{i}", [P, 512]) for i in range(2)]
        x_loaded = [s.sem(f"x_loaded{i}") for i in range(2)]
        stored = [s.sem(f"stored{i}") for i in range(2)]
        turned, xt_ready, xw_ready, st_done, s_ready, dch, ach, first = (
            s.sem(n) for n in ("turned", "xt_ready", "xw_ready", "st_done", "s_ready", "dve_steps",
                               "act_steps", "first"))
        block = s.block()

        def walk(eng, body):
            body(0, 0, 1, CTX, 0)
            with eng.Fori(0, NLAT // 2) as j:
                ns = [j * -2 + (NLAT - 1 - u) for u in range(2)]
                for u in range(2):
                    body(j * 2 + (u + 1), (u + 1) % 2, j + (u + 1), ns[u], 1 + u)

        @block.sync
        def _(sp):
            def load(n, par):
                sp.dma_start(X[par][:, :, :], S.XC[0:3, :, bass.ds(n * P, P)].rearrange("f p t -> p f t")).then_inc(x_loaded[par], 16)

            load(CTX, 0)

            def body(k, par, cnt, n, kind):
                if kind == 0:
                    load(NLAT - 1, 1)
                else:
                    sp.wait_ge(s_ready, k + START)
                    sp.dma_start(S.SB[bass.ds(n, 1), :, :].rearrange("n p c -> p (n c)"), Sb[par][:, :]).then_inc(stored[par], 16)

            body(0, 0, 1, CTX, 0)
            with sp.Fori(0, NLAT // 2 - 1) as j:
                ns = [j * -2 + (NLAT - 1 - u) for u in range(3)]
                for u in range(2):
                    k, n = j * 2 + (u + 1), ns[u]
                    sp.wait_ge(turned, k + START)
                    load(ns[u + 1], u % 2)
                    body(k, (u + 1) % 2, 0, n, 1)
            k = NLAT - 1
            sp.wait_ge(turned, k + START)
            load(0, 0)
            body(k, 1, 0, 1, 1)
            body(k + 1, 0, 0, 0, 1)
            for i in range(2):
                sp.wait_ge(stored[i], 16 * NLAT // 2 + START)

        @block.tensor
        def _(pe):
            def body(k, par, cnt, n, kind):
                pe.wait_ge(x_loaded[par], cnt * 16 + START)
                if kind:
                    pe.wait_ge(xt_ready, k + START)
                for f in range(3):
                    pe.transpose(pt[par][:, f * P:(f + 1) * P], X[par][:, f, :], K.ident[:, :])
                rhs = dA[:, bass.ds(n, 1), 4:8].rearrange("p n c -> p (n c)")
                pe.matmul(pt[par][:, 384:388], K.tri[:, BEFORE, :], rhs, start=True, stop=True)
                pe.matmul(pt[par][:, 388:392], K.ones[:, :], rhs, start=True, stop=True).then_inc(turned, 1)
                pe.wait_ge(xw_ready, k + 1 + START)
                pe.matmul(ps[par][:, 0:W4], XT[par][:, 2 * P:3 * P], xw[par][:, :, :].rearrange("p h d -> p (h d)"),
                          start=True, stop=True).then_inc(st_done, 1)

            walk(pe, body)

        @block.scalar
        def _(act):
            step = Chain(act, ach, 1)

            def body(k, par, cnt, n, kind):
                step.tile(k)
                act.wait_ge(turned, k + 1 + START)
                if kind:
                    act.wait_ge(s_ready, k + START)
                    act.wait_ge(st_done, k + START)
                step(act.activation(ex[par][:, :], pt[par][:, 384:392], ACT.Exp))
                emit(act.activation(XT[par][:, :], pt[par][:, 0:384], ACT.Copy), xt_ready, act, k + 1)

            walk(act, body)

        @block.vector
        def _(dve):
            step = Chain(dve, dch, 4)
            emit(dve.tensor_copy(Sc[:, :], Sb[0][:, :]), first, dve, 1)

            def body(k, par, cnt, n, kind):
                step.tile(k)
                dve.wait_ge(xt_ready, k + 1 + START)
                step(dve.tensor_tensor(wt[:, :], ex[par][:, 0:4], dt[:, bass.ds(n, 1), 4:8].rearrange("p n c -> p (n c)"), ALU.mult))
                emit(dve.tensor_tensor(xw[par][:, :, :], XT[par][:, 0:W4].rearrange("p (h d) -> p h d", h=4),
                                       wt[:, :].unsqueeze(2).broadcast_to([P, 4, HD]), ALU.mult), xw_ready, dve, k + 1)
                dve.wait_ge(st_done, k + 1 + START)
                new = Sc if kind == 0 else Sb[1 - par]
                if kind:
                    dve.wait_ge(stored[1 - par], (cnt - 1) * 16 + START)

                def last(ins):
                    if kind:
                        emit(ins, s_ready, dve, k + 1)
                    else:
                        emit(ins, first, dve, 2)
                state_update(dve, step, last, new, Sb[par], ex[par][:, 4:8], ps[par])
                if kind == 0:
                    emit(dve.tensor_copy(Sb[1][:, :], init[:, 1, :]), s_ready, dve, 1)

            walk(dve, body)


def _scan_forward(nc, A, K, S, l, dt, dA, Sp, Sc, init):
    W4 = 4 * HD
    AFTER, BEFORE, UPTO, FROM = range(4)
    with ExitStack() as x:
        s = Scope(nc, x, f"fwd{l}")
        X = [s.sb(f"X{i}", [P, 4, P]) for i in range(2)]
        Y = [s.sb(f"Y{i}", [P, 2, P]) for i in range(2)]
        Z = [s.sb(f"Z{i}", [P, 256]) for i in range(2)]
        XT = s.sb("XT", [P, 3 * P])
        YT = s.sb("YT", [P, 256])
        dts, dAs = s.sb("dts", [P, 8]), s.sb("dAs", [P, 8])
        R = s.sb("R", [P, 2, 4, P])
        L = s.sb("L", [P, 2, 4, P])
        G = s.sb("G", [P, 2, 2, P])
        ex = s.sb("ex", [P, 16])
        wt = s.sb("wt", [P, 4])
        xw = s.sb("xw", [P, 4, HD])
        xdt = s.sb("xdt", [P, 2, 4, HD])
        xd = s.sb("xd", [P, 4, HD])
        T = s.sb("T", [P, 8, HD])
        y = s.sb("y", [P, 256])
        ysq = s.sb("ysq", [P, 256])
        cst = s.sb("cst", [P, 6])
        mv = s.sb("mv", [P, 2])
        md = s.sb("md", [P, 1])
        vv, rr, tt = (s.sb(n, [P, 2]) for n in ("vv", "rr", "tt"))
        ct = s.sb("ct", [P, 256])
        cth = s.sb("cth", [P, 256])
        OB = [s.sb(f"OB{i}", [P, 512]) for i in range(2)]
        dsk = s.sb("dsk", [P, 4])
        ng = s.sb("ng", [P, 256])
        lg = s.sb("lg", [P, 256])
        lb = s.sb("lb", [P, 256])
        fin = s.sb("fin", [P, 4, HD])
        pA, pB, pG, pF, pR, pY, pO, pT = (s.ps(n, [P, 512]) for n in ("pA", "pB", "pG", "pF", "pR", "pY", "pO", "pT"))
        small = s.sem("small")
        loaded = [s.sem(f"loaded{i}") for i in range(2)]
        stored = [s.sem(f"stored{i}") for i in range(2)]
        names = ("turned dts_ready R_ready xt_ready ex_ready G_done seg_done L_ready M_ready y_done off_done y_ready "
                 "ysq_ready c_ready cth_ready ob_ready xw_ready st_done s_ready fin_turned fin_ready xd_ready "
                 "f_stored dve_steps act_steps pool_steps gains").split()
        q = {n: s.sem(n) for n in names}
        block = s.block()

        def walk(eng, body, after=None):
            body(0, 0, 1, CTX, 0)
            if after:
                after()
            with eng.Fori(0, NLAT // 2) as j:
                for u in range(2):
                    body(j * 2 + (u + 1), (u + 1) % 2, j + (u + 1), j * 2 + u, 1)

        def flat(ap):
            return ap.rearrange("p n c -> p (n c)")

        def h4(ap):
            return ap.rearrange("p (h d) -> p h d", d=HD)

        def per_head(ap, w=HD):
            return ap.unsqueeze(2).broadcast_to([P, ap.shape[-1], w])

        @block.sync
        def _(sp):
            with nc.allow_non_contiguous_dma(reason="broadcast gains"):
                for t, src in ((dsk, "ssd_d"), (ng, "ssd_norm_g"), (lg, "cf_ln_g"), (lb, "cf_ln_b")):
                    sp.dma_start(t[:, :], A[src][l].partition_broadcast(P)).then_inc(small, 16)

            def load(n, par, ctx=False):
                sp.dma_start(X[par][:, :, :], S.XC[:, :, bass.ds(n * P, P)].rearrange("f p t -> p f t")).then_inc(loaded[par], 16)
                sp.dma_start(Y[par][:, :, :], S.YC[:, :, bass.ds(n * P, P)].rearrange("f p t -> p f t")).then_inc(loaded[par], 16)
                sp.dma_start(Z[par][:, :], S.G[bass.ds(n * P, P), 256:512]).then_inc(loaded[par], 16)
                if not ctx:
                    sp.dma_start(Sp[par][:, W4:2 * W4], S.SB[bass.ds(n, 1), :, :].rearrange("n p c -> p (n c)")).then_inc(loaded[par], 16)

            def store(k, par, n):
                sp.wait_ge(q["ob_ready"], k + 1 + START)
                sp.dma_start(S.O[bass.ds(n * P, P), 512:D], OB[par][:, :]).then_inc(stored[par], 16)

            load(CTX, 0, True)
            load(0, 1)
            store(0, 0, CTX)
            with sp.Fori(0, NLAT // 2 - 1) as j:
                for u in range(2):
                    sp.wait_ge(q["st_done"], j * 2 + (u + 1) + START)
                    load(j * 2 + (u + 1), u)
                    store(j * 2 + (u + 1), (u + 1) % 2, j * 2 + u)
            load(NLAT - 1, 0)
            store(NLAT - 1, 1, NLAT - 2)
            store(NLAT, 0, NLAT - 1)
            sp.wait_ge(q["fin_ready"], 1 + START)
            for dr in range(2):
                for g in range(2):
                    sp.dma_start(A["new_state_ssd"][0, l, dr, 2 * g:2 * g + 2].rearrange("h p n -> (h p) n"),
                                 fin[:, 2 * dr + g, :]).then_inc(q["f_stored"], 16)
            sp.wait_ge(stored[0], 16 * (NT + 1) // 2 + START)
            sp.wait_ge(stored[1], 16 * NLAT // 2 + START)
            sp.wait_ge(q["f_stored"], 64 + START)

        @block.tensor
        def _(pe):
            def body(k, par, cnt, n, kind):
                if kind:
                    pe.wait_ge(loaded[par], 64 * cnt - (16 if par == 0 else 0) + START)
                    pe.wait_ge(q["s_ready"], k + 1 + START)
                    pe.wait_ge(q["ob_ready"], k + START)
                else:
                    pe.wait_ge(loaded[par], 48 + START)
                for f in range(3):
                    pe.transpose(pA[:, f * P:(f + 1) * P], X[par][:, f, :], K.ident[:, :])
                for f in range(2):
                    pe.transpose(pB[:, f * P:(f + 1) * P], Y[par][:, f, :], K.ident[:, :])
                f4, b4 = flat(dA[:, bass.ds(n, 1), 0:4]), flat(dA[:, bass.ds(n, 1), 4:8])
                for i, (tri, d4) in enumerate(((K.tri[:, AFTER, :], f4), (K.tri[:, UPTO, :], f4),
                                               (K.tri[:, FROM, :], b4), (K.ones[:, :], f4))):
                    mm = pe.matmul(pA[:, 384 + 4 * i:388 + 4 * i], tri, d4, start=True, stop=True)
                mm.then_inc(q["turned"], 1)
                for g in range(2):
                    rows = slice(g * HD, (g + 1) * HD)
                    mm = pe.matmul((pG if g == 0 else pT)[:, 0:P], X[par][rows, 2, :], X[par][rows, 3, :],
                                   start=True, stop=True)
                mm.then_inc(q["G_done"], 1)
                pe.matmul(pO[:, :], X[par][:, 3, :], Sp[par][:, :], start=True, stop=True).then_inc(q["off_done"], 1)
                pe.wait_ge(q["R_ready"], 2 * k + 2 + START)
                pe.matmul(pF[:, :], K.tri[:, AFTER, :], R[:, 0, :, :].rearrange("p h i -> p (h i)"), start=True, stop=True)
                pe.matmul(pR[:, :], K.tri[:, BEFORE, :], R[:, 1, :, :].rearrange("p h i -> p (h i)"),
                          start=True, stop=True).then_inc(q["seg_done"], 1)
                pe.wait_ge(q["M_ready"], k + 1 + START)
                for h in range(4):
                    cols = slice(h * HD, (h + 1) * HD)
                    pe.matmul(pY[:, cols], L[:, 0, h, :], xdt[:, 0, h, :], start=True, stop=False)
                    mm = pe.matmul(pY[:, cols], L[:, 1, h, :], xdt[:, 1, h, :], start=False, stop=True)
                mm.then_inc(q["y_done"], 1)
                pe.wait_ge(q["xw_ready"], k + 1 + START)
                pe.matmul(pT[:, 0:W4], XT[:, 2 * P:3 * P], xw[:, :, :].rearrange("p h d -> p (h d)"),
                          start=True, stop=True).then_inc(q["st_done"], 1)

            def after():
                pe.wait_ge(q["s_ready"], 1 + START)
                for i in range(4):
                    src = Sp[1][:, :] if i < 2 else Sc[:, :]
                    mm = pe.transpose(pF[:, i * P:(i + 1) * P], src[:, (i % 2) * P:(i % 2 + 1) * P], K.ident[:, :])
                mm.then_inc(q["fin_turned"], 1)
                pe.wait_ge(q["fin_ready"], 1 + START)

            walk(pe, body, after)

        @block.scalar
        def _(act):
            step = Chain(act, q["act_steps"], 1)

            def body(k, par, cnt, n, kind):
                step.tile(k)
                act.wait_ge(q["turned"], k + 1 + START)
                emit(act.activation(ex[:, :], pA[:, 384:400], ACT.Exp), q["ex_ready"], act, k + 1)
                emit(act.activation(XT[:, :], pA[:, 0:384], ACT.Copy), q["xt_ready"], act, k + 1)
                act.wait_ge(q["seg_done"], k + 1 + START)
                step(act.activation(L[:, 0, :, :], pF[:, :], ACT.Exp))
                emit(act.activation(L[:, 1, :, :], pR[:, :], ACT.Exp), q["L_ready"], act, k + 1)
                act.wait_ge(q["c_ready"], k + 1 + START)
                emit(act.activation(cth[:, :], ct[:, :], ACT.Tanh), q["cth_ready"], act, k + 1)
                act.wait_ge(q["y_ready"], k + 1 + START)
                emit(act.activation(ysq[:, :], y[:, :], ACT.Square, accum_out=vv[:, 0:1]), q["ysq_ready"], act, k + 1)

            def after():
                act.wait_ge(q["fin_turned"], 1 + START)
                for i in range(4):
                    g = i % 2
                    ins = act.activation(fin[:, i, :], pF[:, i * P + g * HD:i * P + (g + 1) * HD], ACT.Copy)
                emit(ins, q["fin_ready"], act, 1)

            walk(act, body, after)

        @block.gpsimd
        def _(pool):
            def body(k, par, cnt, n, kind):
                pool.wait_ge(q["dts_ready"], k + 1 + START)
                if kind:
                    pool.wait_ge(q["seg_done"], k + START)
                for dr, tri in ((0, UPTO), (1, FROM)):
                    emit(pool.tensor_tensor(R[:, dr, :, :], K.tri[:, tri, :].unsqueeze(1).broadcast_to([P, 4, P]),
                                            per_head(dAs[:, 4 * dr:4 * dr + 4], P), ALU.mult),
                         q["R_ready"], pool, 2 * k + 1 + dr)
                pool.wait_ge(q["xt_ready"], k + 1 + START)
                if kind:
                    pool.wait_ge(q["y_ready"], k + START)
                emit(pool.tensor_tensor(xd[:, :, :], h4(XT[:, 0:W4]), per_head(dsk[:, :]), ALU.mult),
                     q["xd_ready"], pool, k + 1)

            pool.wait_ge(small, 64 + START)
            walk(pool, body)

        @block.vector
        def _(dve):
            setup = Chain(dve, q["gains"])
            dve.wait_ge(small, 64 + START)
            setup(dve.tensor_scalar(lg[:, :], lg[:, :], 0.5, None, ALU.mult))
            setup(dve.tensor_scalar(lb[:, :], lb[:, :], 0.5, None, ALU.mult))
            step = Chain(dve, q["dve_steps"], 1 + 7 + RSQRT + 2 + 2 + 1 + 4 + 1 + 4 + 3 + 1 + RSQRT + 1)

            def body(k, par, cnt, n, kind):
                step.tile(k)
                if kind:
                    dve.wait_ge(q["R_ready"], 2 * k + START)
                step(dve.tensor_copy(dts[:, :], flat(dt[:, bass.ds(n, 1), :])))
                emit(dve.tensor_copy(dAs[:, :], flat(dA[:, bass.ds(n, 1), :])), q["dts_ready"], dve, k + 1)
                dve.wait_ge(q["turned"], k + 1 + START)
                step(dve.bn_stats(cst[:, :], pB[:, 0:256]))
                halves_ = cst[:, :].rearrange("p (o c) -> p o c", o=2)
                step(dve.tensor_tensor(mv[:, :], halves_[:, 0, 1:3], halves_[:, 1, 1:3], ALU.add))
                step(dve.tensor_tensor(md[:, 0:1], cst[:, 1:2], cst[:, 4:5], ALU.subtract))
                step(dve.scalar_tensor_tensor(md[:, 0:1], md[:, 0:1], 0.25, md[:, 0:1], ALU.mult, ALU.mult))
                step(dve.scalar_tensor_tensor(md[:, 0:1], mv[:, 1:2], 1.0 / 256, md[:, 0:1], ALU.mult, ALU.add))
                step(dve.tensor_scalar(vv[:, 1:2], md[:, 0:1], EPS, None, ALU.add))
                step(dve.tensor_scalar(mv[:, 0:1], mv[:, 0:1], 0.5, None, ALU.mult))
                rsqrt_steps(dve, step, rr[:, 1:2], vv[:, 1:2], tt[:, 1:2])
                step(dve.tensor_scalar(ct[:, :], pB[:, 0:256], mv[:, 0:1], rr[:, 1:2], ALU.subtract, ALU.mult))
                step(dve.tensor_tensor(ct[:, :], ct[:, :], lg[:, :], ALU.mult))
                emit(dve.tensor_tensor(ct[:, :], ct[:, :], lb[:, :], ALU.add), q["c_ready"], dve, k + 1)
                dve.wait_ge(q["xt_ready"], k + 1 + START)
                xs = h4(XT[:, 0:W4])
                for dr in range(2):
                    step(dve.tensor_tensor(xdt[:, dr, :, :], xs, per_head(dts[:, 4 * dr:4 * dr + 4]), ALU.mult))
                dve.wait_ge(q["ex_ready"], k + 1 + START)
                step(dve.tensor_tensor(wt[:, :], dts[:, 0:4], ex[:, 0:4], ALU.mult))
                emit(dve.tensor_tensor(xw[:, :, :], xs, per_head(wt[:, :]), ALU.mult), q["xw_ready"], dve, k + 1)
                dve.wait_ge(q["G_done"], k + 1 + START)
                for g in range(2):
                    for dr, tri in ((0, UPTO), (1, FROM)):
                        step(dve.tensor_tensor(G[:, dr, g, :], (pG if g == 0 else pT)[:, 0:P], K.tri[:, tri, :], ALU.mult))
                dve.wait_ge(q["L_ready"], k + 1 + START)
                for dr in range(2):
                    Lv = L[:, dr, :, :].rearrange("p (g r) i -> p g r i", g=2)
                    ins = dve.tensor_tensor(Lv, Lv, G[:, dr, :, :].unsqueeze(2).broadcast_to([P, 2, 2, P]), ALU.mult)
                    if dr == 0:
                        step(ins)
                    else:
                        emit(ins, q["M_ready"], dve, k + 1)
                dve.wait_ge(q["off_done"], k + 1 + START)
                step(dve.tensor_tensor(T[:, :, :], h4(pO[:, :]), per_head(ex[:, 4:12]), ALU.mult))
                step(dve.tensor_tensor(T[:, 0:4, :], T[:, 0:4, :], T[:, 4:8, :], ALU.add))
                dve.wait_ge(q["xd_ready"], k + 1 + START)
                step(dve.tensor_tensor(T[:, 0:4, :], T[:, 0:4, :], xd[:, :, :], ALU.add))
                dve.wait_ge(q["y_done"], k + 1 + START)
                step(dve.tensor_tensor(y[:, :], pY[:, 0:256], T[:, 0:4, :].rearrange("p h d -> p (h d)"), ALU.add))
                emit(dve.scalar_tensor_tensor(y[:, :], y[:, :], 0.5, Z[par][:, :], ALU.mult, ALU.mult), q["y_ready"], dve, k + 1)
                dve.wait_ge(q["st_done"], k + 1 + START)
                if kind:
                    state_update(dve, step, lambda i: emit(i, q["s_ready"], dve, k + 2), Sp[1 - par], Sp[par], ex[:, 12:16], pT)
                else:
                    state_update(dve, step, lambda i: emit(i, q["s_ready"], dve, 1), Sp[1], Sp[0], ex[:, 12:16], pT)
                    dve.wait_ge(q["fin_turned"], 1 + START)
                    emit(dve.tensor_copy(Sp[1][:, 0:W4], init[:, 0, :]), q["s_ready"], dve, 2)
                dve.wait_ge(q["ysq_ready"], k + 1 + START)
                step(dve.tensor_scalar(vv[:, 0:1], vv[:, 0:1], 1.0 / 256, EPS, ALU.mult, ALU.add))
                rsqrt_steps(dve, step, rr[:, 0:1], vv[:, 0:1], tt[:, 0:1])
                if kind:
                    dve.wait_ge(stored[par], (cnt - 1) * 16 + START)
                step(dve.scalar_tensor_tensor(OB[par][:, 0:256], y[:, :], rr[:, 0:1], ng[:, :], ALU.mult, ALU.mult))
                dve.wait_ge(q["cth_ready"], k + 1 + START)
                emit(dve.scalar_tensor_tensor(OB[par][:, 256:512], cth[:, :], 1.0, ct[:, :], ALU.add, ALU.mult),
                     q["ob_ready"], dve, k + 1)
                step.end()

            walk(dve, body)


def attention_phase(nc, A, K, S, l):
    NKT = NLAT + 1
    KEYS = NKT * P
    R1 = QK + 1
    NB = 4
    BODY = 2 * NB
    NPAIR = (NKT + 1) // 2
    CH = [436, 436, 436, 436, 432]
    CA = [0, 436, 872, 1308, 1744]
    NCH = 4 * len(CH)
    CHUNKS_AT = [3, 3, 3, 3, 3, 3, 2, 0, 0]
    with ExitStack() as x:
        s = Scope(nc, x, f"attn{l}")
        kraw = s.sb("kraw", [QK, KEYS])
        qraw = s.sb("qraw", [QK, LAT])
        Kh = [s.sb(f"Kh{i}", [R1, KEYS], F32R) for i in range(2)]
        Kl = [s.sb(f"Kl{i}", [R1, KEYS], F32R) for i in range(2)]
        Qh = [s.sb(f"Qh{i}", [R1, LAT], F32R) for i in range(2)]
        Ql = [s.sb(f"Ql{i}", [R1, LAT], F32R) for i in range(2)]
        V = [s.sb(f"V{i}", [P, NKT, HD]) for i in range(2)]
        Pb = [s.sb(f"Pb{i}", [P, 1024]) for i in range(3)]
        acc = [s.sb(f"acc{i}", [P, 1024]) for i in range(2)]
        OTs = s.sb("OTs", [P, 512])
        mx = s.sb("mx", [P, 4, len(CH)])
        mt = s.sb("mt", [P, 4, R1])
        den = s.sb("den", [P, 4])
        Ost = [s.sb(f"Ost{i}", [P, 4, HD]) for i in range(2)]
        p1 = [s.ps(f"p1{i}", [P, 512]) for i in range(2)]
        ST = [s.ps(f"ST{i}", [P, 1024]) for i in range(2)]
        OT = s.ps("OT", [P, 512])
        misc = s.ps("misc", [P, 512])
        names = ("k_loaded q_loaded v_loaded0 v_loaded1 init hi_ready split_ready st_done exp_done pv_done acc_done "
                 "p1_done red_done negm_ready mrow_done mrow_ready ot_copied fin_done o_ready stored0 stored1 "
                 "dve_steps pool_steps").split()
        q = {n: s.sem(n) for n in names}
        block = s.block()

        def walk(eng, body):
            with eng.Fori(0, 3) as j:
                body(j, False)
            body(3, True)

        @block.sync
        def _(sp):
            def body(j, final):
                for hb in range(2):
                    for b in range(NB):
                        i = NB * hb + b
                        sp.wait_ge(q["o_ready"], j * BODY + i + 1 + START)
                        sp.dma_start(S.O[b * 512:(b + 1) * 512, bass.ds((j * 2 + hb) * HD, HD)].rearrange("(t p) d -> p t d", p=P),
                                     Ost[b % 2][:, :, :]).then_inc(q[f"stored{b % 2}"], 16)

            walk(sp, body)
            for i in range(2):
                sp.wait_ge(q[f"stored{i}"], 16 * NH * NB // 2 + START)

        @block.gpsimd
        def _(pool):
            init = Chain(pool, q["init"])
            for i in range(2):
                init(pool.memset(Kh[i][QK:R1, :].bitcast(F32), 1.0))
                init(pool.memset(Kl[i][QK:R1, :].bitcast(F32), 0.0))
                init(pool.memset(Ql[i][QK:R1, :].bitcast(F32), 0.0))
            init(pool.memset(mt[:, :, :], 0.0))
            step = Chain(pool, q["pool_steps"], 3)

            def split(h, par):
                step.tile(h)
                pool.wait_ge(q["k_loaded"], h * 16 + 16 + START)
                step(pool.tensor_tensor(Kh[par][0:QK, :], kraw[:, :], K.ones[0:QK, 0:1].broadcast_to([QK, KEYS]), ALU.mult))
                step(pool.tensor_tensor(Kl[par][0:QK, :], kraw[:, :], Kh[par][0:QK, :].bitcast(F32), ALU.subtract))
                pool.wait_ge(q["q_loaded"], h * 16 + 16 + START)
                step(pool.tensor_tensor(Qh[par][0:QK, :], qraw[:, :], K.ones[0:QK, 0:1].broadcast_to([QK, LAT]), ALU.mult))
                emit(pool.tensor_tensor(Ql[par][0:QK, :], qraw[:, :], Qh[par][0:QK, :].bitcast(F32), ALU.subtract),
                     q["split_ready"], pool, h + 1)

            split(0, 0)

            def body(j, final):
                for hb in range(2):
                    if not (final and hb):
                        pool.wait_ge(q["pv_done"], (j * BODY + NB * hb) * NPAIR + START)
                        split(j * 2 + hb + 1, 1 - hb)

            walk(pool, body)

        @block.tensor
        def _(pe):
            def first_pass(B, par, b, c):
                t, k = divmod(c, len(CH))
                if c >= 2:
                    pe.wait_ge(q["red_done"], B * NCH + c - 1 + START)
                else:
                    pe.wait_ge(q["red_done"], B * NCH + START)
                q0 = b * 512 + t * P
                pe.matmul(p1[c % 2][:, 0:CH[k]], Qh[par][0:QK, q0:q0 + P], Kh[par][0:QK, CA[k]:CA[k] + CH[k]],
                          start=True, stop=True).then_inc(q["p1_done"], 1)

            def max_row(B):
                pe.wait_ge(q["negm_ready"], B + 1 + START)
                for t in range(4):
                    mm = pe.matmul(misc[0:R1, t * P:(t + 1) * P], mt[:, t, :], K.ident[:, :], start=True, stop=True)
                mm.then_inc(q["mrow_done"], 1)

            def finish(B, i):
                pe.wait_ge(q["ot_copied"], B + 1 + START)
                pe.wait_ge(q["acc_done"], B * NPAIR + NPAIR + START)
                for t in range(4):
                    cols = slice(t * P, (t + 1) * P)
                    pe.matmul(misc[:, t * (HD + 1):t * (HD + 1) + HD], OTs[:, cols], K.ident2[:, :], start=True, stop=True)
                    for half in range(2):
                        mm = pe.matmul(misc[:, t * (HD + 1) + HD:(t + 1) * (HD + 1)],
                                       acc[i % 2][:, half * 512 + t * P:half * 512 + (t + 1) * P], K.ones[:, 0:1],
                                       start=(half == 0), stop=(half == 1))
                mm.then_inc(q["fin_done"], 1)

            def pv(B, i, p, par):
                pe.wait_ge(q["exp_done"], B * NPAIR + p + 1 + START)
                if p == 0:
                    pe.wait_ge(q["ot_copied"], B + START)
                for kt in range(2 * p, min(2 * p + 2, NKT)):
                    o = kt % 2
                    mm = pe.matmul(OT[o * HD:(o + 1) * HD, :], V[par][:, kt, :], Pb[p % 3][:, o * 512:(o + 1) * 512],
                                   start=(kt < 2), stop=(kt >= NKT - 2))
                mm.then_inc(q["pv_done"], 1)

            pe.wait_ge(q["split_ready"], 1 + START)
            pe.wait_ge(q["init"], 7 + START)
            for c in range(NCH):
                first_pass(0, 0, 0, c)
            max_row(0)

            def body(j, final):
                for i in range(BODY):
                    B, par, b = j * BODY + i, i // NB, i % NB
                    last = final and i == BODY - 1
                    npar, nb = ((i + 1) % BODY) // NB, (i + 1) % NB
                    pe.wait_ge(q["mrow_ready"], B + 1 + START)
                    if b == 0:
                        pe.wait_ge(q[f"v_loaded{par}"], j * 16 + 16 + START)
                    c = 0
                    for p in range(NPAIR):
                        buf = ST[(i + p) % 2]
                        pe.wait_ge(q["exp_done"], B * NPAIR + max(p - 1, 0) + START)
                        for kt in range(2 * p, min(2 * p + 2, NKT)):
                            out = buf[:, (kt % 2) * 512:(kt % 2 + 1) * 512]
                            ks, qs = slice(kt * P, (kt + 1) * P), slice(b * 512, (b + 1) * 512)
                            pe.matmul(out, Kh[par][:, ks], Qh[par][:, qs], start=True, stop=False)
                            pe.matmul(out, Kh[par][:, ks], Ql[par][:, qs], start=False, stop=False)
                            mm = pe.matmul(out, Kl[par][:, ks], Qh[par][:, qs], start=False, stop=True)
                        mm.then_inc(q["st_done"], 1)
                        if not last:
                            if p == 0 and nb == 0:
                                pe.wait_ge(q["split_ready"], j * 2 + par + 2 + START)
                            for _ in range(CHUNKS_AT[p]):
                                first_pass(B + 1, npar, nb, c)
                                c += 1
                        if p > 0:
                            pv(B, i, p - 1, par)
                        if p == 2 and i > 0:
                            finish(B - 1, i - 1)
                        if p == NPAIR - 2 and not last:
                            pe.wait_ge(q["o_ready"], B + START)
                            max_row(B + 1)
                    pv(B, i, NPAIR - 1, par)
                if not final:
                    pe.wait_ge(q["mrow_ready"], j * BODY + BODY + 1 + START)
                else:
                    pe.wait_ge(q["o_ready"], j * BODY + BODY - 1 + START)
                finish(j * BODY + BODY - 1, BODY - 1)

            walk(pe, body)

        @block.scalar
        def _(act):
            def row(B, b, par):
                act.wait_ge(q["mrow_done"], B + 1 + START)
                emit(act.activation(Qh[par][QK:R1, b * 512:(b + 1) * 512], misc[QK:R1, :], ACT.Copy), q["mrow_ready"], act, B + 1)

            def load(h, par):
                act.dma_start(kraw[:, :], S.KT[bass.ds(h, 1), :, 0:KEYS].rearrange("h r t -> r (h t)")).then_inc(q["k_loaded"], 16)
                act.dma_start(qraw[:, :], S.QT[bass.ds(h, 1), :, 0:LAT].rearrange("h r t -> r (h t)")).then_inc(q["q_loaded"], 16)
                act.dma_start(V[par][:, :, :], S.V[bass.ds(h, 1), :, 0:NKT, :].rearrange("h p s d -> p (h s d)")).then_inc(q[f"v_loaded{par}"], 16)

            load(0, 0)
            row(0, 0, 0)

            def body(j, final):
                for i in range(BODY):
                    B, par, b = j * BODY + i, i // NB, i % NB
                    last = final and i == BODY - 1
                    if b == 0 and not (final and par):
                        act.wait_ge(q["split_ready"], j * 2 + par + 1 + START)
                        act.wait_ge(q["pv_done"], B * NPAIR + START)
                        load(j * 2 + par + 1, 1 - par)
                    for p in range(NPAIR):
                        w = 1024 if p < NPAIR - 1 else 512
                        act.wait_ge(q["st_done"], B * NPAIR + p + 1 + START)
                        act.wait_ge(q["pv_done"], B * NPAIR + max(p - 2, 0) + START)
                        act.wait_ge(q["acc_done"], B * NPAIR + max(p - 2, 0) + START)
                        act.activation(Pb[p % 3][:, 0:w], ST[(i + p) % 2][:, 0:w], ACT.Exp).then_inc(q["exp_done"], 1)
                        if p == NPAIR - 2 and not last:
                            row(B + 1, (i + 1) % NB, ((i + 1) % BODY) // NB)
                    act.wait_ge(q["pv_done"], B * NPAIR + NPAIR + START)
                    act.wait_ge(q["fin_done"], B + START)
                    act.activation(OTs[:, :], OT[:, :], ACT.Copy).then_inc(q["ot_copied"], 1)

            walk(act, body)

        @block.vector
        def _(dve):
            step = Chain(dve, q["dve_steps"], 0)

            def reduce(B, c):
                t, k = divmod(c, len(CH))
                dve.wait_ge(q["p1_done"], B * NCH + c + 1 + START)
                dve.tensor_reduce(mx[:, t, k:k + 1], p1[c % 2][:, 0:CH[k]], AX.X, ALU.max).then_inc(q["red_done"], 1)

            def maxima(B):
                dve.wait_ge(q["red_done"], B * NCH + NCH + START)
                dve.tensor_reduce(mt[:, :, QK:R1], mx[:, :, :], AX.X, ALU.max, negate=True).then_inc(q["negm_ready"], 1)

            def output(B, i):
                dve.wait_ge(q["fin_done"], B + 1 + START)
                dve.wait_ge(q[f"stored{i % 2}"], out_count(B, i) + START)
                o = misc[:, 0:4 * (HD + 1)].rearrange("p (t d) -> p t d", d=HD + 1)
                emit(dve.reciprocal(den[:, :], o[:, :, HD]), q["dve_steps"], dve, B + 1)
                dve.tensor_tensor(Ost[i % 2][:, :, :], o[:, :, 0:HD], den[:, :].unsqueeze(2).broadcast_to([P, 4, HD]), ALU.mult)\
                    .then_inc(q["o_ready"], 1)

            def out_count(B, i):
                return (B - i) * 8 + (i // 2) * 16

            dve.wait_ge(q["init"], 7 + START)
            for c in range(NCH):
                reduce(0, c)
            maxima(0)

            def body(j, final):
                for i in range(BODY):
                    B = j * BODY + i
                    last = final and i == BODY - 1
                    c = 0

                    def add(p):
                        dve.wait_ge(q["exp_done"], B * NPAIR + p + 1 + START)
                        if p == 0:
                            if i == 0:
                                dve.wait_ge(q["fin_done"], B + START)
                            ins = dve.tensor_copy(acc[i % 2][:, :], Pb[0][:, :])
                        else:
                            dve.wait_ge(q["acc_done"], B * NPAIR + p + START)
                            w = 1024 if p < NPAIR - 1 else 512
                            ins = dve.tensor_tensor(acc[i % 2][:, 0:w], acc[i % 2][:, 0:w], Pb[p % 3][:, 0:w], ALU.add)
                        ins.then_inc(q["acc_done"], 1)

                    for p in range(NPAIR):
                        if not last:
                            for _ in range(CHUNKS_AT[p]):
                                reduce(B + 1, c)
                                c += 1
                            if p == NPAIR - 3:
                                maxima(B + 1)
                        if p > 0:
                            add(p - 1)
                        if p == 3 and i > 0:
                            output(B - 1, i - 1)
                    add(NPAIR - 1)
                output(j * BODY + BODY - 1, BODY - 1)

            walk(dve, body)


def context_attention_phase(nc, A, K, S, l):
    with ExitStack() as x:
        s = Scope(nc, x, f"cattn{l}")
        Q = s.sb("Q", [QK, NH, P])
        Kt = s.sb("Kt", [QK, NH, P])
        V = s.sb("V", [P, NH, HD])
        mx = s.sb("mx", [P, NH])
        sums = s.sb("sums", [P, NH])
        Pr = s.sb("Pr", [P, NH, P])
        PT = s.sb("PT", [P, NH, P])
        O = s.sb("O", [P, NH, HD])
        pS, pT = s.ps("pS", [P, NH * P]), s.ps("pT", [P, NH * P])
        pO = s.ps("pO", [P, NH * HD])
        loaded, s_done, mx_ready, e_ready, t_done, t_ready, pv_done, r_ready, o_ready, stored = (
            s.sem(n) for n in ("loaded", "s_done", "mx_ready", "e_ready", "t_done", "t_ready", "pv_done", "r_ready",
                               "o_ready", "stored"))
        block = s.block()

        @block.sync
        def _(sp):
            sp.dma_start(Q[:, :, :], S.QT[:, :, CTX * P:].rearrange("h r t -> r h t")).then_inc(loaded, 16)
            sp.dma_start(Kt[:, :, :], S.KT[:, :, (CTX + 1) * P:].rearrange("h r t -> r h t")).then_inc(loaded, 16)
            sp.dma_start(V[:, :, :], S.V[:, :, CTX + 1, :].rearrange("h p d -> p h d")).then_inc(loaded, 16)
            sp.wait_ge(o_ready, 1 + START)
            sp.dma_start(S.O[CTX * P:, 0:NH * HD], O[:, :, :].rearrange("p h d -> p (h d)")).then_inc(stored, 16)
            sp.wait_ge(stored, 16 + START)

        @block.tensor
        def _(pe):
            pe.wait_ge(loaded, 48 + START)
            for h in range(NH):
                mm = pe.matmul(pS[:, h * P:(h + 1) * P], Q[:, h, :], Kt[:, h, :], start=True, stop=True)
            mm.then_inc(s_done, 1)
            pe.wait_ge(e_ready, NH + START)
            for h in range(NH):
                mm = pe.transpose(pT[:, h * P:(h + 1) * P], Pr[:, h, :], K.ident[:, :])
            mm.then_inc(t_done, 1)
            pe.wait_ge(t_ready, 1 + START)
            for h in range(NH):
                mm = pe.matmul(pO[:, h * HD:(h + 1) * HD], PT[:, h, :], V[:, h, :], start=True, stop=True)
            mm.then_inc(pv_done, 1)

        @block.scalar
        def _(act):
            act.wait_ge(mx_ready, 1 + START)
            for h in range(NH):
                act.activation(Pr[:, h, :], pS[:, h * P:(h + 1) * P], ACT.Exp, bias=mx[:, h:h + 1],
                               accum_out=sums[:, h:h + 1]).then_inc(e_ready, 1)
            act.wait_ge(t_done, 1 + START)
            act.activation(PT[:, :, :], pT[:, :], ACT.Copy).then_inc(t_ready, 1)

        @block.vector
        def _(dve):
            dve.wait_ge(s_done, 1 + START)
            dve.tensor_reduce(mx[:, :], pS[:, :].rearrange("p (h k) -> p h k", k=P), AX.X, ALU.max, negate=True).then_inc(mx_ready, 1)
            dve.wait_ge(e_ready, NH + START)
            dve.reciprocal(sums[:, :], sums[:, :]).then_inc(r_ready, 1)
            dve.wait_ge(r_ready, 1 + START)
            dve.wait_ge(pv_done, 1 + START)
            dve.tensor_tensor(O[:, :, :], pO[:, :].rearrange("p (h d) -> p h d", d=HD),
                              sums[:, :].unsqueeze(2).broadcast_to([P, NH, HD]), ALU.mult).then_inc(o_ready, 1)


def output_phase(nc, A, K, S, l, xin, xout):
    with ExitStack() as x:
        s = Scope(nc, x, f"out{l}")
        w = s.sb("w", [P, DC, D])
        O = [s.sb(f"O{i}", [P, D]) for i in range(2)]
        G = [s.sb(f"G{i}", [P, D]) for i in range(2)]
        X = [s.sb(f"X{i}", [P, D]) for i in range(2)]
        og = [s.sb(f"og{i}", [P, D]) for i in range(2)]
        oT = [s.sb(f"oT{i}", [P, DC, P]) for i in range(2)]
        t = s.sb("t", [P, D])
        Y = [s.sb(f"Y{i}", [P, D]) for i in range(2)]
        pT = [s.ps(f"pT{i}", [P, D]) for i in range(2)]
        pY = [s.ps(f"pY{i}", [P, D]) for i in range(2)]
        w_loaded = s.sem("w_loaded")
        loaded = [s.sem(f"loaded{i}") for i in range(2)]
        x_loaded = [s.sem(f"x_loaded{i}") for i in range(2)]
        stored = [s.sem(f"stored{i}") for i in range(2)]
        og_ready, t_done, ot_ready, y_done, y_ready, dch, tch = (
            s.sem(n) for n in ("og_ready", "t_done", "ot_ready", "y_done", "y_ready", "dve_steps", "scaled"))
        block = s.block()

        def walk(eng, body):
            with eng.Fori(0, NLAT // 2) as j:
                for u in range(2):
                    body(j * 2 + u, u, j, False)
            body(CTX, 0, NLAT // 2, True)

        @block.sync
        def _(sp):
            def load(n, par):
                rows = bass.ds(n * P, P)
                sp.dma_start(O[par][:, :], S.O[rows, :]).then_inc(loaded[par], 16)
                sp.dma_start(G[par][:, :], S.G[rows, :]).then_inc(loaded[par], 16)
                sp.dma_start(X[par][:, :], xin[rows, :]).then_inc(x_loaded[par], 16)

            load(0, 0)
            for c in range(DC):
                sp.dma_start(w[:, c, :], A["w_out"][l, c * P:(c + 1) * P, :]).then_inc(w_loaded, 16)

            def body(n, par, j, last):
                if not last:
                    sp.wait_ge(y_ready, n + START)
                    load(n + 1, 1 - par)
                sp.wait_ge(y_ready, n + 1 + START)
                sp.dma_start(xout[bass.ds(n * P, P), :], Y[par][:, :]).then_inc(stored[par], 16)

            walk(sp, body)
            sp.wait_ge(stored[0], 16 * (NT + 1) // 2 + START)
            sp.wait_ge(stored[1], 16 * NLAT // 2 + START)

        @block.tensor
        def _(pe):
            pe.wait_ge(w_loaded, 16 * DC + START)

            def body(n, par, j, last):
                pe.wait_ge(og_ready, n + 1 + START)
                if par == 1 or not isinstance(j, int):
                    pe.wait_ge(ot_ready, n + START)
                for c in range(DC):
                    mm = pe.transpose(pT[par][:, c * P:(c + 1) * P], og[par][:, c * P:(c + 1) * P], K.ident[:, :])
                mm.then_inc(t_done, 1)
                pe.wait_ge(ot_ready, n + 1 + START)
                pe.wait_ge(y_ready, n + START)
                for half in range(2):
                    cols = slice(half * 512, (half + 1) * 512)
                    for c in range(DC):
                        mm = pe.matmul(pY[par][:, cols], oT[par][:, c, :], w[:, c, cols], start=(c == 0), stop=(c == DC - 1))
                mm.then_inc(y_done, 1)

            walk(pe, body)

        @block.scalar
        def _(act):
            def body(n, par, j, last):
                act.wait_ge(t_done, n + 1 + START)
                act.wait_ge(y_done, n + START)
                act.activation(oT[par][:, :, :], pT[par][:, :], ACT.Copy).then_inc(ot_ready, 1)

            walk(act, body)

        @block.vector
        def _(dve):
            step = Chain(dve, dch, 3)

            def gates(n, par, cnt):
                dve.wait_ge(loaded[par], cnt * 32 + 32 + START)
                g, o, out = G[par], O[par], og[par]
                step.tile(n)
                step(dve.tensor_copy(out[:, 256:512], o[:, 512:768]))
                step(dve.scalar_tensor_tensor(out[:, 0:256], g[:, 0:256], 0.5, o[:, 0:256], ALU.mult, ALU.mult))
                step(dve.scalar_tensor_tensor(out[:, 512:768], g[:, 512:768], 0.5, o[:, 768:D], ALU.mult, ALU.mult))
                emit(dve.scalar_tensor_tensor(out[:, 768:D], g[:, 768:D], 0.5, o[:, 256:512], ALU.mult, ALU.mult),
                     og_ready, dve, n + 1)

            gates(0, 0, 0)

            def body(n, par, j, last):
                if not last:
                    gates(n + 1, 1 - par, j + par)
                dve.wait_ge(y_done, n + 1 + START)
                emit(dve.tensor_tensor(t[:, :], pY[par][:, :], K.gate[:, 1 if last else 0, :], ALU.mult), tch, dve, n + 1)
                dve.wait_ge(x_loaded[par], j * 16 + 16 + START)
                dve.wait_ge(stored[par], j * 16 + START)
                emit(dve.tensor_tensor(Y[par][:, :], X[par][:, :], t[:, :], ALU.add), y_ready, dve, n + 1)

            walk(dve, body)


INPUTS = {
    "x": (NT * P, D), "cache_mla_ckv": (1, DEPTH, P, KVR), "cache_mla_krope": (1, DEPTH, P, ROPE),
    "cache_gqa_k": (1, DEPTH, P, 2, HD), "cache_gqa_v": (1, DEPTH, P, 2, HD),
    "state_ssd": (1, DEPTH, 2, 4, HD, HD), "c": (1, D), "c_ctx": (D,), "w_mod": (DEPTH, D, 3 * D),
    "b_mod": (DEPTH, 3 * D), "norm_g": (DEPTH, D), "w_in": (DEPTH, D, IN_W), "w_out": (DEPTH, D, D),
    "mla_q_norm_g": (DEPTH, QR), "mla_w_uq": (DEPTH, QR, 4 * QK), "mla_kv_norm_g": (DEPTH, KVR),
    "mla_w_ukv": (DEPTH, KVR, 4 * P), "mla_q_head_g": (DEPTH, QK), "mla_k_head_g": (DEPTH, QK),
    "ssd_conv_w": (DEPTH, 3, 512), "ssd_conv_b": (DEPTH, 512), "ssd_dt_bias": (DEPTH, 2, 4),
    "ssd_a_log": (DEPTH, 2, 4), "ssd_d": (DEPTH, 4), "ssd_norm_g": (DEPTH, 256),
    "cf_conv_w": (DEPTH, KW, 256), "cf_conv_b": (DEPTH, 256), "cf_ln_g": (DEPTH, 256),
    "cf_ln_b": (DEPTH, 256), "gqa_q_g": (DEPTH, HD), "gqa_k_g": (DEPTH, HD), "rope": (NT * P, RT),
}
OUTPUTS = {
    "y": (NT * P, D), "new_mla_ckv": (1, DEPTH, P, KVR), "new_mla_krope": (1, DEPTH, P, ROPE),
    "new_gqa_k": (1, DEPTH, P, 2, HD), "new_gqa_v": (1, DEPTH, P, 2, HD),
    "new_state_ssd": (1, DEPTH, 2, 4, HD, HD),
}


class Scratch:

    def __init__(self, nc, kind):
        def dram(name, *shape):
            return nc.dram_tensor(f"scratch_{name}", shape, F32, kind=kind).ap()

        self.MODR = dram("MODR", NT * P, 2 * DC)
        self.MOD = self.MODR.rearrange("(n p) c -> n p c", p=P)
        self.QT = dram("QT", NH, QK, NT * P)
        self.KT = dram("KT", NH, QK, NSLOT * P)
        self.V = dram("V", NH, P, NSLOT, HD)
        self.G = dram("G", NT * P, D)
        self.DT = dram("DT", NT * P, 8)
        self.XBC = dram("XBC", 4, P, NT * P)
        self.GLU = dram("GLU", 2, P, NT * P)
        self.XC = dram("XC", 4, P, NT * P)
        self.YC = dram("YC", 2, P, NT * P)
        self.SB = dram("SB", NT, P, 256)
        self.O = dram("O", NT * P, D)
        self.X1 = dram("X1", NT * P, D)


class Persistent:

    def __init__(self, nc, x):
        def sb(name, shape):
            return x.enter_context(nc.sbuf_tensor(name, shape, F32))

        self.ident = sb("ident", [P, P])
        self.ident2 = sb("ident2", [P, HD])
        self.ones = sb("ones", [P, P])
        self.tri = sb("tri", [P, 4, P])
        self.gate = sb("gate", [P, 2, D])


def build(nc, A, phases="cmpkvsao", kind="Internal", layers=DEPTH):
    S = Scratch(nc, kind)
    with ExitStack() as x:
        K = Persistent(nc, x)
        constants_phase(nc, K, S)
        for l in range(layers):
            xin = A["x"] if l == 0 else S.X1
            xout = A["y"] if l == DEPTH - 1 else S.X1
            modulation_phase(nc, A, K, S, l)
            if "p" in phases:
                projection_phase(nc, A, K, S, l, xin)
            if "k" in phases:
                cache_phase(nc, A, K, S, l)
            if "v" in phases:
                convolution_phase(nc, A, K, S, l)
            if "s" in phases:
                scan_phase(nc, A, K, S, l)
            if "a" in phases:
                attention_phase(nc, A, K, S, l)
                context_attention_phase(nc, A, K, S, l)
            if "o" in phases:
                output_phase(nc, A, K, S, l, xin, xout)


def kernel(**inputs):
    import concourse.bacc as bacc
    from concourse.bass_utils import run_bass_kernel_spmd

    arrays = {n: np.asarray(inputs[n]) for n in INPUTS if n not in ("x", "rope")}
    arrays["x"] = np.concatenate([np.asarray(inputs["x_sample"])[0], np.asarray(inputs["x_prompt"])[0]], 0)
    arrays["rope"] = rope_table()
    nc = bacc.Bacc("TRN2", target_bir_lowering=False, num_devices=1)
    A, feeds = {}, {}
    for n, shape in INPUTS.items():
        A[n] = nc.dram_tensor(f"in_{n}", shape, F32, kind="ExternalInput").ap()
        feeds[f"in_{n}"] = np.ascontiguousarray(arrays[n])
    for n, shape in OUTPUTS.items():
        A[n] = nc.dram_tensor(f"out_{n}", shape, F32, kind="ExternalOutput").ap()
    build(nc, A)
    r = run_bass_kernel_spmd(nc, [feeds], core_ids=[0]).results[0]
    y = r["out_y"]
    return (y[LAT:][None], y[:LAT][None]) + tuple(r[f"out_{n}"] for n in OUTPUTS if n != "y")
```

```python
from contextlib import ExitStack

import numpy as np
import concourse.bass as bass
from concourse import mybir

F32 = mybir.dt.float32
F32R = mybir.dt.float32r
I32 = mybir.dt.int32
ALU = mybir.AluOpType
ACT = mybir.ActivationFunctionType
AX = mybir.AxisListType

P = 128
D = 1024
DC = D // P
DEPTH = 2
LAT = 2048
NLAT = LAT // P
NT = NLAT + 1
CTX = NT - 1
NSLOT = NT + 1
EPS = 1e-6
GRID_W = 64
THETA = 10000.0
A_Q, A_KV, A_R, A_G = 0, 192, 320, 352
B_XBC, B_DT, B_Z = 608, 1120, 1128
C_V, C_GL, C_G = 1384, 1640, 1896
D_Q, D_K, D_V, D_G = 2152, 2408, 2536, 2664
IN_W = 2920
QR, KVR, ROPE, NOPE, QK, HD = 192, 128, 32, 64, 96, 64
NH = 8
KW = 31


def rope_table():
    def tab(dim):
        quarter = dim // 4
        inv = np.float32(THETA) ** (-np.arange(quarter, dtype=np.float32) / np.float32(quarter))
        row = np.repeat(np.arange(LAT // GRID_W), GRID_W).astype(np.float32)
        col = np.tile(np.arange(GRID_W), LAT // GRID_W).astype(np.float32)
        ar, ac = row[:, None] * inv, col[:, None] * inv
        ang = np.concatenate([ar, ar, ac, ac], -1).astype(np.float64)
        sign = np.repeat(np.array([-1.0, 1.0, -1.0, 1.0]), quarter)
        return np.cos(ang), np.sin(ang) * sign
    c1, s1 = tab(ROPE)
    c2, s2 = tab(HD)
    lat = np.concatenate([c1, s1, c2, s2], 1)
    ctx = np.concatenate([np.ones((P, ROPE)), np.zeros((P, ROPE)), np.ones((P, HD)), np.zeros((P, HD))], 1)
    return np.concatenate([lat, ctx], 0).astype(np.float32)


RT = 2 * ROPE + 2 * HD
START = 1


class Chain:

    def __init__(self, eng, sem, per=0, n=0):
        self.eng, self.sem, self.base, self.per, self.k = eng, sem, n * per if per else 0, per, 0

    def __call__(self, ins):
        self.k += 1
        ins.then_inc(self.sem, 1)
        self.eng.wait_ge(self.sem, self.base + self.k + START)

    def go(self, ins):
        self.k += 1
        ins.then_inc(self.sem, 1)

    def tile(self, n):
        assert self.k in (0, self.per), (self.sem, self.k)
        self.base, self.k = n * self.per, 0

    def end(self):
        assert self.k in (0, self.per), (self.sem, self.k)


class Lagged(Chain):

    def __call__(self, ins):
        self.k += 1
        ins.then_inc(self.sem, 1)
        if self.k > 1:
            self.eng.wait_ge(self.sem, self.base + self.k - 1 + START)

    def settle(self):
        self.eng.wait_ge(self.sem, self.base + self.k + START)


def emit(ins, sem, eng, value):
    ins.then_inc(sem, 1)
    eng.wait_ge(sem, value + START)


def rsqrt_steps(dve, step, y, v, t):
    step(dve.tensor_scalar(y.bitcast(I32), v.bitcast(I32), -0.5, 1597463007.0, ALU.mult, ALU.add))
    for _ in range(3):
        step(dve.scalar_tensor_tensor(t, y, -0.5, y, ALU.mult, ALU.mult))
        step(dve.tensor_tensor(t, t, v, ALU.mult))
        step(dve.scalar_tensor_tensor(y, t, 1.5, y, ALU.add, ALU.mult))


RSQRT = 10


class Scope:

    def __init__(self, nc, x, tag):
        self.nc, self.x, self.tag, self.sems = nc, x, tag, []

    def sb(self, name, shape, dt=F32):
        return self.x.enter_context(self.nc.sbuf_tensor(f"{self.tag}_{name}", shape, dt))

    def ps(self, name, shape):
        return self.x.enter_context(self.nc.psum_tensor(f"{self.tag}_{name}", shape, F32))

    def sem(self, name):
        self.sems.append(self.x.enter_context(self.nc.semaphore(f"{self.tag}_{name}")))
        return self.sems[-1]

    def block(self):
        for sem in self.sems:
            self.nc.gpsimd.sem_clear(sem)
            self.nc.gpsimd.sem_inc(sem, START)
        self.nc.all_engine_barrier()
        return self.x.enter_context(self.nc.Block())


def constants_phase(nc, K, S):
    with ExitStack() as x:
        s = Scope(nc, x, "const")
        made, stored = s.sem("made"), s.sem("stored")
        zeros = s.sb("zeros", [32, 2304])
        block = s.block()

        @block.gpsimd
        def _(pool):
            step = Chain(pool, made)
            step(pool.memset(K.ident[:, :], 0.0))
            step(pool.affine_select(out=K.ident[:, :], in_=K.ident[:, :], compare_op=ALU.not_equal, fill=1.0,
                                    base=0, pattern=[[-1, P]], channel_multiplier=1))
            step(pool.memset(K.ident2[:, :], 0.0))
            for base in (0, -HD):
                step(pool.affine_select(out=K.ident2[:, :], in_=K.ident2[:, :], compare_op=ALU.not_equal,
                                        fill=1.0, base=base, pattern=[[-1, HD]], channel_multiplier=1))
            step(pool.memset(K.ones[:, :], 1.0))
            for m, (cm, pat, base) in enumerate([(1, -1, -1), (-1, 1, -1), (-1, 1, 0), (1, -1, 0)]):
                step(pool.affine_select(out=K.tri[:, m, :], in_=K.ones[:, :], compare_op=ALU.is_ge, fill=0.0,
                                        base=base, pattern=[[pat, P]], channel_multiplier=cm))
            step(pool.memset(zeros[:, :], 0.0))

        @block.sync
        def _(sp):
            sp.wait_ge(made, 11 + START)
            for h in range(4, NH):
                sp.dma_start(S.QT[h, HD:QK, :], zeros[:, 0:NT * P]).then_inc(stored, 16)
                sp.dma_start(S.KT[h, HD:QK, :], zeros[:, 0:NSLOT * P]).then_inc(stored, 16)
            sp.wait_ge(stored, 16 * 8 + START)


def modulation_phase(nc, A, K, S, l):
    with ExitStack() as x:
        s = Scope(nc, x, f"mod{l}")
        w = s.sb("w", [P, DC, 3 * D])
        cc = s.sb("cc", [P, 2, DC])
        th = s.sb("th", [P, 2, DC])
        sc = s.sb("sc", [P, 2, DC])
        scb = s.sb("scb", [P, 2, DC, P])
        bm = s.sb("bm", [P, 2 * DC])
        ng = s.sb("ng", [P, DC])
        gb = s.sb("gb", [P, D])
        out = s.sb("out", [P, 2, 2 * DC])
        pm = s.ps("pm", [P, 2 * DC, 2])
        pg = [s.ps(f"pg{i}", [P, 512]) for i in range(4)]
        small, wl, tanhed, silued, mods, gates, dch, kept, stored = (
            s.sem(n) for n in ("small", "wl", "tanhed", "silued", "mods", "gates", "dch", "kept", "stored"))
        block = s.block()

        @block.sync
        def _(sp):
            with nc.allow_non_contiguous_dma(reason="small vectors, channels on partitions"):
                sp.dma_start(cc[:, 0, :], A["c"][0].rearrange("(c p) -> p c", p=P)).then_inc(small, 16)
                sp.dma_start(cc[:, 1, :], A["c_ctx"].rearrange("(c p) -> p c", p=P)).then_inc(small, 16)
                sp.dma_start(bm[:, :], A["b_mod"][l, 0:2 * D].rearrange("(c p) -> p c", p=P)).then_inc(small, 16)
                sp.dma_start(ng[:, :], A["norm_g"][l].rearrange("(c p) -> p c", p=P)).then_inc(small, 16)
                sp.dma_start(gb[:, :], A["b_mod"][l, 2 * D:3 * D].partition_broadcast(P)).then_inc(small, 16)
                for c in range(DC):
                    sp.dma_start(w[:, c, :], A["w_mod"][l, c * P:(c + 1) * P, :]).then_inc(wl, 16)
                sp.wait_ge(kept, 1 + START)
                for n in range(NT):
                    sp.dma_start(S.MOD[n], out[:, 1 if n == CTX else 0, :]).then_inc(stored, 16)
                sp.wait_ge(stored, 16 * NT + START)

        @block.scalar
        def _(act):
            act.wait_ge(small, 80 + START)
            act.activation(th[:, :, :], cc[:, :, :], ACT.Tanh, scale=0.5).then_inc(tanhed, 1)

        @block.vector
        def _(dve):
            step = Chain(dve, dch)
            dve.wait_ge(tanhed, 1 + START)
            step(dve.scalar_tensor_tensor(sc[:, :, :], th[:, :, :], 1.0, cc[:, :, :], ALU.add, ALU.mult))
            step(dve.tensor_scalar(sc[:, :, :], sc[:, :, :], 0.5, None, ALU.mult))
            for k in range(2):
                ins = dve.tensor_copy(scb[:, k, :, :], sc[:, k, :].unsqueeze(2).broadcast_to([P, DC, P]))
                emit(ins, silued, dve, k + 1)
            dve.wait_ge(mods, 1 + START)
            for k in range(2):
                step(dve.tensor_tensor(out[:, k, DC:2 * DC], pm[:, 0:DC, k], bm[:, 0:DC], ALU.add))
                step(dve.tensor_tensor(out[:, k, 0:DC], pm[:, DC:2 * DC, k], bm[:, DC:2 * DC], ALU.add))
                step(dve.scalar_tensor_tensor(out[:, k, 0:DC], out[:, k, 0:DC], 1.0, ng[:, :], ALU.add, ALU.mult))
            dve.wait_ge(gates, 1 + START)
            for k in range(2):
                for j in range(2):
                    cols = slice(512 * j, 512 * (j + 1))
                    step(dve.tensor_tensor(K.gate[:, k, cols], pg[2 * k + j][:, :], gb[:, cols], ALU.add))
            dve.nop().then_inc(kept, 1)

        @block.tensor
        def _(pe):
            pe.wait_ge(silued, 2 + START)
            pe.wait_ge(wl, 16 * DC + START)
            for m in range(2 * DC):
                for c in range(DC):
                    mm = pe.matmul(pm[:, m, :], w[:, c, m * P:(m + 1) * P], sc[:, :, c],
                                   start=(c == 0), stop=(c == DC - 1))
            mm.then_inc(mods, 1)
            for k in range(2):
                for j in range(2):
                    for c in range(DC):
                        mm = pe.matmul(pg[2 * k + j][:, :], scb[:, k, c, :],
                                       w[:, c, 2 * D + 512 * j:2 * D + 512 * (j + 1)],
                                       start=(c == 0), stop=(c == DC - 1))
            mm.then_inc(gates, 1)


def halves(ap, b):
    q = ap.shape[-1] // 4
    return ap.rearrange("p h (a b q) -> p h a b q", a=2, b=2, q=q)[:, :, :, b, :]


def rope_steps(pool, step, t1, t2, src, cos, sin):
    h = src.shape[1]

    def over_heads(tab):
        return tab.unsqueeze(1).broadcast_to([P, h, tab.shape[-1]])

    step(pool.tensor_tensor(t1, src, over_heads(cos), ALU.mult))
    q = src.shape[-1] // 4
    for b in range(2):
        sb = sin.rearrange("p (a b q) -> p a b q", a=2, b=2, q=q)[:, :, b, :]
        step(pool.tensor_tensor(halves(t2, b), halves(src, 1 - b), sb.unsqueeze(1).broadcast_to([P, h, 2, q]),
                                ALU.mult))


def projection_phase(nc, A, K, S, l, xin):
    hx, hg = 1, KW // 2
    with ExitStack() as x:
        s = Scope(nc, x, f"proj{l}")
        w = s.sb("w", [P, DC, IN_W])
        wuq = s.sb("wuq", [QK, 2, 4 * QK])
        wukv = s.sb("wukv", [P, 4 * P])
        gq = s.sb("gq", [P, QR])
        gkv = s.sb("gkv", [P, KVR])
        qkg = s.sb("qkg", [P, 8, QK])
        gg = s.sb("gg", [P, 6, HD])
        xt = [s.sb(f"xt{i}", [P, D]) for i in range(2)]
        md = [s.sb(f"md{i}", [P, 2 * DC]) for i in range(2)]
        rp = s.sb("rp", [P, RT])
        xn = s.sb("xn", [P, D])
        hT = [s.sb(f"hT{i}", [P, DC, P]) for i in range(2)]
        junk = s.sb("junk", [P, D])
        pss, pv, pr, ptmp = (s.sb(n, [P, 1]) for n in ("pss", "pv", "pr", "ptmp"))
        E0 = s.sb("E0", [P, 360])
        ss0, v0, r0, tmp0 = (s.sb(n, [P, 2]) for n in ("ss0", "v0", "r0", "tmp0"))
        krss = s.sb("krss", [P, 1])
        ql = s.sb("ql", [P, QR])
        ck = s.sb("ck", [P, KVR])
        LT = s.sb("LT", [P, 3, P])
        qsq = s.sb("qsq", [P, 4, QK])
        KV = s.sb("KV", [P, 4, P])
        ksq = s.sb("ksq", [P, 4, NOPE])
        ssh, vh, rh, tmph = (s.sb(n, [P, 8]) for n in ("ssh", "vh", "rh", "tmph"))
        QKt = s.sb("QKt", [P, 8, QK])
        E3 = s.sb("E3", [P, 8, HD])
        gsq = s.sb("gsq", [P, 6, HD])
        ssg, vg, rg, tmpg = (s.sb(n, [P, 6]) for n in ("ssg", "vg", "rg", "tmpg"))
        GN = s.sb("GN", [P, 6, HD])
        GR = s.sb("GR", [P, 6, HD])
        t1 = s.sb("t1", [P, 6, HD])
        t2 = s.sb("t2", [P, 6, HD])
        m1 = s.sb("m1", [P, 8, ROPE])
        m2 = s.sb("m2", [P, 8, ROPE])
        TH = [s.sb(f"TH{i}", [P, 512]) for i in range(2)]
        TG = s.sb("TG", [P, 256])
        GT = s.sb("GT", [P, D])
        XW = [s.sb(f"XW{i}", [P, 4, 2 * hx + P]) for i in range(2)]
        GW = [s.sb(f"GW{i}", [P, 2, 2 * hg + P]) for i in range(2)]
        TX = s.sb("TX", [P, 4, 4 * hx + P])
        TW = s.sb("TW", [P, 2, 4 * hg + P])
        XY = s.sb("XY", [P, 4, P + 2 * hx])
        XH = s.sb("XH", [P, 4, P + 2 * hx])
        XZ = s.sb("XZ", [P, 4, P + 2 * hx])
        GY = [s.sb(f"GY{i}", [P, 2, P + 2 * hg]) for i in range(2)]
        cw = s.sb("cw", [P, 4, 3])
        cb = s.sb("cb", [P, 4])
        fw = s.sb("fw", [P, 2, KW])
        fb = s.sb("fb", [P, 2])
        QST = s.sb("QST", [QK, 4, P])
        KST = s.sb("KST", [QK, 4, P])
        GST = s.sb("GST", [P, 3, P])
        b = [s.ps(f"b{i}", [P, 512]) for i in range(8)]
        names = ("w_loaded small x_loaded md_loaded rp_loaded gains ss_ready r_ready xn_ready xT_done ht_act ht_dve "
                 "t0_done t1_done t2_done t3_done s1_done s2_done s3_done s5_done f0_done f1_done e0_ready e3_ready "
                 "th1_ready th2_ready th3_ready qlck_ready lt_ready sq_ready qk_ready qkr_ready gn_ready gr_ready "
                 "gate1_ready gates_ready fb_ready fg_ready qst_ready kst_ready gst_ready "
                 "st_dt st_v3 st_v st_q st_k st_g st_gd st_xc st_yc st_out act_steps act_pre dve_steps dve_pre "
                 "taps padded hist_ready xy_ready xh_ready xc_ready conv_ready conv_steps act_hist "
                 "pool_steps").split()
        q = {n: s.sem(n) for n in names}
        block = s.block()

        @block.sync
        def _(sp):
            def walk(tile):
                tile(0, 0, False, False)
                with sp.Fori(0, NLAT // 2 - 1) as j:
                    for u in range(2):
                        tile(j * 2 + (u + 1), 1 - u, False)
                tile(NLAT - 1, 1, False)
                tile(CTX, 0, True)

            with nc.allow_non_contiguous_dma(reason="broadcast gains"):
                sp.dma_start(wuq[:, :, :], A["mla_w_uq"][l].rearrange("(a p) n -> p a n", a=2)).then_inc(q["small"], 16)
                sp.dma_start(wukv[:, :], A["mla_w_ukv"][l]).then_inc(q["small"], 16)
                sp.dma_start(gq[:, :], A["mla_q_norm_g"][l].partition_broadcast(P)).then_inc(q["small"], 16)
                sp.dma_start(gkv[:, :], A["mla_kv_norm_g"][l].partition_broadcast(P)).then_inc(q["small"], 16)
                for h in range(8):
                    g = A["mla_q_head_g" if h < 4 else "mla_k_head_g"]
                    sp.dma_start(qkg[:, h, :], g[l].partition_broadcast(P)).then_inc(q["small"], 16)
                for h in range(6):
                    g = A["gqa_q_g" if h < 4 else "gqa_k_g"]
                    sp.dma_start(gg[:, h, :], g[l].partition_broadcast(P)).then_inc(q["small"], 16)

            def load_x(m, par):
                if not (isinstance(m, int) and m == 0):
                    sp.wait_ge(q["xn_ready"], m + START)
                    sp.wait_ge(q["ht_act"], m + START)
                    sp.wait_ge(q["ht_dve"], m + START)
                sp.dma_start(xt[par][:, :], xin[bass.ds(m * P, P), :]).then_inc(q["x_loaded"], 16)
                sp.dma_start(md[par][:, :], S.MODR[bass.ds(m * P, P), :]).then_inc(q["md_loaded"], 16)

            load_x(0, 0)
            sp.dma_start(rp[:, :], A["rope"][0:P, :]).then_inc(q["rp_loaded"], 16)
            for c in range(DC):
                sp.dma_start(w[:, c, :], A["w_in"][l, c * P:(c + 1) * P, :]).then_inc(q["w_loaded"], 16)
            with nc.allow_non_contiguous_dma(reason="taps, channels on partitions"):
                for f in range(4):
                    sp.dma_start(cw[:, f, :], A["ssd_conv_w"][l][:, f * P:(f + 1) * P].rearrange("k p -> p k")).then_inc(q["taps"], 16)
                sp.dma_start(cb[:, :], A["ssd_conv_b"][l].rearrange("(f p) -> p f", p=P)).then_inc(q["taps"], 16)
                for f in range(2):
                    sp.dma_start(fw[:, f, :], A["cf_conv_w"][l][:, f * P:(f + 1) * P].rearrange("k p -> p k")).then_inc(q["taps"], 16)
                sp.dma_start(fb[:, :], A["cf_conv_b"][l].rearrange("(f p) -> p f", p=P)).then_inc(q["taps"], 16)

            def store_conv(m, at, width, par):
                sp.wait_ge(q["xc_ready"], m + 1 + START)
                sp.dma_start(S.XC[:, :, bass.ds(at, P + 2 * hx * width)].rearrange("f p t -> p f t"),
                             XZ[:, :, 0:P + 2 * hx * width]).then_inc(q["st_xc"], 16)
                sp.wait_ge(q["conv_ready"], m + 1 + START)
                sp.dma_start(S.YC[:, :, bass.ds(at, P + 2 * hg * width)].rearrange("f p t -> p f t"),
                             GY[par][:, :, 0:P + 2 * hg * width]).then_inc(q["st_yc"], 16)

            def tile(n, par, last, conv=True):
                if not last:
                    load_x(n + 1, 1 - par)
                sp.wait_ge(q["e0_ready"], n + 1 + START)
                sp.dma_start(S.DT[bass.ds(n * P, P), :], E0[:, 352:360]).then_inc(q["st_dt"], 16)
                if last:
                    sp.dma_start(A["new_mla_krope"][0, l], E0[:, A_R:A_R + ROPE]).then_inc(q["st_out"], 16)
                    sp.wait_ge(q["qlck_ready"], n + 1 + START)
                    sp.dma_start(A["new_mla_ckv"][0, l], ck[:, :]).then_inc(q["st_out"], 16)
                sp.wait_ge(q["e3_ready"], n + 1 + START)
                for r in range(2):
                    sp.dma_start(S.V[4 + r:NH:2, :, bass.ds(n + 1, 1), :].rearrange("h p s d -> p h (s d)"),
                                 E3[:, 6:8, :]).then_inc(q["st_v3"], 16)
                if last:
                    sp.dma_start(A["new_gqa_v"][0, l], E3[:, 6:8, :]).then_inc(q["st_out"], 16)
                    sp.wait_ge(q["gn_ready"], n + 1 + START)
                    sp.dma_start(A["new_gqa_k"][0, l], GN[:, 4:6, :]).then_inc(q["st_out"], 16)
                sp.wait_ge(q["gates_ready"], n + 1 + START)
                sp.dma_start(S.G[bass.ds(n * P, P), :], GT[:, :]).then_inc(q["st_gd"], 16)
                if not last:
                    sp.wait_ge(q["qkr_ready"], n + 1 + START)
                    sp.dma_start(rp[:, :], A["rope"][bass.ds((n + 1) * P, P), :]).then_inc(q["rp_loaded"], 16)
                if conv:
                    store_conv(n - 1, n * P - P, 0, 1 - par)

            walk(tile)
            store_conv(CTX, CTX * P, 1, 0)
            for n, per in (("st_dt", 16), ("st_v3", 32), ("st_v", 16), ("st_q", 16), ("st_k", 16), ("st_g", 96),
                           ("st_gd", 16), ("st_xc", 16), ("st_yc", 16)):
                sp.wait_ge(q[n], per * NT + START)
            sp.wait_ge(q["st_out"], 64 + START)

        @block.scalar
        def _(act):
            step = Chain(act, q["act_steps"], 7)

            def pre(m, par):
                act.wait_ge(q["x_loaded"], (m + 1) * 16 + START)
                emit(act.activation(junk[:, :], xt[par][:, :], ACT.Square, accum_out=pss[:, :]), q["ss_ready"], act, m + 1)
                act.wait_ge(q["r_ready"], m + 1 + START)
                act.wait_ge(q["xT_done"], m + START)
                emit(act.activation(xn[:, :], xt[par][:, :], ACT.Copy, scale=pr[:, :]), q["xn_ready"], act, m + 1)

            def evac_hT(m, par):
                act.wait_ge(q["xT_done"], m + 1 + START)
                act.wait_ge(q["md_loaded"], (m + 1) * 16 + START)
                pst = Chain(act, q["act_pre"], 3, m)
                for c in range(4):
                    ins = act.activation(hT[par][:, c, :], b[0][:, c * P:(c + 1) * P], ACT.Identity,
                                         scale=md[par][:, c:c + 1], bias=md[par][:, DC + c:DC + c + 1])
                    if c < 3:
                        pst(ins)
                    else:
                        emit(ins, q["ht_act"], act, m + 1)

            def tile(n, par, last, conv=True):
                step.tile(n)
                act.wait_ge(q["t0_done"], n + 1 + START)
                act.wait_ge(q["st_dt"], n * 16 + START)
                step(act.activation(E0[:, :], b[2][:, 0:360], ACT.Copy))
                step(act.activation(junk[:, 0:QR], E0[:, 0:QR], ACT.Square, accum_out=ss0[:, 0:1]))
                step(act.activation(junk[:, 0:KVR], E0[:, A_KV:A_R], ACT.Square, accum_out=ss0[:, 1:2]))
                emit(act.activation(junk[:, 0:ROPE], E0[:, A_R:A_G], ACT.Square, accum_out=krss[:, :]),
                     q["e0_ready"], act, n + 1)
                if not last:
                    pre(n + 1, 1 - par)
                act.wait_ge(q["t3_done"], n + 1 + START)
                act.wait_ge(q["st_v3"], n * 32 + START)
                step(act.activation(E3[:, :, :], b[5][:, :], ACT.Copy))
                emit(act.activation(gsq[:, :, :], E3[:, 0:6, :], ACT.Square), q["e3_ready"], act, n + 1)
                act.wait_ge(q["t1_done"], n + 1 + START)
                emit(act.activation(TH[0][:, :], b[3][:, :], ACT.Tanh, scale=0.5), q["th1_ready"], act, n + 1)
                act.wait_ge(q["s1_done"], n + 1 + START)
                step(act.activation(LT[0:QK, 0:2, :], b[7][0:QK, 0:2 * P], ACT.Copy))
                emit(act.activation(LT[:, 2, :], b[7][:, 2 * P:3 * P], ACT.Copy), q["lt_ready"], act, n + 1)
                act.wait_ge(q["t2_done"], n + 1 + START)
                emit(act.activation(TH[1][:, :], b[4][:, :], ACT.Tanh, scale=0.5), q["th2_ready"], act, n + 1)
                act.wait_ge(q["s2_done"], n + 1 + START)
                step(act.activation(qsq[:, :, :], b[2][:, 0:4 * QK], ACT.Square))
                act.wait_ge(q["st_v"], n * 16 + START)
                step(act.activation(KV[:, :, :], b[7][:, :], ACT.Copy))
                emit(act.activation(ksq[:, :, :], KV[:, :, 0:NOPE], ACT.Square), q["sq_ready"], act, n + 1)
                act.dma_start(S.V[0:4, :, bass.ds(n + 1, 1), :].rearrange("h p s d -> p h (s d)"),
                             KV[:, :, NOPE:P]).then_inc(q["st_v"], 16)
                act.wait_ge(q["f0_done"], n + 1 + START)
                if conv:
                    act.wait_ge(q["conv_ready"], n - 1 + START)
                if last:
                    act.wait_ge(q["padded"], 4 + START)
                to = TX[:, :, 3 * hx:3 * hx + P] if last else XW[par][:, :, 2 * hx:]
                emit(act.activation(to, b[6][:, :].rearrange("p (f t) -> p f t", f=4), ACT.Copy), q["fb_ready"], act, n + 1)
                if conv:
                    act.wait_ge(q["fg_ready"], n + START)
                    to, tog = (TX, TW) if last else (XW[par], GW[par])
                    emit(act.activation(to[:, :, 0:2 * hx], XW[1 - par][:, :, P:], ACT.Copy), q["act_hist"], act, n)
                    emit(act.activation(tog[:, :, 0:2 * hg], GW[1 - par][:, :, P:], ACT.Copy), q["hist_ready"], act, n)
                    silu_tanh(n - 1, 0)
                act.wait_ge(q["s3_done"], n + 1 + START)
                act.wait_ge(q["st_q"], n * 16 + START)
                emit(act.activation(QST[:, :, :], b[2][0:QK, :], ACT.Copy), q["qst_ready"], act, n + 1)
                act.dma_start(S.QT[0:4, :, bass.ds(n * P, P)].rearrange("h r t -> r h t"), QST[:, :, :]).then_inc(q["st_q"], 16)
                act.wait_ge(q["st_k"], n * 16 + START)
                emit(act.activation(KST[:, :, :], b[7][0:QK, :], ACT.Copy), q["kst_ready"], act, n + 1)
                act.dma_start(S.KT[0:4, :, bass.ds((n + 1) * P, P)].rearrange("h r t -> r h t"), KST[:, :, :]).then_inc(q["st_k"], 16)
                if not last:
                    evac_hT(n + 1, 1 - par)
                act.wait_ge(q["f1_done"], n + 1 + START)
                emit(act.activation(TG[:, :], b[6][:, 256:512], ACT.Tanh, scale=0.5), q["th3_ready"], act, n + 1)
                act.wait_ge(q["s5_done"], n + 1 + START)
                act.wait_ge(q["st_g"], n * 96 + START)
                emit(act.activation(GST[:, :, :], b[5][:, 0:3 * P], ACT.Copy), q["gst_ready"], act, n + 1)
                for o in range(2):
                    rows = slice(o * HD, (o + 1) * HD)
                    act.dma_start(S.QT[4 + o:NH:2, 0:HD, bass.ds(n * P, P)].rearrange("h r t -> r h t"),
                                 GST[rows, 0:2, :]).then_inc(q["st_g"], 16)
                    for h in (4 + 2 * o, 5 + 2 * o):
                        act.dma_start(S.KT[h, 0:HD, bass.ds((n + 1) * P, P)], GST[rows, 2, :]).then_inc(q["st_g"], 16)
                step.end()

            def silu_tanh(m, width):
                act.wait_ge(q["xy_ready"], m + 1 + START)
                w_ = P + 2 * hx * width
                act.activation(XH[:, :, 0:w_], XY[:, :, 0:w_], ACT.Tanh).then_inc(q["xh_ready"], 1)

            act.wait_ge(q["small"], 16 * 18 + START)
            act.wait_ge(q["x_loaded"], 16 + START)
            emit(act.activation(junk[:, :], xt[0][:, :], ACT.Square, accum_out=pss[:, :]), q["ss_ready"], act, 1)
            act.wait_ge(q["r_ready"], 1 + START)
            emit(act.activation(xn[:, :], xt[0][:, :], ACT.Copy, scale=pr[:, :]), q["xn_ready"], act, 1)
            evac_hT(0, 0)
            tile(0, 0, False, False)
            with act.Fori(0, NLAT // 2 - 1) as j:
                for u in range(2):
                    tile(j * 2 + (u + 1), 1 - u, False)
            tile(NLAT - 1, 1, False)
            tile(CTX, 0, True)
            silu_tanh(CTX, 1)

        @block.vector
        def _(dve):
            setup = Chain(dve, q["gains"])
            dve.wait_ge(q["small"], 16 * 18 + START)
            setup(dve.tensor_scalar(qkg[:, 0:4, :], qkg[:, 0:4, :], float(QK) ** -0.5, None, ALU.mult))
            setup(dve.tensor_scalar(gg[:, 0:4, :], gg[:, 0:4, :], float(HD) ** -0.5, None, ALU.mult))
            step = Chain(dve, q["dve_steps"], 3 + RSQRT + 3 + RSQRT + 7 + RSQRT)
            conv = Lagged(dve, q["conv_steps"], 3 * 4 + 2 * KW - 2)

            def halved_taps():
                dve.wait_ge(q["taps"], 16 * 8 + START)
                for t in (cw, fw):
                    setup(dve.tensor_scalar(t[:, :, :], t[:, :, :], 0.5, None, ALU.mult))
                setup(dve.tensor_scalar(cb[:, :], cb[:, :], 0.5, None, ALU.mult))

            def conv_x(m, par, width=0):
                X, w_ = TX if width else XW[par], P + 2 * hx * width
                conv.tile(m)
                dve.wait_ge(q["hist_ready"], m + START)
                dve.wait_ge(q["fb_ready"], m + 1 + START)
                for f in range(4):
                    conv(dve.tensor_scalar(XY[:, f, 0:w_], X[:, f, 1:1 + w_], cw[:, f, 1:2], cb[:, f:f + 1], ALU.mult, ALU.add))
                for k in (0, 2):
                    for f in range(4):
                        final = k == 2 and f == 3
                        if final:
                            conv.settle()
                        ins = dve.scalar_tensor_tensor(XY[:, f, 0:w_], X[:, f, k:k + w_], cw[:, f, k:k + 1], XY[:, f, 0:w_],
                                                       ALU.mult, ALU.add)
                        if final:
                            emit(ins, q["xy_ready"], dve, m + 1)
                        else:
                            conv(ins)

            def conv_silu(m, width=0):
                w_ = P + 2 * hx * width
                dve.wait_ge(q["xh_ready"], m + 1 + START)
                dve.wait_ge(q["st_xc"], m * 16 + START)
                emit(dve.scalar_tensor_tensor(XZ[:, :, 0:w_], XH[:, :, 0:w_], 1.0, XY[:, :, 0:w_], ALU.add, ALU.mult),
                     q["xc_ready"], dve, m + 1)

            def conv_g(m, par, taps, width=0):
                X, w_ = TW if width else GW[par], P + 2 * hg * width
                for k in taps:
                    for f in range(2):
                        y = GY[par][:, f, 0:w_]
                        if k == 0:
                            conv(dve.tensor_scalar(y, X[:, f, 0:w_], fw[:, f, 0:1], fb[:, f:f + 1], ALU.mult, ALU.add))
                            continue
                        final = k == KW - 1 and f == 1
                        if final:
                            conv.settle()
                        ins = dve.scalar_tensor_tensor(y, X[:, f, k:k + w_], fw[:, f, k:k + 1], y, ALU.mult, ALU.add)
                        if final:
                            emit(ins, q["conv_ready"], dve, m + 1)
                        else:
                            conv(ins)

            def pre(m, par):
                pst = Chain(dve, q["dve_pre"], RSQRT + 3, m)
                dve.wait_ge(q["ss_ready"], m + 1 + START)
                pst(dve.tensor_scalar(pv[:, :], pss[:, :], 1.0 / D, EPS, ALU.mult, ALU.add))
                rsqrt_steps(dve, lambda i: pst(i) if pst.k < RSQRT else emit(i, q["r_ready"], dve, m + 1),
                            pr[:, :], pv[:, :], ptmp[:, :])
                assert pst.k == RSQRT

            def evac_hT(m, par):
                pst = Chain(dve, q["dve_pre"], RSQRT + 3, m)
                pst.k = RSQRT
                dve.wait_ge(q["xT_done"], m + 1 + START)
                dve.wait_ge(q["md_loaded"], (m + 1) * 16 + START)
                for c in range(4, 8):
                    ins = dve.tensor_scalar(hT[par][:, c, :], b[1][:, (c - 4) * P:(c - 3) * P],
                                            md[par][:, c:c + 1], md[par][:, DC + c:DC + c + 1], ALU.mult, ALU.add)
                    if c < 7:
                        pst(ins)
                    else:
                        emit(ins, q["ht_dve"], dve, m + 1)
                pst.end()

            def tile(n, par, last, with_conv=True):
                step.tile(n)

                def g_taps(a, e):
                    if with_conv:
                        conv_g(n - 1, 1 - par, range(a, e))

                dve.wait_ge(q["e0_ready"], n + 1 + START)
                step(dve.tensor_scalar(v0[:, 0:1], ss0[:, 0:1], 1.0 / QR, EPS, ALU.mult, ALU.add))
                step(dve.tensor_scalar(v0[:, 1:2], ss0[:, 1:2], 1.0 / KVR, EPS, ALU.mult, ALU.add))
                rsqrt_steps(dve, step, r0[:, :], v0[:, :], tmp0[:, :])
                step(dve.scalar_tensor_tensor(ql[:, :], E0[:, 0:QR], r0[:, 0:1], gq[:, :], ALU.mult, ALU.mult))
                emit(dve.scalar_tensor_tensor(ck[:, :], E0[:, A_KV:A_R], r0[:, 1:2], gkv[:, :], ALU.mult, ALU.mult),
                     q["qlck_ready"], dve, n + 1)
                if not last:
                    pre(n + 1, 1 - par)
                if with_conv:
                    conv_x(n - 1, 1 - par)
                dve.wait_ge(q["e3_ready"], n + 1 + START)
                step(dve.tensor_reduce(ssg[:, :], gsq[:, :, :], AX.X, ALU.add))
                step(dve.tensor_scalar(vg[:, :], ssg[:, :], 1.0 / HD, EPS, ALU.mult, ALU.add))
                rsqrt_steps(dve, step, rg[:, :], vg[:, :], tmpg[:, :])
                step(dve.tensor_tensor(GN[:, :, :], E3[:, 0:6, :], rg[:, :].unsqueeze(2).broadcast_to([P, 6, HD]), ALU.mult))
                emit(dve.tensor_tensor(GN[:, :, :], GN[:, :, :], gg[:, :, :], ALU.mult), q["gn_ready"], dve, n + 1)
                g_taps(0, 6)
                dve.wait_ge(q["th1_ready"], n + 1 + START)
                dve.wait_ge(q["st_gd"], n * 16 + START)
                emit(dve.scalar_tensor_tensor(GT[:, 0:512], TH[0][:, :], 1.0, b[3][:, :], ALU.add, ALU.mult),
                     q["gate1_ready"], dve, n + 1)
                g_taps(6, 12)
                dve.wait_ge(q["th2_ready"], n + 1 + START)
                emit(dve.scalar_tensor_tensor(GT[:, 512:D], TH[1][:, :], 1.0, b[4][:, :], ALU.add, ALU.mult),
                     q["gates_ready"], dve, n + 1)
                g_taps(12, 18)
                dve.wait_ge(q["sq_ready"], n + 1 + START)
                step(dve.tensor_reduce(ssh[:, 0:4], qsq[:, :, :], AX.X, ALU.add))
                step(dve.tensor_reduce(ssh[:, 4:8], ksq[:, :, :], AX.X, ALU.add))
                step(dve.tensor_scalar(ssh[:, 4:8], ssh[:, 4:8], krss[:, 0:1], None, ALU.add))
                step(dve.tensor_scalar(vh[:, :], ssh[:, :], 1.0 / QK, EPS, ALU.mult, ALU.add))
                rsqrt_steps(dve, step, rh[:, :], vh[:, :], tmph[:, :])

                def rows(a, b_, w_):
                    return rh[:, a:b_].unsqueeze(2).broadcast_to([P, b_ - a, w_])

                step(dve.tensor_tensor(QKt[:, 0:4, :], b[2][:, 0:4 * QK].rearrange("p (h d) -> p h d", h=4),
                                       rows(0, 4, QK), ALU.mult))
                step(dve.tensor_tensor(QKt[:, 4:8, 0:NOPE], KV[:, :, 0:NOPE], rows(4, 8, NOPE), ALU.mult))
                step(dve.tensor_tensor(QKt[:, 4:8, NOPE:QK], E0[:, A_R:A_G].unsqueeze(1).broadcast_to([P, 4, ROPE]),
                                       rows(4, 8, ROPE), ALU.mult))
                emit(dve.tensor_tensor(QKt[:, :, :], QKt[:, :, :], qkg[:, :, :], ALU.mult), q["qk_ready"], dve, n + 1)
                g_taps(18, 22)
                if not last:
                    evac_hT(n + 1, 1 - par)
                if with_conv:
                    conv_silu(n - 1)
                g_taps(22, KW)
                dve.wait_ge(q["th3_ready"], n + 1 + START)
                to = TW[:, :, 3 * hg:3 * hg + P] if last else GW[par][:, :, 2 * hg:]
                emit(dve.scalar_tensor_tensor(to, TG[:, :].rearrange("p (f t) -> p f t", f=2), 1.0,
                                              b[6][:, 0:256].rearrange("p (f t) -> p f t", f=2), ALU.add, ALU.mult),
                     q["fg_ready"], dve, n + 1)
                step.end()

            pre(0, 0)
            evac_hT(0, 0)
            tile(0, 0, False, False)
            halved_taps()
            dve.wait_ge(q["padded"], 4 + START)
            with dve.Fori(0, NLAT // 2 - 1) as j:
                for u in range(2):
                    tile(j * 2 + (u + 1), 1 - u, False)
            tile(NLAT - 1, 1, False)
            tile(CTX, 0, True)
            conv_x(CTX, 0, 1)
            conv_silu(CTX, 1)
            conv_g(CTX, 0, range(KW), 1)

        @block.gpsimd
        def _(pool):
            step = Chain(pool, q["pool_steps"], 6)

            def tile(n, par, last):
                step.tile(n)
                pool.wait_ge(q["rp_loaded"], (n + 1) * 16 + START)
                pool.wait_ge(q["gn_ready"], n + 1 + START)
                rope_steps(pool, step, t1[:, :, :], t2[:, :, :], GN[:, :, :], rp[:, 64:128], rp[:, 128:192])
                emit(pool.tensor_tensor(GR[:, :, :], t1[:, :, :], t2[:, :, :], ALU.add), q["gr_ready"], pool, n + 1)
                pool.wait_ge(q["qk_ready"], n + 1 + START)
                rope_steps(pool, step, m1[:, :, :], m2[:, :, :], QKt[:, :, NOPE:QK], rp[:, 0:32], rp[:, 32:64])
                emit(pool.tensor_tensor(QKt[:, :, NOPE:QK], m1[:, :, :], m2[:, :, :], ALU.add), q["qkr_ready"], pool, n + 1)
                step.end()

            pad = Chain(pool, q["padded"])
            for i, t in enumerate((XW[0][:, :, 0:2 * hx], GW[0][:, :, 0:2 * hg], TX[:, :, :], TW[:, :, :])):
                pad(pool.memset(t, 0.0))
            with pool.Fori(0, NLAT // 2) as j:
                for u in range(2):
                    tile(j * 2 + u, u, False)
            tile(CTX, 0, True)

        @block.tensor
        def _(pe):
            def xT(m):
                pe.wait_ge(q["xn_ready"], m + 1 + START)
                pe.wait_ge(q["ht_act"], m + START)
                pe.wait_ge(q["ht_dve"], m + START)
                for c in range(DC):
                    mm = pe.transpose(b[c // 4][:, (c % 4) * P:(c % 4 + 1) * P], xn[:, c * P:(c + 1) * P], K.ident[:, :])
                mm.then_inc(q["xT_done"], 1)

            def tokens(par, bank, parts):
                at = 0
                for a, e in parts:
                    for c in range(DC):
                        mm = pe.matmul(b[bank][:, at:at + e - a], hT[par][:, c, :], w[:, c, a:e],
                                       start=(c == 0), stop=(c == DC - 1))
                    at += e - a
                return mm

            def channels(par, bank, cols):
                for f, a in enumerate(cols):
                    for c in range(DC):
                        mm = pe.matmul(b[bank][:, f * P:(f + 1) * P], w[:, c, a:a + P], hT[par][:, c, :],
                                       start=(c == 0), stop=(c == DC - 1))
                return mm

            def tile(n, par, last):
                pe.wait_ge(q["ht_act"], n + 1 + START)
                pe.wait_ge(q["ht_dve"], n + 1 + START)
                pe.wait_ge(q["qst_ready"], n + START)
                tokens(par, 2, [(A_Q, A_G), (B_DT, B_Z)]).then_inc(q["t0_done"], 1)
                pe.wait_ge(q["gst_ready"], n + START)
                tokens(par, 5, [(D_Q, D_G)]).then_inc(q["t3_done"], 1)
                pe.wait_ge(q["gate1_ready"], n + START)
                tokens(par, 3, [(A_G, B_XBC), (B_Z, C_V)]).then_inc(q["t1_done"], 1)
                pe.wait_ge(q["kst_ready"], n + START)
                pe.wait_ge(q["qlck_ready"], n + 1 + START)
                for a in range(2):
                    pe.transpose(b[7][0:QK, a * P:(a + 1) * P], ql[:, a * QK:(a + 1) * QK], K.ident[:, :])
                pe.transpose(b[7][:, 2 * P:3 * P], ck[:, :], K.ident[:, :]).then_inc(q["s1_done"], 1)
                pe.wait_ge(q["gates_ready"], n + START)
                tokens(par, 4, [(C_G, D_Q), (D_G, IN_W)]).then_inc(q["t2_done"], 1)
                pe.wait_ge(q["lt_ready"], n + 1 + START)
                for a in range(2):
                    pe.matmul(b[2][:, 0:4 * QK], LT[0:QK, a, :], wuq[:, a, :], start=(a == 0), stop=(a == 1))
                pe.matmul(b[7][:, :], LT[:, 2, :], wukv[:, :], start=True, stop=True).then_inc(q["s2_done"], 1)
                pe.wait_ge(q["fg_ready"], n + START)
                channels(par, 6, [B_XBC + P * f for f in range(4)]).then_inc(q["f0_done"], 1)
                pe.wait_ge(q["qkr_ready"], n + 1 + START)
                for h in range(8):
                    mm = pe.transpose(b[2 if h < 4 else 7][0:QK, (h % 4) * P:(h % 4 + 1) * P], QKt[:, h, :], K.ident[:, :])
                mm.then_inc(q["s3_done"], 1)
                if not last:
                    xT(n + 1)
                pe.wait_ge(q["fb_ready"], n + 1 + START)
                channels(par, 6, [C_V, C_V + P, C_GL, C_GL + P]).then_inc(q["f1_done"], 1)
                pe.wait_ge(q["gr_ready"], n + 1 + START)
                for pair in range(3):
                    mm = pe.transpose(b[5][:, pair * P:(pair + 1) * P],
                                      GR[:, 2 * pair:2 * pair + 2, :].rearrange("p h d -> p (h d)"), K.ident[:, :])
                mm.then_inc(q["s5_done"], 1)

            pe.wait_ge(q["xn_ready"], 1 + START)
            xT(0)
            pe.wait_ge(q["small"], 16 * 18 + START)
            pe.wait_ge(q["w_loaded"], 16 * DC + START)
            with pe.Fori(0, NLAT // 2) as j:
                for u in range(2):
                    tile(j * 2 + u, u, False)
            tile(CTX, 0, True)


def cache_phase(nc, A, K, S, l):
    with ExitStack() as x:
        s = Scope(nc, x, f"cache{l}")
        wukv = s.sb("wukv", [P, 4 * P])
        kg = s.sb("kg", [P, QK])
        ck = s.sb("ck", [P, KVR])
        kr = s.sb("kr", [P, ROPE])
        gk = s.sb("gk", [P, 2, HD])
        gv = s.sb("gv", [P, 2, HD])
        ckT = s.sb("ckT", [P, P])
        KV = s.sb("KV", [P, 4, P])
        sq = s.sb("sq", [P, 4, NOPE])
        sqr = s.sb("sqr", [P, ROPE])
        krss = s.sb("krss", [P, 1])
        ss, v, r, tmp = (s.sb(n, [P, 4]) for n in ("ss", "v", "r", "tmp"))
        KN = s.sb("KN", [P, 4, QK])
        KST = s.sb("KST", [QK, 4, P])
        GST = s.sb("GST", [HD, 2, P])
        pt, pkv, pk, pgk = (s.ps(n, [P, 512]) for n in ("pt", "pkv", "pk", "pgk"))
        loaded, turned, copied, kv_done, sq_ready, kn_ready, kt_done, st_ready, stored, ach, dch = (
            s.sem(n) for n in ("loaded", "turned", "copied", "kv_done", "sq_ready", "kn_ready", "kt_done",
                               "st_ready", "stored", "act_steps", "dve_steps"))
        block = s.block()

        @block.sync
        def _(sp):
            with nc.allow_non_contiguous_dma(reason="broadcast gain"):
                sp.dma_start(ck[:, :], A["cache_mla_ckv"][0, l]).then_inc(loaded, 16)
                sp.dma_start(kr[:, :], A["cache_mla_krope"][0, l]).then_inc(loaded, 16)
                sp.dma_start(gk[:, :, :], A["cache_gqa_k"][0, l]).then_inc(loaded, 16)
                sp.dma_start(gv[:, :, :], A["cache_gqa_v"][0, l]).then_inc(loaded, 16)
                sp.dma_start(wukv[:, :], A["mla_w_ukv"][l]).then_inc(loaded, 16)
                sp.dma_start(kg[:, :], A["mla_k_head_g"][l].partition_broadcast(P)).then_inc(loaded, 16)
            sp.wait_ge(loaded, 96 + START)
            for rep in range(2):
                sp.dma_start(S.V[4 + rep:NH:2, :, 0, :].rearrange("h p d -> p h d"), gv[:, :, :]).then_inc(stored, 16)
            sp.wait_ge(sq_ready, 1 + START)
            sp.dma_start(S.V[0:4, :, 0, :].rearrange("h p d -> p h d"), KV[:, :, NOPE:P]).then_inc(stored, 16)
            sp.wait_ge(st_ready, 1 + START)
            sp.dma_start(S.KT[0:4, :, 0:P].rearrange("h r t -> r h t"), KST[:, :, :]).then_inc(stored, 16)
            for rep in range(2):
                sp.dma_start(S.KT[4 + rep:NH:2, 0:HD, 0:P].rearrange("h r t -> r h t"), GST[:, :, :]).then_inc(stored, 16)
            sp.wait_ge(stored, 96 + START)

        @block.tensor
        def _(pe):
            pe.wait_ge(loaded, 96 + START)
            pe.transpose(pt[:, 0:P], ck[:, :], K.ident[:, :]).then_inc(turned, 1)
            pe.wait_ge(copied, 1 + START)
            pe.matmul(pkv[:, :], ckT[:, :], wukv[:, :], start=True, stop=True).then_inc(kv_done, 1)
            for h in range(2):
                pe.transpose(pgk[0:HD, h * P:(h + 1) * P], gk[:, h, :], K.ident[:, :])
            pe.wait_ge(kn_ready, 1 + START)
            for h in range(4):
                mm = pe.transpose(pk[0:QK, h * P:(h + 1) * P], KN[:, h, :], K.ident[:, :])
            mm.then_inc(kt_done, 1)

        @block.scalar
        def _(act):
            step = Chain(act, ach)
            act.wait_ge(loaded, 96 + START)
            act.wait_ge(turned, 1 + START)
            emit(act.activation(ckT[:, :], pt[:, 0:P], ACT.Copy), copied, act, 1)
            act.wait_ge(kv_done, 1 + START)
            step(act.activation(KV[:, :, :], pkv[:, :], ACT.Copy))
            step(act.activation(sqr[:, :], kr[:, :], ACT.Square, accum_out=krss[:, :]))
            emit(act.activation(sq[:, :, :], KV[:, :, 0:NOPE], ACT.Square), sq_ready, act, 1)
            act.wait_ge(kt_done, 1 + START)
            step(act.activation(KST[:, :, :], pk[0:QK, :], ACT.Copy))
            emit(act.activation(GST[:, :, :], pgk[0:HD, 0:2 * P], ACT.Copy), st_ready, act, 1)

        @block.vector
        def _(dve):
            step = Chain(dve, dch)
            dve.wait_ge(sq_ready, 1 + START)
            step(dve.tensor_reduce(ss[:, :], sq[:, :, :], AX.X, ALU.add))
            step(dve.tensor_scalar(ss[:, :], ss[:, :], krss[:, 0:1], None, ALU.add))
            step(dve.tensor_scalar(v[:, :], ss[:, :], 1.0 / QK, EPS, ALU.mult, ALU.add))
            rsqrt_steps(dve, step, r[:, :], v[:, :], tmp[:, :])
            step(dve.tensor_tensor(KN[:, :, 0:NOPE], KV[:, :, 0:NOPE], r[:, :].unsqueeze(2).broadcast_to([P, 4, NOPE]), ALU.mult))
            step(dve.tensor_tensor(KN[:, :, NOPE:QK], kr[:, :].unsqueeze(1).broadcast_to([P, 4, ROPE]),
                                   r[:, :].unsqueeze(2).broadcast_to([P, 4, ROPE]), ALU.mult))
            emit(dve.tensor_tensor(KN[:, :, :], KN[:, :, :], kg[:, :].unsqueeze(1).broadcast_to([P, 4, QK]), ALU.mult),
                 kn_ready, dve, 1)


def scan_phase(nc, A, K, S, l):
    W4 = 4 * HD
    AFTER, BEFORE, UPTO, FROM = range(4)
    with ExitStack() as xs_:
        s = Scope(nc, xs_, f"scan{l}")
        dt = s.sb("dt", [P, NT, 8])
        dA = s.sb("dA", [P, NT, 8])
        Sb = [s.sb(f"Sb{i}", [P, W4]) for i in range(2)]
        Sp = [s.sb(f"Sp{i}", [P, 2 * W4]) for i in range(2)]
        Sc = s.sb("Sc", [P, W4])
        init = s.sb("init", [P, 2, W4])
        _scan_prepare(nc, A, K, S, l, dt, dA, Sb, Sp, init)
        _scan_backward(nc, A, K, S, l, dt, dA, Sb, Sc, init)
        _scan_forward(nc, A, K, S, l, dt, dA, Sp, Sc, init)


def _scan_prepare(nc, A, K, S, l, dt, dA, Sb, Sp, init):
    with ExitStack() as x:
        s = Scope(nc, x, f"prep{l}")
        n8 = [P, NT, 8]
        bias = s.sb("bias", [P, 8])
        al = s.sb("al", [P, 8])
        t, u, d, e, g = (s.sb(n, n8) for n in ("t", "u", "d", "e", "g"))
        si = s.sb("si", [P, 2, 2, P])
        pt = s.ps("pt", [P, 512])
        loaded, zeroed, s_loaded, t_ready, u_ready, ln_ready, turned, dch = (
            s.sem(n) for n in ("loaded", "zeroed", "s_loaded", "t_ready", "u_ready", "ln_ready", "turned", "dve_steps"))
        block = s.block()

        @block.sync
        def _(sp):
            with nc.allow_non_contiguous_dma(reason="narrow rows"):
                sp.dma_start(dt[:, :, :], S.DT.rearrange("(n p) c -> p n c", p=P)).then_inc(loaded, 16)
                sp.dma_start(bias[:, :], A["ssd_dt_bias"][l].rearrange("d h -> (d h)").partition_broadcast(P)).then_inc(loaded, 16)
                sp.dma_start(al[:, :], A["ssd_a_log"][l].rearrange("d h -> (d h)").partition_broadcast(P)).then_inc(loaded, 16)
                sp.wait_ge(zeroed, 1 + START)
                for dr in range(2):
                    for grp in range(2):
                        sp.dma_start(si[:, dr, grp, grp * HD:(grp + 1) * HD],
                                     A["state_ssd"][0, l, dr, 2 * grp:2 * grp + 2].rearrange("h p n -> (h p) n")).then_inc(s_loaded, 16)

        @block.gpsimd
        def _(pool):
            for i in range(2):
                pool.memset(Sb[i][:, :], 0.0)
                pool.memset(Sp[i][:, :], 0.0)
            pool.memset(si[:, :, :, :], 0.0).then_inc(zeroed, 1)

        @block.tensor
        def _(pe):
            pe.wait_ge(s_loaded, 64 + START)
            for i in range(4):
                mm = pe.transpose(pt[:, i * P:(i + 1) * P], si[:, i // 2, i % 2, :], K.ident[:, :])
            mm.then_inc(turned, 1)

        @block.scalar
        def _(act):
            act.wait_ge(t_ready, 1 + START)
            act.activation(t[:, :, :], t[:, :, :], ACT.Exp)
            act.activation(al[:, :], al[:, :], ACT.Exp).then_inc(u_ready, 1)
            act.wait_ge(t_ready, 2 + START)
            act.activation(g[:, :, :], u[:, :, :], ACT.Ln).then_inc(ln_ready, 1)

        @block.vector
        def _(dve):
            step = Chain(dve, dch)
            dve.wait_ge(loaded, 48 + START)
            step(dve.tensor_tensor(dt[:, :, :], dt[:, :, :], bias[:, :].unsqueeze(1).broadcast_to(n8), ALU.add))
            emit(dve.scalar_tensor_tensor(t[:, :, :], dt[:, :, :], -1.0, dt[:, :, :], ALU.mult, ALU.min), t_ready, dve, 1)
            dve.wait_ge(u_ready, 1 + START)
            emit(dve.tensor_scalar(u[:, :, :], t[:, :, :], 1.0, None, ALU.add), t_ready, dve, 2)
            step(dve.tensor_scalar(d[:, :, :], u[:, :, :], -1.0, None, ALU.add))
            step(dve.tensor_scalar(e[:, :, :], d[:, :, :], 0.0, None, ALU.is_equal))
            step(dve.tensor_tensor(d[:, :, :], d[:, :, :], e[:, :, :], ALU.add))
            step(dve.reciprocal(d[:, :, :], d[:, :, :]))
            dve.wait_ge(ln_ready, 1 + START)
            step(dve.tensor_tensor(g[:, :, :], g[:, :, :], e[:, :, :], ALU.add))
            step(dve.tensor_tensor(g[:, :, :], g[:, :, :], t[:, :, :], ALU.mult))
            step(dve.tensor_tensor(g[:, :, :], g[:, :, :], d[:, :, :], ALU.mult))
            step(dve.scalar_tensor_tensor(dt[:, :, :], dt[:, :, :], 0.0, g[:, :, :], ALU.max, ALU.add))
            step(dve.scalar_tensor_tensor(dA[:, :, :], dt[:, :, :], -1.0, al[:, :].unsqueeze(1).broadcast_to(n8),
                                          ALU.mult, ALU.mult))
            dve.wait_ge(turned, 1 + START)
            step(dve.tensor_copy(init[:, :, :], pt[:, :]))


def is_ctx(n):
    return isinstance(n, int) and n == CTX


def conv_at(n, half):
    return LAT + 2 * half if is_ctx(n) else n * P + half


def state_update(dve, step, last, new, old, decay, made):
    def v(ap, g):
        return ap[g * HD:(g + 1) * HD, 2 * g * HD:(2 * g + 2) * HD].rearrange("p (h d) -> p h d", h=2)

    for g, order in ((0, step.go), (1, step)):
        dec = decay[g * HD:(g + 1) * HD, 2 * g:2 * g + 2].unsqueeze(2).broadcast_to([HD, 2, HD])
        order(dve.tensor_tensor(v(new, g), v(old, g), dec, ALU.mult))
    step(dve.tensor_tensor(v(new, 0), v(new, 0), v(made, 0), ALU.add))
    last(dve.tensor_tensor(v(new, 1), v(new, 1), v(made, 1), ALU.add))


def _scan_backward(nc, A, K, S, l, dt, dA, Sb, Sc, init):
    W4 = 4 * HD
    AFTER, BEFORE, UPTO, FROM = range(4)
    with ExitStack() as x:
        s = Scope(nc, x, f"back{l}")
        X = [s.sb(f"X{i}", [P, 3, P]) for i in range(2)]
        XT = [s.sb(f"XT{i}", [P, 3 * P]) for i in range(2)]
        ex = [s.sb(f"ex{i}", [P, 8]) for i in range(2)]
        wt = s.sb("wt", [P, 4])
        xw = [s.sb(f"xw{i}", [P, 4, HD]) for i in range(2)]
        pt = [s.ps(f"pt{i}", [P, 512]) for i in range(2)]
        ps = [s.ps(f"ps{i}", [P, 512]) for i in range(2)]
        x_loaded = [s.sem(f"x_loaded{i}") for i in range(2)]
        stored = [s.sem(f"stored{i}") for i in range(2)]
        turned, xt_ready, xw_ready, st_done, s_ready, dch, uch, ach, first = (
            s.sem(n) for n in ("turned", "xt_ready", "xw_ready", "st_done", "s_ready", "dve_steps", "update_steps",
                               "act_steps", "first"))
        block = s.block()

        def walk(eng, body):
            body(0, 0, 1, CTX, NLAT - 1, 1)
            with eng.Fori(0, NLAT // 2 - 1) as j:
                ns = [j * -2 + (NLAT - 1 - u) for u in range(3)]
                for u in range(2):
                    body(j * 2 + (u + 1), 1 - u, j + (u + 1), ns[u], ns[u + 1], j + 2)
            body(NLAT - 1, 1, NLAT // 2, 1, 0, NLAT // 2 + 1)
            body(NLAT, 0, NLAT // 2 + 1, 0, None, 0)

        @block.sync
        def _(sp):
            def load(n, par):
                sp.dma_start(X[par][:, :, :], S.XC[0:3, :, bass.ds(conv_at(n, 1), P)].rearrange("f p t -> p f t")).then_inc(x_loaded[par], 16)

            load(CTX, 0)

            def body(k, par, cnt, n, kind):
                if kind == 0:
                    load(NLAT - 1, 1)
                else:
                    sp.wait_ge(s_ready, k + START)
                    sp.dma_start(S.SB[bass.ds(n, 1), :, :].rearrange("n p c -> p (n c)"), Sb[par][:, :]).then_inc(stored[par], 16)

            body(0, 0, 1, CTX, 0)
            with sp.Fori(0, NLAT // 2 - 1) as j:
                ns = [j * -2 + (NLAT - 1 - u) for u in range(3)]
                for u in range(2):
                    k, n = j * 2 + (u + 1), ns[u]
                    sp.wait_ge(turned, k + START)
                    load(ns[u + 1], u % 2)
                    body(k, (u + 1) % 2, 0, n, 1)
            k = NLAT - 1
            sp.wait_ge(turned, k + START)
            load(0, 0)
            body(k, 1, 0, 1, 1)
            body(k + 1, 0, 0, 0, 1)
            for i in range(2):
                sp.wait_ge(stored[i], 16 * NLAT // 2 + START)

        @block.tensor
        def _(pe):
            def turn(k, par, n, cnt, waits=True):
                pe.wait_ge(x_loaded[par], cnt * 16 + START)
                if waits:
                    pe.wait_ge(xt_ready, k - 1 + START)
                for f in range(3):
                    pe.transpose(pt[par][:, f * P:(f + 1) * P], X[par][:, f, :], K.ident[:, :])
                rhs = dA[:, bass.ds(n, 1), 4:8].rearrange("p n c -> p (n c)")
                pe.matmul(pt[par][:, 384:388], K.tri[:, BEFORE, :], rhs, start=True, stop=True)
                pe.matmul(pt[par][:, 388:392], K.ones[:, :], rhs, start=True, stop=True).then_inc(turned, 1)

            def body(k, par, cnt, n, n_next, cnt_next):
                if n_next is not None:
                    turn(k + 1, 1 - par, n_next, cnt_next, not is_ctx(n))
                pe.wait_ge(xw_ready, k + 1 + START)
                pe.matmul(ps[par][:, 0:W4], XT[par][:, 2 * P:3 * P], xw[par][:, :, :].rearrange("p h d -> p (h d)"),
                          start=True, stop=True).then_inc(st_done, 1)

            turn(0, 0, CTX, 1, False)
            walk(pe, body)

        @block.scalar
        def _(act):
            step = Chain(act, ach, 1)

            def body(k, par, cnt, n, n_next, cnt_next):
                step.tile(k)
                act.wait_ge(turned, k + 1 + START)
                if not is_ctx(n):
                    act.wait_ge(s_ready, k - 1 + START)
                step(act.activation(ex[par][:, :], pt[par][:, 384:392], ACT.Exp))
                emit(act.activation(XT[par][:, :], pt[par][:, 0:384], ACT.Copy), xt_ready, act, k + 1)

            walk(act, body)

        @block.vector
        def _(dve):
            emit(dve.tensor_copy(Sc[:, :], Sb[0][:, :]), first, dve, 1)

            def weigh(k, par, n):
                step.tile(k)
                dve.wait_ge(xt_ready, k + 1 + START)
                step(dve.tensor_tensor(wt[:, :], ex[par][:, 0:4], dt[:, bass.ds(n, 1), 4:8].rearrange("p n c -> p (n c)"), ALU.mult))
                emit(dve.tensor_tensor(xw[par][:, :, :], XT[par][:, 0:W4].rearrange("p (h d) -> p h d", h=4),
                                       wt[:, :].unsqueeze(2).broadcast_to([P, 4, HD]), ALU.mult), xw_ready, dve, k + 1)

            def body(k, par, cnt, n, n_next, cnt_next):
                if n_next is not None:
                    weigh(k + 1, 1 - par, n_next)
                update.tile(k)
                dve.wait_ge(st_done, k + 1 + START)
                if is_ctx(n):
                    state_update(dve, update, lambda ins: emit(ins, first, dve, 2), Sc, Sb[par], ex[par][:, 4:8], ps[par])
                    emit(dve.tensor_copy(Sb[1][:, :], init[:, 1, :]), s_ready, dve, 1)
                else:
                    dve.wait_ge(stored[1 - par], (cnt - 1) * 16 + START)
                    state_update(dve, update, lambda ins: emit(ins, s_ready, dve, k + 1), Sb[1 - par], Sb[par],
                                 ex[par][:, 4:8], ps[par])

            step, update = Chain(dve, dch, 1), Chain(dve, uch, 3)
            weigh(0, 0, CTX)
            walk(dve, body)


def _scan_forward(nc, A, K, S, l, dt, dA, Sp, Sc, init):
    W4 = 4 * HD
    AFTER, BEFORE, UPTO, FROM = range(4)
    with ExitStack() as x:
        s = Scope(nc, x, f"fwd{l}")
        X = [s.sb(f"X{i}", [P, 4, P]) for i in range(2)]
        Z = [s.sb(f"Z{i}", [P, 256]) for i in range(2)]
        XT = [s.sb(f"XT{i}", [P, 3 * P]) for i in range(2)]
        ex = [s.sb(f"ex{i}", [P, 16]) for i in range(2)]
        dts = [s.sb(f"dts{i}", [P, 8]) for i in range(2)]
        dAs = [s.sb(f"dAs{i}", [P, 8]) for i in range(2)]
        R = s.sb("R", [P, 2, 4, P])
        L = s.sb("L", [P, 2, 4, P])
        G = s.sb("G", [P, 2, 2, P])
        wt = s.sb("wt", [P, 4])
        xw = s.sb("xw", [P, 4, HD])
        xdt = s.sb("xdt", [P, 2, 4, HD])
        xd = s.sb("xd", [P, 4, HD])
        T = s.sb("T", [P, 8, HD])
        y = s.sb("y", [P, 256])
        OB = [s.sb(f"OB{i}", [P, 256]) for i in range(2)]
        dsk = s.sb("dsk", [P, 4])
        fin = s.sb("fin", [P, 4, HD])
        pA, pG0, pG1, pF, pR, pY, pO, pT = (s.ps(n, [P, 512]) for n in ("pA", "pG0", "pG1", "pF", "pR", "pY", "pO", "pT"))
        small = s.sem("small")
        loaded = [s.sem(f"loaded{i}") for i in range(2)]
        stored = [s.sem(f"stored{i}") for i in range(2)]
        names = ("turned dts_ready R_ready xt_ready G_done seg_done L_ready M_ready y_done off_done y_ready "
                 "xw_ready st_done s_ready fin_turned fin_ready xd_ready f_stored L_half dve_steps dts_steps act_steps").split()
        q = {n: s.sem(n) for n in names}
        block = s.block()

        def walk(eng, body):
            body(0, 0, CTX, 1, 0)
            with eng.Fori(0, NLAT // 2 - 1) as j:
                for u in range(2):
                    body(j * 2 + (u + 1), 1 - u, j * 2 + u, j + 2, j + u)
            body(NLAT - 1, 1, NLAT - 2, NLAT // 2 + 1, NLAT // 2 - 1)
            body(NLAT, 0, NLAT - 1, 0, NLAT // 2)

        def flat(ap):
            return ap.rearrange("p n c -> p (n c)")

        def h4(ap):
            return ap.rearrange("p (h d) -> p h d", d=HD)

        def per_head(ap, w=HD):
            return ap.unsqueeze(2).broadcast_to([P, ap.shape[-1], w])

        def is_last(k):
            return isinstance(k, int) and k == NLAT

        @block.sync
        def _(sp):
            with nc.allow_non_contiguous_dma(reason="broadcast"):
                sp.dma_start(dsk[:, :], A["ssd_d"][l].partition_broadcast(P)).then_inc(small, 16)

            def load(n, par, ctx=False):
                sp.dma_start(X[par][:, :, :], S.XC[:, :, bass.ds(conv_at(n, 1), P)].rearrange("f p t -> p f t")).then_inc(loaded[par], 16)
                sp.dma_start(Z[par][:, :], S.G[bass.ds(n * P, P), 256:512]).then_inc(loaded[par], 16)
                if not ctx:
                    sp.dma_start(Sp[par][:, W4:2 * W4], S.SB[bass.ds(n, 1), :, :].rearrange("n p c -> p (n c)")).then_inc(loaded[par], 16)

            def store(k, par, n):
                sp.wait_ge(q["y_ready"], k + 1 + START)
                sp.dma_start(S.O[bass.ds(n * P, P), 512:768], OB[par][:, :]).then_inc(stored[par], 16)

            load(CTX, 0, True)
            load(0, 1)
            store(0, 0, CTX)
            with sp.Fori(0, NLAT // 2 - 1) as j:
                for u in range(2):
                    sp.wait_ge(q["off_done"], j * 2 + (u + 1) + START)
                    load(j * 2 + (u + 1), u)
                    store(j * 2 + (u + 1), (u + 1) % 2, j * 2 + u)
            load(NLAT - 1, 0)
            store(NLAT - 1, 1, NLAT - 2)
            store(NLAT, 0, NLAT - 1)
            sp.wait_ge(q["fin_ready"], 1 + START)
            for dr in range(2):
                for g in range(2):
                    sp.dma_start(A["new_state_ssd"][0, l, dr, 2 * g:2 * g + 2].rearrange("h p n -> (h p) n"),
                                 fin[:, 2 * dr + g, :]).then_inc(q["f_stored"], 16)
            sp.wait_ge(stored[0], 16 * (NT + 1) // 2 + START)
            sp.wait_ge(stored[1], 16 * NLAT // 2 + START)
            sp.wait_ge(q["f_stored"], 64 + START)

        @block.tensor
        def _(pe):
            def turn(k, par, n, count):
                pe.wait_ge(loaded[par], count + START)
                for f in range(3):
                    pe.transpose(pA[:, f * P:(f + 1) * P], X[par][:, f, :], K.ident[:, :])
                f4, b4 = flat(dA[:, bass.ds(n, 1), 0:4]), flat(dA[:, bass.ds(n, 1), 4:8])
                for i, (tri, d4) in enumerate(((K.tri[:, AFTER, :], f4), (K.tri[:, UPTO, :], f4),
                                               (K.tri[:, FROM, :], b4), (K.ones[:, :], f4))):
                    mm = pe.matmul(pA[:, 384 + 4 * i:388 + 4 * i], tri, d4, start=True, stop=True)
                mm.then_inc(q["turned"], 1)

            def score(par):
                for g, bank in enumerate((pG0, pG1)):
                    rows = slice(g * HD, (g + 1) * HD)
                    mm = pe.matmul(bank[:, 0:P], X[par][rows, 2, :], X[par][rows, 3, :], start=True, stop=True)
                mm.then_inc(q["G_done"], 1)

            def carried(par):
                pe.matmul(pO[:, :], X[par][:, 3, :], Sp[par][:, :], start=True, stop=True).then_inc(q["off_done"], 1)

            def body(k, par, n, cnt_next, cnt):
                pe.wait_ge(q["R_ready"], 2 * k + 2 + START)
                pe.wait_ge(q["L_ready"], k + START)
                pe.matmul(pF[:, :], K.tri[:, AFTER, :], R[:, 0, :, :].rearrange("p h i -> p (h i)"), start=True, stop=True)
                pe.matmul(pR[:, :], K.tri[:, BEFORE, :], R[:, 1, :, :].rearrange("p h i -> p (h i)"),
                          start=True, stop=True).then_inc(q["seg_done"], 1)
                if not is_last(k):
                    pe.wait_ge(q["xt_ready"], k + 1 + START)
                    turn(k + 1, 1 - par, k, 48 * cnt_next - (16 if par == 1 else 0))
                pe.wait_ge(q["xw_ready"], k + 1 + START)
                pe.wait_ge(q["s_ready"], (0 if is_ctx(n) else k + 1) + START)
                pe.matmul(pT[:, 0:W4], XT[par][:, 2 * P:3 * P], xw[:, :, :].rearrange("p h d -> p (h d)"),
                          start=True, stop=True).then_inc(q["st_done"], 1)
                pe.wait_ge(q["M_ready"], k + 1 + START)
                for h in range(4):
                    cols = slice(h * HD, (h + 1) * HD)
                    pe.matmul(pY[:, cols], L[:, 0, h, :], xdt[:, 0, h, :], start=True, stop=False)
                    mm = pe.matmul(pY[:, cols], L[:, 1, h, :], xdt[:, 1, h, :], start=False, stop=True)
                mm.then_inc(q["y_done"], 1)
                if is_ctx(n):
                    pe.wait_ge(q["s_ready"], 1 + START)
                    for i in range(4):
                        src = Sp[1][:, :] if i < 2 else Sc[:, :]
                        mm = pe.transpose(pF[:, i * P:(i + 1) * P], src[:, (i % 2) * P:(i % 2 + 1) * P], K.ident[:, :])
                    mm.then_inc(q["fin_turned"], 1)
                    pe.wait_ge(q["fin_ready"], 1 + START)
                if not is_last(k):
                    score(1 - par)
                    pe.wait_ge(q["s_ready"], k + 2 + START)
                    carried(1 - par)

            turn(0, 0, CTX, 32)
            score(0)
            carried(0)
            walk(pe, body)

        @block.scalar
        def _(act):
            step = Chain(act, q["act_steps"], 1)

            def copy(k, par):
                act.wait_ge(q["turned"], k + 1 + START)
                step.tile(k)
                step(act.activation(ex[par][:, :], pA[:, 384:400], ACT.Exp))
                emit(act.activation(XT[par][:, :], pA[:, 0:384], ACT.Copy), q["xt_ready"], act, k + 1)

            def body(k, par, n, cnt_next, cnt):
                act.wait_ge(q["seg_done"], k + 1 + START)
                act.wait_ge(q["y_done"], k + START)
                act.activation(L[:, 0, :, :], pF[:, :], ACT.Exp).then_inc(q["L_half"], 1)
                act.wait_ge(q["L_half"], k + 1 + START)
                emit(act.activation(L[:, 1, :, :], pR[:, :], ACT.Exp), q["L_ready"], act, k + 1)
                if not is_last(k):
                    act.wait_ge(q["s_ready"], (0 if is_ctx(n) else k + 1) + START)
                    copy(k + 1, 1 - par)
                if is_ctx(n):
                    act.wait_ge(q["fin_turned"], 1 + START)
                    for i in range(4):
                        g = i % 2
                        ins = act.activation(fin[:, i, :], pF[:, i * P + g * HD:i * P + (g + 1) * HD], ACT.Copy)
                    emit(ins, q["fin_ready"], act, 1)

            copy(0, 0)
            walk(act, body)

        @block.gpsimd
        def _(pool):
            def body(k, par, n, cnt_next, cnt):
                pool.wait_ge(q["dts_ready"], k + 1 + START)
                pool.wait_ge(q["seg_done"], k + START)
                for dr, tri in ((0, UPTO), (1, FROM)):
                    emit(pool.tensor_tensor(R[:, dr, :, :], K.tri[:, tri, :].unsqueeze(1).broadcast_to([P, 4, P]),
                                            per_head(dAs[par][:, 4 * dr:4 * dr + 4], P), ALU.mult),
                         q["R_ready"], pool, 2 * k + 1 + dr)
                pool.wait_ge(q["xt_ready"], k + 1 + START)
                pool.wait_ge(q["y_ready"], k + START)
                emit(pool.tensor_tensor(xd[:, :, :], h4(XT[par][:, 0:W4]), per_head(dsk[:, :]), ALU.mult),
                     q["xd_ready"], pool, k + 1)

            pool.wait_ge(small, 16 + START)
            walk(pool, body)

        @block.vector
        def _(dve):
            step = Chain(dve, q["dve_steps"], 15)
            ahead = Chain(dve, q["dts_steps"], 1)

            def steps_of(k, par, n):
                ahead.tile(k)
                ahead(dve.tensor_copy(dts[par][:, :], flat(dt[:, bass.ds(n, 1), :])))
                emit(dve.tensor_copy(dAs[par][:, :], flat(dA[:, bass.ds(n, 1), :])), q["dts_ready"], dve, k + 1)

            def body(k, par, n, cnt_next, cnt):
                step.tile(k)
                if not is_last(k):
                    if not is_ctx(n):
                        dve.wait_ge(q["R_ready"], 2 * k + START)
                    steps_of(k + 1, 1 - par, k)
                dve.wait_ge(q["xt_ready"], k + 1 + START)
                xs, e = h4(XT[par][:, 0:W4]), ex[par]
                step.go(dve.tensor_tensor(wt[:, :], dts[par][:, 0:4], e[:, 0:4], ALU.mult))
                for dr, order in ((0, step.go), (1, step)):
                    order(dve.tensor_tensor(xdt[:, dr, :, :], xs, per_head(dts[par][:, 4 * dr:4 * dr + 4]), ALU.mult))
                emit(dve.tensor_tensor(xw[:, :, :], xs, per_head(wt[:, :]), ALU.mult), q["xw_ready"], dve, k + 1)
                dve.wait_ge(q["G_done"], k + 1 + START)
                for g, bank in enumerate((pG0, pG1)):
                    for dr, tri in ((0, UPTO), (1, FROM)):
                        (step if g and dr else step.go)(dve.tensor_tensor(G[:, dr, g, :], bank[:, 0:P], K.tri[:, tri, :], ALU.mult))
                dve.wait_ge(q["L_ready"], k + 1 + START)
                for dr in range(2):
                    Lv = L[:, dr, :, :].rearrange("p (g r) i -> p g r i", g=2)
                    ins = dve.tensor_tensor(Lv, Lv, G[:, dr, :, :].unsqueeze(2).broadcast_to([P, 2, 2, P]), ALU.mult)
                    if dr == 0:
                        step(ins)
                    else:
                        emit(ins, q["M_ready"], dve, k + 1)
                dve.wait_ge(q["off_done"], k + 1 + START)
                step(dve.tensor_tensor(T[:, :, :], h4(pO[:, :]), per_head(e[:, 4:12]), ALU.mult))
                step(dve.tensor_tensor(T[:, 0:4, :], T[:, 0:4, :], T[:, 4:8, :], ALU.add))
                dve.wait_ge(q["xd_ready"], k + 1 + START)
                step(dve.tensor_tensor(T[:, 0:4, :], T[:, 0:4, :], xd[:, :, :], ALU.add))
                dve.wait_ge(q["st_done"], k + 1 + START)
                if not is_ctx(n):
                    state_update(dve, step, lambda i: emit(i, q["s_ready"], dve, k + 2), Sp[1 - par], Sp[par], e[:, 12:16], pT)
                else:
                    state_update(dve, step, lambda i: emit(i, q["s_ready"], dve, 1), Sp[1], Sp[0], e[:, 12:16], pT)
                dve.wait_ge(q["y_done"], k + 1 + START)
                step(dve.tensor_tensor(y[:, :], pY[:, 0:256], T[:, 0:4, :].rearrange("p h d -> p (h d)"), ALU.add))
                dve.wait_ge(stored[par], cnt * 16 + START)
                emit(dve.scalar_tensor_tensor(OB[par][:, :], y[:, :], 0.5, Z[par][:, :], ALU.mult, ALU.mult), q["y_ready"], dve, k + 1)
                if is_ctx(n):
                    dve.wait_ge(q["fin_turned"], 1 + START)
                    emit(dve.tensor_copy(Sp[1][:, 0:W4], init[:, 0, :]), q["s_ready"], dve, 2)
                step.end()

            steps_of(0, 0, CTX)
            walk(dve, body)


def attention_phase(nc, A, K, S, l):
    NKT = NLAT + 1
    KEYS = NKT * P
    R1 = QK + 1
    NB = 4
    BODY = 2 * NB
    NPAIR = (NKT + 1) // 2
    CH = [436, 436, 436, 436, 432]
    CA = [0, 436, 872, 1308, 1744]
    NCH = 4 * len(CH)
    CHUNKS_AT = [3, 3, 3, 3, 2, 2, 2, 2, 0]
    POOL_PAIRS = (1, 2)
    DP = [p for p in range(NPAIR) if p not in POOL_PAIRS]
    ND, NPP = len(DP), len(POOL_PAIRS)
    with ExitStack() as x:
        s = Scope(nc, x, f"attn{l}")
        kraw = s.sb("kraw", [QK, KEYS])
        qraw = s.sb("qraw", [QK, LAT])
        Kh = [s.sb(f"Kh{i}", [R1, KEYS], F32R) for i in range(2)]
        Kl = [s.sb(f"Kl{i}", [R1, KEYS], F32R) for i in range(2)]
        Qh = [s.sb(f"Qh{i}", [R1, LAT], F32R) for i in range(2)]
        Ql = [s.sb(f"Ql{i}", [R1, LAT], F32R) for i in range(2)]
        V = [s.sb(f"V{i}", [P, NKT, HD]) for i in range(2)]
        Pb = [s.sb(f"Pb{i}", [P, 1024]) for i in range(3)]
        acc = [s.sb(f"acc{i}", [P, 512]) for i in range(2)]
        pacc = [s.sb(f"pacc{i}", [P, 512]) for i in range(2)]
        OTs = s.sb("OTs", [P, 512])
        mx = s.sb("mx", [P, 4, len(CH)])
        mt = s.sb("mt", [P, 4, R1])
        den = s.sb("den", [P, 4])
        Ost = [s.sb(f"Ost{i}", [P, 4, HD]) for i in range(2)]
        p1 = [s.ps(f"p1{i}", [P, 512]) for i in range(2)]
        ST = [s.ps(f"ST{i}", [P, 1024]) for i in range(2)]
        OT = s.ps("OT", [P, 512])
        misc = s.ps("misc", [P, 512])
        names = ("k_loaded q_loaded v_loaded0 v_loaded1 init hi_ready split_ready st_done exp_done pv_done acc_done pacc_done "
                 "p1_done red_done negm_ready mrow_done mrow_ready ot_copied fin_done o_ready stored0 stored1 "
                 "dve_steps dve_first half_added pool_steps").split()
        q = {n: s.sem(n) for n in names}
        block = s.block()

        def walk(eng, body):
            with eng.Fori(0, 3) as j:
                body(j, False)
            body(3, True)

        @block.sync
        def _(sp):
            def body(j, final):
                for hb in range(2):
                    for b in range(NB):
                        i = NB * hb + b
                        sp.wait_ge(q["o_ready"], j * BODY + i + 1 + START)
                        sp.dma_start(S.O[b * 512:(b + 1) * 512, bass.ds((j * 2 + hb) * HD, HD)].rearrange("(t p) d -> p t d", p=P),
                                     Ost[b % 2][:, :, :]).then_inc(q[f"stored{b % 2}"], 16)

            walk(sp, body)
            for i in range(2):
                sp.wait_ge(q[f"stored{i}"], 16 * NH * NB // 2 + START)

        @block.gpsimd
        def _(pool):
            init = Chain(pool, q["init"])
            for i in range(2):
                init(pool.memset(Kh[i][QK:R1, :].bitcast(F32), 1.0))
                init(pool.memset(Kl[i][QK:R1, :].bitcast(F32), 0.0))
                init(pool.memset(Ql[i][QK:R1, :].bitcast(F32), 0.0))
            init(pool.memset(mt[:, :, :], 0.0))
            step = Chain(pool, q["pool_steps"], 3)
            padd = Chain(pool, q["pacc_done"], 2 * NPP - 1)

            def split(h, par, b):
                if b == 0:
                    pool.wait_ge(q["k_loaded"], h * 16 + 16 + START)
                    step(pool.tensor_tensor(Kh[par][0:QK, :], kraw[:, :], K.ones[0:QK, 0:1].broadcast_to([QK, KEYS]), ALU.mult))
                    step(pool.tensor_tensor(Kl[par][0:QK, :], kraw[:, :], Kh[par][0:QK, :].bitcast(F32), ALU.subtract))
                elif b == 1:
                    pool.wait_ge(q["q_loaded"], h * 16 + 16 + START)
                    step(pool.tensor_tensor(Qh[par][0:QK, :], qraw[:, :], K.ones[0:QK, 0:1].broadcast_to([QK, LAT]), ALU.mult))
                else:
                    emit(pool.tensor_tensor(Ql[par][0:QK, :], qraw[:, :], Qh[par][0:QK, :].bitcast(F32), ALU.subtract),
                         q["split_ready"], pool, h + 1)

            def body(j, final):
                for i in range(BODY):
                    B, par, b = j * BODY + i, i // NB, i % NB
                    for k, p in enumerate(POOL_PAIRS):
                        pool.wait_ge(q["exp_done"], B * NPAIR + p + 1 + START)
                        if k == 0:
                            padd.tile(B)
                            if i >= 2:
                                pool.wait_ge(q["acc_done"], (B - 1) * ND + START)
                            padd(pool.tensor_tensor(pacc[i % 2][:, :], Pb[p % 3][:, 0:512], Pb[p % 3][:, 512:1024], ALU.add))
                        else:
                            for half in range(2):
                                padd(pool.tensor_tensor(pacc[i % 2][:, :], pacc[i % 2][:, :],
                                                        Pb[p % 3][:, half * 512:(half + 1) * 512], ALU.add))
                    if b < 3 and not (final and par):
                        if b == 0:
                            step.tile(j * 2 + par)
                            pool.wait_ge(q["pv_done"], B * NPAIR + START)
                        split(j * 2 + par + 1, 1 - par, b)

            walk(pool, body)

        @block.tensor
        def _(pe):
            def first_pass(B, par, b, c):
                t, k = divmod(c, len(CH))
                if c >= 2:
                    pe.wait_ge(q["red_done"], B * NCH + c - 1 + START)
                else:
                    pe.wait_ge(q["red_done"], B * NCH + START)
                q0 = b * 512 + t * P
                pe.matmul(p1[c % 2][:, 0:CH[k]], Qh[par][0:QK, q0:q0 + P], Kh[par][0:QK, CA[k]:CA[k] + CH[k]],
                          start=True, stop=True).then_inc(q["p1_done"], 1)

            def max_row(B):
                pe.wait_ge(q["negm_ready"], B + 1 + START)
                for t in range(4):
                    mm = pe.matmul(misc[0:R1, t * P:(t + 1) * P], mt[:, t, :], K.ident[:, :], start=True, stop=True)
                mm.then_inc(q["mrow_done"], 1)

            def finish(B, i, t):
                if t == 0:
                    pe.wait_ge(q["ot_copied"], B + 1 + START)
                    pe.wait_ge(q["acc_done"], B * ND + ND + START)
                at, cols = t * (HD + 1), slice(t * P, (t + 1) * P)
                pe.matmul(misc[:, at:at + HD], OTs[:, cols], K.ident2[:, :], start=True, stop=True)
                mm = pe.matmul(misc[:, at + HD:at + HD + 1], acc[i % 2][:, cols], K.ones[:, 0:1], start=True, stop=True)
                if t == 3:
                    mm.then_inc(q["fin_done"], 1)

            def scores(B, i, b, par, kt):
                out = ST[(i + kt // 2) % 2][:, (kt % 2) * 512:(kt % 2 + 1) * 512]
                ks, qs = slice(kt * P, (kt + 1) * P), slice(b * 512, (b + 1) * 512)
                pe.matmul(out, Kh[par][:, ks], Qh[par][:, qs], start=True, stop=False)
                pe.matmul(out, Kh[par][:, ks], Ql[par][:, qs], start=False, stop=False)
                mm = pe.matmul(out, Kl[par][:, ks], Qh[par][:, qs], start=False, stop=True)
                if kt % 2 or kt == NKT - 1:
                    mm.then_inc(q["st_done"], 1)

            def pv(B, par, kt):
                p, o = kt // 2, kt % 2
                if o == 0:
                    pe.wait_ge(q["exp_done"], B * NPAIR + p + 1 + START)
                    if p == 0:
                        pe.wait_ge(q["ot_copied"], B + START)
                mm = pe.matmul(OT[o * HD:(o + 1) * HD, :], V[par][:, kt, :], Pb[p % 3][:, o * 512:(o + 1) * 512],
                               start=(kt < 2), stop=(kt >= NKT - 2))
                if o or kt == NKT - 1:
                    mm.then_inc(q["pv_done"], 1)

            pe.wait_ge(q["split_ready"], 1 + START)
            pe.wait_ge(q["init"], 7 + START)
            for c in range(NCH):
                first_pass(0, 0, 0, c)
            max_row(0)

            def body(j, final):
                for i in range(BODY):
                    B, par, b = j * BODY + i, i // NB, i % NB
                    last = final and i == BODY - 1
                    npar, nb = ((i + 1) % BODY) // NB, (i + 1) % NB
                    pe.wait_ge(q["mrow_ready"], B + 1 + START)
                    if b == 0:
                        pe.wait_ge(q[f"v_loaded{par}"], j * 16 + 16 + START)
                    c = 0
                    for p in range(NPAIR):
                        if p > 0:
                            pe.wait_ge(q["exp_done"], B * NPAIR + p - 1 + START)
                        elif i > 0:
                            pe.wait_ge(q["exp_done"], B * NPAIR - 1 + START)
                        else:
                            pe.wait_ge(q["exp_done"], B * NPAIR + START)
                        chunks = 0 if last else CHUNKS_AT[p]
                        if chunks and p == 0 and nb == 0:
                            pe.wait_ge(q["split_ready"], j * 2 + par + 2 + START)
                        for o in range(2):
                            if 2 * p + o < NKT:
                                scores(B, i, b, par, 2 * p + o)
                            if o < chunks:
                                first_pass(B + 1, npar, nb, c)
                                c += 1
                            if p in (2, 3) and i > 0:
                                finish(B - 1, i - 1, 2 * (p - 2) + o)
                        if p == NPAIR - 1 and not last:
                            pe.wait_ge(q["o_ready"], B + START)
                            max_row(B + 1)
                        if p > 0:
                            pv(B, par, 2 * p - 2)
                            pv(B, par, 2 * p - 1)
                        if chunks > 2:
                            first_pass(B + 1, npar, nb, c)
                            c += 1
                    pv(B, par, NKT - 1)
                if not final:
                    pe.wait_ge(q["mrow_ready"], j * BODY + BODY + 1 + START)
                else:
                    pe.wait_ge(q["o_ready"], j * BODY + BODY - 1 + START)
                for t in range(4):
                    finish(j * BODY + BODY - 1, BODY - 1, t)

            walk(pe, body)

        @block.scalar
        def _(act):
            def row(B, b, par):
                act.wait_ge(q["mrow_done"], B + 1 + START)
                emit(act.activation(Qh[par][QK:R1, b * 512:(b + 1) * 512], misc[QK:R1, :], ACT.Copy), q["mrow_ready"], act, B + 1)

            def load(h, par):
                act.dma_start(kraw[:, :], S.KT[bass.ds(h, 1), :, 0:KEYS].rearrange("h r t -> r (h t)")).then_inc(q["k_loaded"], 16)
                act.dma_start(qraw[:, :], S.QT[bass.ds(h, 1), :, 0:LAT].rearrange("h r t -> r (h t)")).then_inc(q["q_loaded"], 16)
                act.dma_start(V[par][:, :, :], S.V[bass.ds(h, 1), :, 0:NKT, :].rearrange("h p s d -> p (h s d)")).then_inc(q[f"v_loaded{par}"], 16)

            load(0, 0)
            row(0, 0, 0)

            def copy_ot(B):
                act.wait_ge(q["pv_done"], B * NPAIR + NPAIR + START)
                act.wait_ge(q["fin_done"], B + START)
                act.activation(OTs[:, :], OT[:, :], ACT.Copy).then_inc(q["ot_copied"], 1)

            def body(j, final):
                for i in range(BODY):
                    B, par, b = j * BODY + i, i // NB, i % NB
                    last = final and i == BODY - 1
                    for p in range(NPAIR):
                        w = 1024 if p < NPAIR - 1 else 512
                        act.wait_ge(q["st_done"], B * NPAIR + p + 1 + START)
                        if p >= 3:
                            act.wait_ge(q["pv_done"], B * NPAIR + p - 2 + START)
                            if p - 3 in POOL_PAIRS:
                                act.wait_ge(q["pacc_done"], B * (2 * NPP - 1) + 2 * POOL_PAIRS.index(p - 3) + 1 + START)
                            else:
                                act.wait_ge(q["acc_done"], B * ND + DP.index(p - 3) + 1 + START)
                        elif i > 0:
                            act.wait_ge(q["pv_done"], B * NPAIR - 2 + p + START)
                            act.wait_ge(q["acc_done"], B * ND - 2 + p + START)
                        else:
                            act.wait_ge(q["pv_done"], B * NPAIR + START)
                            act.wait_ge(q["acc_done"], B * ND + START)
                        act.activation(Pb[p % 3][:, 0:w], ST[(i + p) % 2][:, 0:w], ACT.Exp).then_inc(q["exp_done"], 1)
                        if p == 0:
                            if i > 0:
                                copy_ot(B - 1)
                            if b == 0 and not (final and par):
                                act.wait_ge(q["split_ready"], j * 2 + par + 1 + START)
                                act.wait_ge(q["pv_done"], B * NPAIR + START)
                                load(j * 2 + par + 1, 1 - par)
                        if p == NPAIR - 1 and not last:
                            row(B + 1, (i + 1) % NB, ((i + 1) % BODY) // NB)
                copy_ot(j * BODY + BODY - 1)

            walk(act, body)

        @block.vector
        def _(dve):
            step = Chain(dve, q["dve_steps"], 0)

            def reduce(B, c):
                t, k = divmod(c, len(CH))
                dve.wait_ge(q["p1_done"], B * NCH + c + 1 + START)
                dve.tensor_reduce(mx[:, t, k:k + 1], p1[c % 2][:, 0:CH[k]], AX.X, ALU.max).then_inc(q["red_done"], 1)

            def maxima(B):
                dve.wait_ge(q["red_done"], B * NCH + NCH + START)
                dve.tensor_reduce(mt[:, :, QK:R1], mx[:, :, :], AX.X, ALU.max, negate=True).then_inc(q["negm_ready"], 1)

            def output(B, i):
                dve.wait_ge(q["fin_done"], B + 1 + START)
                dve.wait_ge(q[f"stored{i % 2}"], out_count(B, i) + START)
                o = misc[:, 0:4 * (HD + 1)].rearrange("p (t d) -> p t d", d=HD + 1)
                emit(dve.reciprocal(den[:, :], o[:, :, HD]), q["dve_steps"], dve, B + 1)
                dve.tensor_tensor(Ost[i % 2][:, :, :], o[:, :, 0:HD], den[:, :].unsqueeze(2).broadcast_to([P, 4, HD]), ALU.mult)\
                    .then_inc(q["o_ready"], 1)

            def out_count(B, i):
                return (B - i) * 8 + (i // 2) * 16

            first = Chain(dve, q["dve_first"])
            dve.wait_ge(q["k_loaded"], 16 + START)
            first(dve.tensor_copy(Kh[0][0:QK, :], kraw[:, :]))
            first(dve.tensor_tensor(Kl[0][0:QK, :], kraw[:, :], Kh[0][0:QK, :].bitcast(F32), ALU.subtract))
            dve.wait_ge(q["q_loaded"], 16 + START)
            first(dve.tensor_copy(Qh[0][0:QK, :], qraw[:, :]))
            emit(dve.tensor_tensor(Ql[0][0:QK, :], qraw[:, :], Qh[0][0:QK, :].bitcast(F32), ALU.subtract), q["split_ready"], dve, 1)
            dve.wait_ge(q["init"], 7 + START)
            for c in range(NCH):
                reduce(0, c)
            maxima(0)

            half_added = Chain(dve, q["half_added"], ND - 1)

            def add(B, i, p):
                sums, pair = acc[i % 2], Pb[p % 3]
                dve.wait_ge(q["exp_done"], B * NPAIR + p + 1 + START)
                if p == 0:
                    if i >= 2:
                        dve.wait_ge(q["fin_done"], B - 1 + START)
                    half_added.tile(B)
                    ins = dve.tensor_tensor(sums[:, :], pair[:, 0:512], pair[:, 512:1024], ALU.add)
                else:
                    if p < NPAIR - 1:
                        half_added(dve.tensor_tensor(sums[:, :], sums[:, :], pair[:, 512:1024], ALU.add))
                    else:
                        dve.wait_ge(q["pacc_done"], (B + 1) * (2 * NPP - 1) + START)
                        half_added(dve.tensor_tensor(sums[:, :], sums[:, :], pacc[i % 2][:, :], ALU.add))
                    ins = dve.tensor_tensor(sums[:, :], sums[:, :], pair[:, 0:512], ALU.add)
                emit(ins, q["acc_done"], dve, B * ND + DP.index(p) + 1)

            def body(j, final):
                for i in range(BODY):
                    B = j * BODY + i
                    last = final and i == BODY - 1
                    c = 0
                    for p in range(NPAIR):
                        chunks = 0 if last else CHUNKS_AT[p]
                        if chunks:
                            reduce(B + 1, c)
                            c += 1
                        if chunks == 2:
                            reduce(B + 1, c)
                            c += 1
                            if p == NPAIR - 2:
                                maxima(B + 1)
                        if p > 0 and p - 1 not in POOL_PAIRS:
                            add(B, i, p - 1)
                        if chunks == 3:
                            for _ in range(2):
                                reduce(B + 1, c)
                                c += 1
                        if p == 4 and i > 0:
                            output(B - 1, i - 1)
                    add(B, i, NPAIR - 1)
                output(j * BODY + BODY - 1, BODY - 1)

            walk(dve, body)


def context_attention_phase(nc, A, K, S, l):
    with ExitStack() as x:
        s = Scope(nc, x, f"cattn{l}")
        Q = s.sb("Q", [QK, NH, P])
        Kt = s.sb("Kt", [QK, NH, P])
        V = s.sb("V", [P, NH, HD])
        mx = s.sb("mx", [P, NH])
        sums = s.sb("sums", [P, NH])
        Pr = s.sb("Pr", [P, NH, P])
        PT = s.sb("PT", [P, NH, P])
        O = s.sb("O", [P, NH, HD])
        pS, pT = s.ps("pS", [P, NH * P]), s.ps("pT", [P, NH * P])
        pO = s.ps("pO", [P, NH * HD])
        loaded, s_done, mx_ready, e_ready, t_done, t_ready, pv_done, r_ready, o_ready, stored = (
            s.sem(n) for n in ("loaded", "s_done", "mx_ready", "e_ready", "t_done", "t_ready", "pv_done", "r_ready",
                               "o_ready", "stored"))
        block = s.block()

        @block.sync
        def _(sp):
            sp.dma_start(Q[:, :, :], S.QT[:, :, CTX * P:].rearrange("h r t -> r h t")).then_inc(loaded, 16)
            sp.dma_start(Kt[:, :, :], S.KT[:, :, (CTX + 1) * P:].rearrange("h r t -> r h t")).then_inc(loaded, 16)
            sp.dma_start(V[:, :, :], S.V[:, :, CTX + 1, :].rearrange("h p d -> p h d")).then_inc(loaded, 16)
            sp.wait_ge(o_ready, 1 + START)
            sp.dma_start(S.O[CTX * P:, 0:NH * HD], O[:, :, :].rearrange("p h d -> p (h d)")).then_inc(stored, 16)
            sp.wait_ge(stored, 16 + START)

        @block.tensor
        def _(pe):
            pe.wait_ge(loaded, 48 + START)
            for h in range(NH):
                mm = pe.matmul(pS[:, h * P:(h + 1) * P], Q[:, h, :], Kt[:, h, :], start=True, stop=True)
            mm.then_inc(s_done, 1)
            pe.wait_ge(e_ready, NH + START)
            for h in range(NH):
                mm = pe.transpose(pT[:, h * P:(h + 1) * P], Pr[:, h, :], K.ident[:, :])
            mm.then_inc(t_done, 1)
            pe.wait_ge(t_ready, 1 + START)
            for h in range(NH):
                mm = pe.matmul(pO[:, h * HD:(h + 1) * HD], PT[:, h, :], V[:, h, :], start=True, stop=True)
            mm.then_inc(pv_done, 1)

        @block.scalar
        def _(act):
            act.wait_ge(mx_ready, 1 + START)
            for h in range(NH):
                act.activation(Pr[:, h, :], pS[:, h * P:(h + 1) * P], ACT.Exp, bias=mx[:, h:h + 1],
                               accum_out=sums[:, h:h + 1]).then_inc(e_ready, 1)
            act.wait_ge(t_done, 1 + START)
            act.activation(PT[:, :, :], pT[:, :], ACT.Copy).then_inc(t_ready, 1)

        @block.vector
        def _(dve):
            dve.wait_ge(s_done, 1 + START)
            dve.tensor_reduce(mx[:, :], pS[:, :].rearrange("p (h k) -> p h k", k=P), AX.X, ALU.max, negate=True).then_inc(mx_ready, 1)
            dve.wait_ge(e_ready, NH + START)
            dve.reciprocal(sums[:, :], sums[:, :]).then_inc(r_ready, 1)
            dve.wait_ge(r_ready, 1 + START)
            dve.wait_ge(pv_done, 1 + START)
            dve.tensor_tensor(O[:, :, :], pO[:, :].rearrange("p (h d) -> p h d", d=HD),
                              sums[:, :].unsqueeze(2).broadcast_to([P, NH, HD]), ALU.mult).then_inc(o_ready, 1)


def output_phase(nc, A, K, S, l, xin, xout):
    with ExitStack() as x:
        s = Scope(nc, x, f"out{l}")
        w = s.sb("w", [P, DC, D])
        O = [s.sb(f"O{i}", [P, 768]) for i in range(2)]
        C = [s.sb(f"C{i}", [P, 2, P]) for i in range(2)]
        cst = s.sb("cst", [P, 6])
        mv = s.sb("mv", [P, 2])
        md = s.sb("md", [P, 1])
        vv, rr, tt = (s.sb(n, [P, 2]) for n in ("vv", "rr", "tt"))
        ct, cth, c1, sq = (s.sb(n, [P, 256]) for n in ("ct", "cth", "c1", "sq"))
        ng, lg, lb = (s.sb(n, [P, 256]) for n in ("ng", "lg", "lb"))
        G = [s.sb(f"G{i}", [P, D]) for i in range(2)]
        X = [s.sb(f"X{i}", [P, D]) for i in range(2)]
        og = [s.sb(f"og{i}", [P, D]) for i in range(2)]
        oT = [s.sb(f"oT{i}", [P, DC, P]) for i in range(2)]
        t = s.sb("t", [P, D])
        Y = [s.sb(f"Y{i}", [P, D]) for i in range(2)]
        pT = [s.ps(f"pT{i}", [P, D]) for i in range(2)]
        pY = [s.ps(f"pY{i}", [P, D]) for i in range(2)]
        w_loaded = s.sem("w_loaded")
        loaded = [s.sem(f"loaded{i}") for i in range(2)]
        x_loaded = [s.sem(f"x_loaded{i}") for i in range(2)]
        stored = [s.sem(f"stored{i}") for i in range(2)]
        og_ready, t_done, ot_ready, y_done, y_ready, dch, tch, gains, halved, ct_done, sq_ready, c_ready, cth_ready = (
            s.sem(n) for n in ("og_ready", "t_done", "ot_ready", "y_done", "y_ready", "dve_steps", "scaled", "gains",
                               "halved", "ct_done", "sq_ready", "c_ready", "cth_ready"))
        block = s.block()

        def walk(eng, body):
            with eng.Fori(0, NLAT // 2) as j:
                for u in range(2):
                    body(j * 2 + u, u, j, False)
            body(CTX, 0, NLAT // 2, True)

        @block.sync
        def _(sp):
            def load(n, par):
                rows = bass.ds(n * P, P)
                sp.dma_start(C[par][:, :, :], S.YC[:, :, bass.ds(conv_at(n, KW // 2), P)].rearrange("f p t -> p f t")).then_inc(loaded[par], 16)
                sp.dma_start(O[par][:, :], S.O[rows, :]).then_inc(loaded[par], 16)
                sp.dma_start(G[par][:, :], S.G[rows, :]).then_inc(loaded[par], 16)

            def load_x(n, par):
                sp.dma_start(X[par][:, :], xin[bass.ds(n * P, P), :]).then_inc(x_loaded[par], 16)

            load(0, 0)
            load_x(0, 0)
            load(1, 1)
            with nc.allow_non_contiguous_dma(reason="broadcast gains"):
                for t_, src in ((ng, "ssd_norm_g"), (lg, "cf_ln_g"), (lb, "cf_ln_b")):
                    sp.dma_start(t_[:, :], A[src][l].partition_broadcast(P)).then_inc(gains, 16)
            for c in range(DC):
                sp.dma_start(w[:, c, :], A["w_out"][l, c * P:(c + 1) * P, :]).then_inc(w_loaded, 16)

            def body(n, par, load_b, load_xt):
                if load_b:
                    sp.wait_ge(og_ready, n + 1 + START)
                    load(n + 2, par)
                if load_xt:
                    sp.wait_ge(y_ready, n + START)
                    load_x(n + 1, 1 - par)
                sp.wait_ge(y_ready, n + 1 + START)
                sp.dma_start(xout[bass.ds(n * P, P), :], Y[par][:, :]).then_inc(stored[par], 16)

            with sp.Fori(0, NLAT // 2 - 1) as j:
                for u in range(2):
                    body(j * 2 + u, u, True, True)
            body(NLAT - 2, 0, True, True)
            body(NLAT - 1, 1, False, True)
            body(CTX, 0, False, False)
            sp.wait_ge(stored[0], 16 * (NT + 1) // 2 + START)
            sp.wait_ge(stored[1], 16 * NLAT // 2 + START)

        @block.tensor
        def _(pe):
            def turn_conv(n, par, cnt):
                pe.wait_ge(loaded[par], cnt * 48 + 48 + START)
                pe.wait_ge(ot_ready, (0 if isinstance(n, int) and n < 2 else n - 1) + START)
                for f in range(2):
                    mm = pe.transpose(pT[par][:, f * P:(f + 1) * P], C[par][:, f, :], K.ident[:, :])
                mm.then_inc(ct_done, 1)

            def turn(n, par):
                pe.wait_ge(og_ready, n + 1 + START)
                for c in range(DC):
                    mm = pe.transpose(pT[par][:, c * P:(c + 1) * P], og[par][:, c * P:(c + 1) * P], K.ident[:, :])
                mm.then_inc(t_done, 1)

            def body(n, par, cnt, turn_next=True, conv_next=True):
                pe.wait_ge(ot_ready, n + 1 + START)
                pe.wait_ge(tch, (0 if isinstance(n, int) and n < 2 else n - 1) + START)
                for half in range(2):
                    cols = slice(half * 512, (half + 1) * 512)
                    for c in range(DC):
                        if half and c == DC // 2 and turn_next:
                            turn(n + 1, 1 - par)
                        mm = pe.matmul(pY[par][:, cols], oT[par][:, c, :], w[:, c, cols], start=(c == 0), stop=(c == DC - 1))
                mm.then_inc(y_done, 1)
                if conv_next:
                    turn_conv(n + 2, par, cnt + 1)

            turn_conv(0, 0, 0)
            turn(0, 0)
            turn_conv(1, 1, 0)
            pe.wait_ge(w_loaded, 16 * DC + START)
            body(0, 0, 0)
            body(1, 1, 0)
            with pe.Fori(0, NLAT // 2 - 2) as j:
                for u in range(2):
                    body(j * 2 + (u + 2), u, j + 1)
            body(NLAT - 2, 0, NLAT // 2 - 1)
            body(NLAT - 1, 1, NLAT // 2 - 1, True, False)
            body(CTX, 0, NLAT // 2, False, False)

        @block.scalar
        def _(act):
            def square(n, par, cnt):
                act.wait_ge(loaded[par], cnt * 48 + 48 + START)
                emit(act.activation(sq[:, :], O[par][:, 512:768], ACT.Square, accum_out=vv[:, 0:1]), sq_ready, act, n + 1)
                act.wait_ge(c_ready, n + 1 + START)
                emit(act.activation(cth[:, :], ct[:, :], ACT.Tanh), cth_ready, act, n + 1)

            square(0, 0, 0)

            def body(n, par, j, last):
                act.wait_ge(t_done, n + 1 + START)
                act.wait_ge(y_done, n + START)
                act.activation(oT[par][:, :, :], pT[par][:, :], ACT.Copy).then_inc(ot_ready, 1)
                if not last:
                    square(n + 1, 1 - par, j + par)

            walk(act, body)

        @block.vector
        def _(dve):
            step = Chain(dve, dch, 24)
            setup = Chain(dve, halved)
            dve.wait_ge(gains, 48 + START)
            setup(dve.tensor_scalar(lg[:, :], lg[:, :], 0.5, None, ALU.mult))
            setup(dve.tensor_scalar(lb[:, :], lb[:, :], 0.5, None, ALU.mult))

            def gates(n, par, cnt):
                step.tile(n)
                dve.wait_ge(ct_done, n + 1 + START)
                conv = pT[par][:, 0:256]
                step(dve.bn_stats(cst[:, :], conv))
                halves_ = cst[:, :].rearrange("p (o c) -> p o c", o=2)
                step.go(dve.tensor_tensor(mv[:, :], halves_[:, 0, 1:3], halves_[:, 1, 1:3], ALU.add))
                step(dve.tensor_tensor(md[:, 0:1], cst[:, 1:2], cst[:, 4:5], ALU.subtract))
                step(dve.scalar_tensor_tensor(md[:, 0:1], md[:, 0:1], 0.25, md[:, 0:1], ALU.mult, ALU.mult))
                step(dve.scalar_tensor_tensor(md[:, 0:1], mv[:, 1:2], 1.0 / 256, md[:, 0:1], ALU.mult, ALU.add))
                step.go(dve.tensor_scalar(vv[:, 1:2], md[:, 0:1], EPS, None, ALU.add))
                step.go(dve.tensor_scalar(mv[:, 0:1], mv[:, 0:1], 0.5, None, ALU.mult))
                dve.wait_ge(sq_ready, n + 1 + START)
                step(dve.tensor_scalar(vv[:, 0:1], vv[:, 0:1], 1.0 / 256, EPS, ALU.mult, ALU.add))
                rsqrt_steps(dve, step, rr[:, :], vv[:, :], tt[:, :])
                step(dve.tensor_scalar(ct[:, :], conv, mv[:, 0:1], rr[:, 1:2], ALU.subtract, ALU.mult))
                step(dve.tensor_tensor(ct[:, :], ct[:, :], lg[:, :], ALU.mult))
                emit(dve.tensor_tensor(ct[:, :], ct[:, :], lb[:, :], ALU.add), c_ready, dve, n + 1)
                dve.wait_ge(loaded[par], cnt * 48 + 48 + START)
                g, o, out = G[par], O[par], og[par]
                step.go(dve.scalar_tensor_tensor(out[:, 256:512], o[:, 512:768], rr[:, 0:1], ng[:, :], ALU.mult, ALU.mult))
                step.go(dve.scalar_tensor_tensor(out[:, 0:256], g[:, 0:256], 0.5, o[:, 0:256], ALU.mult, ALU.mult))
                step.go(dve.scalar_tensor_tensor(out[:, 768:D], g[:, 768:D], 0.5, o[:, 256:512], ALU.mult, ALU.mult))
                dve.wait_ge(cth_ready, n + 1 + START)
                step(dve.scalar_tensor_tensor(c1[:, :], cth[:, :], 1.0, ct[:, :], ALU.add, ALU.mult))
                emit(dve.scalar_tensor_tensor(out[:, 512:768], g[:, 512:768], 0.5, c1[:, :], ALU.mult, ALU.mult),
                     og_ready, dve, n + 1)

            gates(0, 0, 0)

            def body(n, par, j, last):
                if not last:
                    gates(n + 1, 1 - par, j + par)
                dve.wait_ge(y_done, n + 1 + START)
                emit(dve.tensor_tensor(t[:, :], pY[par][:, :], K.gate[:, 1 if last else 0, :], ALU.mult), tch, dve, n + 1)
                dve.wait_ge(x_loaded[par], j * 16 + 16 + START)
                dve.wait_ge(stored[par], j * 16 + START)
                emit(dve.tensor_tensor(Y[par][:, :], X[par][:, :], t[:, :], ALU.add), y_ready, dve, n + 1)

            walk(dve, body)


INPUTS = {
    "x": (NT * P, D), "cache_mla_ckv": (1, DEPTH, P, KVR), "cache_mla_krope": (1, DEPTH, P, ROPE),
    "cache_gqa_k": (1, DEPTH, P, 2, HD), "cache_gqa_v": (1, DEPTH, P, 2, HD),
    "state_ssd": (1, DEPTH, 2, 4, HD, HD), "c": (1, D), "c_ctx": (D,), "w_mod": (DEPTH, D, 3 * D),
    "b_mod": (DEPTH, 3 * D), "norm_g": (DEPTH, D), "w_in": (DEPTH, D, IN_W), "w_out": (DEPTH, D, D),
    "mla_q_norm_g": (DEPTH, QR), "mla_w_uq": (DEPTH, QR, 4 * QK), "mla_kv_norm_g": (DEPTH, KVR),
    "mla_w_ukv": (DEPTH, KVR, 4 * P), "mla_q_head_g": (DEPTH, QK), "mla_k_head_g": (DEPTH, QK),
    "ssd_conv_w": (DEPTH, 3, 512), "ssd_conv_b": (DEPTH, 512), "ssd_dt_bias": (DEPTH, 2, 4),
    "ssd_a_log": (DEPTH, 2, 4), "ssd_d": (DEPTH, 4), "ssd_norm_g": (DEPTH, 256),
    "cf_conv_w": (DEPTH, KW, 256), "cf_conv_b": (DEPTH, 256), "cf_ln_g": (DEPTH, 256),
    "cf_ln_b": (DEPTH, 256), "gqa_q_g": (DEPTH, HD), "gqa_k_g": (DEPTH, HD), "rope": (NT * P, RT),
}
OUTPUTS = {
    "y": (NT * P, D), "new_mla_ckv": (1, DEPTH, P, KVR), "new_mla_krope": (1, DEPTH, P, ROPE),
    "new_gqa_k": (1, DEPTH, P, 2, HD), "new_gqa_v": (1, DEPTH, P, 2, HD),
    "new_state_ssd": (1, DEPTH, 2, 4, HD, HD),
}


class Scratch:

    def __init__(self, nc, kind):
        def dram(name, *shape):
            return nc.dram_tensor(f"scratch_{name}", shape, F32, kind=kind).ap()

        self.MODR = dram("MODR", NT * P, 2 * DC)
        self.MOD = self.MODR.rearrange("(n p) c -> n p c", p=P)
        self.QT = dram("QT", NH, QK, NT * P)
        self.KT = dram("KT", NH, QK, NSLOT * P)
        self.V = dram("V", NH, P, NSLOT, HD)
        self.G = dram("G", NT * P, D)
        self.DT = dram("DT", NT * P, 8)
        self.XC = dram("XC", 4, P, NT * P + 2)
        self.YC = dram("YC", 2, P, NT * P + 2 * (KW // 2))
        self.SB = dram("SB", NT, P, 256)
        self.O = dram("O", NT * P, 768)
        self.X1 = dram("X1", NT * P, D)


class Persistent:

    def __init__(self, nc, x):
        def sb(name, shape):
            return x.enter_context(nc.sbuf_tensor(name, shape, F32))

        self.ident = sb("ident", [P, P])
        self.ident2 = sb("ident2", [P, HD])
        self.ones = sb("ones", [P, P])
        self.tri = sb("tri", [P, 4, P])
        self.gate = sb("gate", [P, 2, D])


def build(nc, A, phases="pksao", kind="Internal", layers=DEPTH):
    S = Scratch(nc, kind)
    with ExitStack() as x:
        K = Persistent(nc, x)
        constants_phase(nc, K, S)
        for l in range(layers):
            xin = A["x"] if l == 0 else S.X1
            xout = A["y"] if l == DEPTH - 1 else S.X1
            modulation_phase(nc, A, K, S, l)
            if "p" in phases:
                projection_phase(nc, A, K, S, l, xin)
            if "k" in phases:
                cache_phase(nc, A, K, S, l)
            if "s" in phases:
                scan_phase(nc, A, K, S, l)
            if "a" in phases:
                attention_phase(nc, A, K, S, l)
                context_attention_phase(nc, A, K, S, l)
            if "o" in phases:
                output_phase(nc, A, K, S, l, xin, xout)


def kernel(**inputs):
    import concourse.bacc as bacc
    from concourse.bass_utils import run_bass_kernel_spmd

    arrays = {n: np.asarray(inputs[n]) for n in INPUTS if n not in ("x", "rope")}
    arrays["x"] = np.concatenate([np.asarray(inputs["x_sample"])[0], np.asarray(inputs["x_prompt"])[0]], 0)
    arrays["rope"] = rope_table()
    nc = bacc.Bacc("TRN2", target_bir_lowering=False, num_devices=1)
    A, feeds = {}, {}
    for n, shape in INPUTS.items():
        A[n] = nc.dram_tensor(f"in_{n}", shape, F32, kind="ExternalInput").ap()
        feeds[f"in_{n}"] = np.ascontiguousarray(arrays[n])
    for n, shape in OUTPUTS.items():
        A[n] = nc.dram_tensor(f"out_{n}", shape, F32, kind="ExternalOutput").ap()
    build(nc, A)
    r = run_bass_kernel_spmd(nc, [feeds], core_ids=[0]).results[0]
    y = r["out_y"]
    return (y[LAT:][None], y[:LAT][None]) + tuple(r[f"out_{n}"] for n in OUTPUTS if n != "y")
```

```python
from contextlib import ExitStack

import numpy as np
import concourse.bass as bass
from concourse import mybir

F32 = mybir.dt.float32
F32R = mybir.dt.float32r
I32 = mybir.dt.int32
ALU = mybir.AluOpType
ACT = mybir.ActivationFunctionType
AX = mybir.AxisListType

P = 128
D = 1024
DC = D // P
DEPTH = 2
LAT = 2048
NLAT = LAT // P
NT = NLAT + 1
CTX = NT - 1
NSLOT = NT + 1
EPS = 1e-6
GRID_W = 64
THETA = 10000.0
A_Q, A_KV, A_R, A_G = 0, 192, 320, 352
B_XBC, B_DT, B_Z = 608, 1120, 1128
C_V, C_GL, C_G = 1384, 1640, 1896
D_Q, D_K, D_V, D_G = 2152, 2408, 2536, 2664
IN_W = 2920
NDT = B_Z - B_DT
QR, KVR, ROPE, NOPE, QK, HD = 192, 128, 32, 64, 96, 64
NH = 8
KW = 31


def rope_table():
    def tab(dim):
        quarter = dim // 4
        inv = np.float32(THETA) ** (-np.arange(quarter, dtype=np.float32) / np.float32(quarter))
        row = np.repeat(np.arange(LAT // GRID_W), GRID_W).astype(np.float32)
        col = np.tile(np.arange(GRID_W), LAT // GRID_W).astype(np.float32)
        ar, ac = row[:, None] * inv, col[:, None] * inv
        ang = np.concatenate([ar, ar, ac, ac], -1).astype(np.float64)
        sign = np.repeat(np.array([-1.0, 1.0, -1.0, 1.0]), quarter)
        return np.cos(ang), np.sin(ang) * sign
    c1, s1 = tab(ROPE)
    c2, s2 = tab(HD)
    lat = np.concatenate([c1, s1, c2, s2], 1)
    ctx = np.concatenate([np.ones((P, ROPE)), np.zeros((P, ROPE)), np.ones((P, HD)), np.zeros((P, HD))], 1)
    return np.concatenate([lat, ctx], 0).astype(np.float32)


RT = 2 * ROPE + 2 * HD
START = 1


class Chain:

    def __init__(self, eng, sem, per=0, n=0):
        self.eng, self.sem, self.base, self.per, self.k = eng, sem, n * per if per else 0, per, 0

    def __call__(self, ins):
        self.k += 1
        ins.then_inc(self.sem, 1)
        self.eng.wait_ge(self.sem, self.base + self.k + START)

    def go(self, ins):
        self.k += 1
        ins.then_inc(self.sem, 1)

    def tile(self, n):
        assert self.k in (0, self.per), (self.sem, self.k)
        self.base, self.k = n * self.per, 0

    def end(self):
        assert self.k in (0, self.per), (self.sem, self.k)


class Lagged(Chain):

    def __call__(self, ins):
        self.k += 1
        ins.then_inc(self.sem, 1)
        if self.k > 1:
            self.eng.wait_ge(self.sem, self.base + self.k - 1 + START)

    def settle(self):
        self.eng.wait_ge(self.sem, self.base + self.k + START)


def emit(ins, sem, eng, value):
    ins.then_inc(sem, 1)
    eng.wait_ge(sem, value + START)


def rsqrt_steps(dve, step, y, v, t):
    step(dve.tensor_scalar(y.bitcast(I32), v.bitcast(I32), -0.5, 1597463007.0, ALU.mult, ALU.add))
    for _ in range(3):
        step(dve.scalar_tensor_tensor(t, y, -0.5, y, ALU.mult, ALU.mult))
        step(dve.tensor_tensor(t, t, v, ALU.mult))
        step(dve.scalar_tensor_tensor(y, t, 1.5, y, ALU.add, ALU.mult))


RSQRT = 10


def is_ctx(n):
    return isinstance(n, int) and n == CTX


class Scope:

    def __init__(self, nc, x, tag):
        self.nc, self.x, self.tag, self.sems = nc, x, tag, []

    def sb(self, name, shape, dt=F32):
        return self.x.enter_context(self.nc.sbuf_tensor(f"{self.tag}_{name}", shape, dt))

    def ps(self, name, shape):
        return self.x.enter_context(self.nc.psum_tensor(f"{self.tag}_{name}", shape, F32))

    def sem(self, name):
        self.sems.append(self.x.enter_context(self.nc.semaphore(f"{self.tag}_{name}")))
        return self.sems[-1]

    def start(self):
        for sem in self.sems:
            self.nc.gpsimd.sem_clear(sem)
            self.nc.gpsimd.sem_inc(sem, START)
        self.nc.all_engine_barrier()

    def block(self):
        self.start()
        return self.x.enter_context(self.nc.Block())


def constants_phase(nc, K, S):
    with ExitStack() as x:
        s = Scope(nc, x, "const")
        made = s.sem("made")
        block = s.block()

        @block.gpsimd
        def _(pool):
            step = Chain(pool, made)
            step(pool.memset(K.ident[:, :], 0.0))
            step(pool.affine_select(out=K.ident[:, :], in_=K.ident[:, :], compare_op=ALU.not_equal, fill=1.0,
                                    base=0, pattern=[[-1, P]], channel_multiplier=1))
            step(pool.memset(K.ident2[:, :], 0.0))
            for base in (0, -HD):
                step(pool.affine_select(out=K.ident2[:, :], in_=K.ident2[:, :], compare_op=ALU.not_equal,
                                        fill=1.0, base=base, pattern=[[-1, HD]], channel_multiplier=1))
            step(pool.memset(K.ones[:, :], 1.0))
            for m, (cm, pat, base) in enumerate([(1, -1, -1), (-1, 1, -1), (-1, 1, 0), (1, -1, 0)]):
                step(pool.affine_select(out=K.tri[:, m, :], in_=K.ones[:, :], compare_op=ALU.is_ge, fill=0.0,
                                        base=base, pattern=[[pat, P]], channel_multiplier=cm))


def modulation_phase(nc, A, K, S, w_in, w_in_loaded):
    RING, NB = 4, 6
    with ExitStack() as x:
        s = Scope(nc, x, "mod")
        w = [s.sb(f"w{i}", [P, 3 * D]) for i in range(RING)]
        cc = s.sb("cc", [P, 2, DC])
        th = s.sb("th", [P, 2, DC])
        sc = s.sb("sc", [P, 2, DC])
        bias = s.sb("bias", [HD + 2, DEPTH, NB // 2, 512])
        rows = s.sb("rows", [HD + 2, DEPTH, NB // 2, 512])
        ng = s.sb("ng", [P, DEPTH, DC])
        sel = s.sb("sel", [HD + 2, 2, P])
        pm = [[s.ps(f"pm{l}{i}", [P, 512]) for i in range(NB // 2)] for l in range(DEPTH)]
        pt = s.ps("pt", [P, 2 * DC, 2])
        pg = s.ps("pg", [P, 512])
        small, cond, tanhed, silued, rowed, turned, kept, spread, gated, dch = (
            s.sem(n) for n in ("small", "cond", "tanhed", "silued", "rowed", "turned", "kept", "spread", "gated", "dch"))
        loaded = [s.sem(f"loaded{i}") for i in range(RING)]
        used, zeroed, stored = s.sem("used"), s.sem("zeroed"), s.sem("stored")
        zeros = s.sb("zeros", [QK - HD, NSLOT * P])
        block = s.block()
        halves_ = [(HD * h, HD * h + 2) for h in range(2)]

        def turned_at(l, h):
            return pt if h == 0 else pm[l][0][:, 0:4 * DC].rearrange("p (m k) -> p m k", k=2)

        @block.sync
        def _(sp):
            def load(i):
                sp.dma_start(w[i % RING][:, :], A["w_mod"][i // DC, (i % DC) * P:(i % DC + 1) * P, :]).then_inc(loaded[i % RING], 16)

            with nc.allow_non_contiguous_dma(reason="small vectors, channels on partitions"):
                sp.dma_start(cc[:, 0, :], A["c"][0].rearrange("(c p) -> p c", p=P)).then_inc(cond, 16)
                sp.dma_start(cc[:, 1, :], A["c_ctx"].rearrange("(c p) -> p c", p=P)).then_inc(cond, 16)
                for i in range(RING):
                    load(i)
                for l in range(DEPTH):
                    sp.dma_start(ng[:, l, :], A["norm_g"][l].rearrange("(c p) -> p c", p=P)).then_inc(small, 16)
                    for h, (p0, p1) in enumerate(halves_):
                        src = A["b_mod"][l].rearrange("(i h n) -> i h n", h=2, n=512)[:, h, :]
                        sp.dma_start(bias[p0:p1, l, :, :], src.partition_broadcast(2)).then_inc(small, 16)
            for i in range(RING, DEPTH * DC):
                sp.wait_ge(used, i - RING + 1 + START)
                load(i)
            sp.wait_ge(zeroed, 1 + START)
            for h in range(4, NH):
                sp.dma_start(S.QT[h, HD:QK, :], zeros[:, 0:NT * P]).then_inc(stored, 16)
                sp.dma_start(S.KT[h, HD:QK, :], zeros[:, :]).then_inc(stored, 16)
            for half in range(2):
                load_input_weights(sp, A, 0, w_in[half], half * DC // 2, w_in_loaded)
            sp.wait_ge(stored, 16 * 8 + START)

        @block.gpsimd
        def _(pool):
            pool.memset(zeros[:, :], 0.0).then_inc(zeroed, 1)

        @block.tensor
        def _(pe):
            pe.wait_ge(silued, 1 + START)
            for i in range(DEPTH * DC):
                l, c = divmod(i, DC)
                pe.wait_ge(loaded[i % RING], 16 * (i // RING + 1) + START)
                for blk in range(NB):
                    p0, p1 = halves_[blk % 2]
                    mm = pe.matmul(pm[l][blk // 2][p0:p1, :], sc[:, :, c], w[i % RING][:, 512 * blk:512 * (blk + 1)],
                                   start=(c == 0), stop=(c == DC - 1))
                mm.then_inc(used, 1)
            for l in range(DEPTH):
                pe.wait_ge(rowed, l + 1 + START)
                if l:
                    pe.wait_ge(kept, l + START)
                for m in range(2 * DC):
                    blk, at = divmod(m * P, 512)
                    p0, p1 = halves_[blk % 2]
                    mm = pe.matmul(turned_at(l, blk % 2)[:, m, :], rows[p0:p1, l, blk // 2, at:at + P], K.ident[p0:p1, p0:p1], start=True, stop=True)
                mm.then_inc(turned, 1)
                for k in range(2):
                    for h, (p0, p1) in enumerate(halves_):
                        pe.wait_ge(gated, 4 * l + 2 * k + h + START)
                        pe.matmul(pg[:, :], sel[p0:p1, k, :], rows[p0:p1, l, 2, :], start=True, stop=True).then_inc(spread, 1)

        @block.scalar
        def _(act):
            act.wait_ge(cond, 32 + START)
            act.activation(th[:, :, :], cc[:, :, :], ACT.Tanh, scale=0.5).then_inc(tanhed, 1)
            for i in range(4 * DEPTH):
                act.wait_ge(spread, i + 1 + START)
                l, k, h = i // 4, i // 2 % 2, i % 2
                act.activation(K.gate[:, 2 * l + k, 512 * h:512 * (h + 1)], pg[:, :], ACT.Copy, scale=0.5).then_inc(gated, 1)

        @block.vector
        def _(dve):
            step = Chain(dve, dch)
            dve.wait_ge(tanhed, 1 + START)
            step(dve.scalar_tensor_tensor(sc[:, :, :], th[:, :, :], 1.0, cc[:, :, :], ALU.add, ALU.mult))
            emit(dve.tensor_scalar(sc[:, :, :], sc[:, :, :], 0.5, None, ALU.mult), silued, dve, 1)
            for p0, p1 in halves_:
                step(dve.tensor_copy(sel[p0:p1, :, :], K.ident[p0:p1, p0:p1].unsqueeze(2).broadcast_to([2, 2, P])))
            dve.wait_ge(small, 16 * 3 * DEPTH + START)
            for l in range(DEPTH):
                dve.wait_ge(used, DC * (l + 1) + START)
                for p0, p1 in halves_:
                    for i in range(NB // 2):
                        ins = dve.tensor_tensor(rows[p0:p1, l, i, :], pm[l][i][p0:p1, :], bias[p0:p1, l, i, :], ALU.add)
                        if i < NB // 2 - 1 or p0 == 0:
                            step(ins)
                emit(ins, rowed, dve, l + 1)
            for l in range(DEPTH):
                dve.wait_ge(turned, l + 1 + START)
                for k in range(2):
                    for h in range(2):
                        c, src = slice(4 * h, 4 * h + 4), turned_at(l, h)
                        step(dve.tensor_copy(K.mod[:, l, k, DC + 4 * h:DC + 4 * h + 4], src[:, c, k]))
                        ins = dve.scalar_tensor_tensor(K.mod[:, l, k, c], src[:, DC + 4 * h:DC + 4 * h + 4, k], 1.0, ng[:, l, c],
                                                       ALU.add, ALU.mult)
                        if not (k and h):
                            step(ins)
                emit(ins, kept, dve, l + 1)


def halves(ap, b):
    q = ap.shape[-1] // 4
    return ap.rearrange("p h (a b q) -> p h a b q", a=2, b=2, q=q)[:, :, :, b, :]


def rope_steps(pool, step, t1, t2, src, cos, sin):
    h = src.shape[1]

    def over_heads(tab):
        return tab.unsqueeze(1).broadcast_to([P, h, tab.shape[-1]])

    step(pool.tensor_tensor(t1, src, over_heads(cos), ALU.mult))
    q = src.shape[-1] // 4
    for b in range(2):
        sb = sin.rearrange("p (a b q) -> p a b q", a=2, b=2, q=q)[:, :, b, :]
        step(pool.tensor_tensor(halves(t2, b), halves(src, 1 - b), sb.unsqueeze(1).broadcast_to([P, h, 2, q]),
                                ALU.mult))


def load_input_weights(sp, A, l, w, first, loaded):
    w_in = A["w_in"][l]
    for c in range(w.shape[1]):
        rows = slice((first + c) * P, (first + c + 1) * P)
        sp.dma_start(w[:, c, 0:A_G], w_in[rows, 0:A_G]).then_inc(loaded, 16)
        sp.dma_start(w[:, c, A_G:A_G + NDT], w_in[rows, B_DT:B_Z]).then_inc(loaded, 16)
        sp.dma_start(w[:, c, A_G + NDT:B_Z], w_in[rows, A_G:B_DT]).then_inc(loaded, 16)
        sp.dma_start(w[:, c, B_Z:], w_in[rows, B_Z:]).then_inc(loaded, 16)


class InputWeights:

    def __init__(self, nc, x, l):
        self.s = Scope(nc, x, f"w_in{l}")
        self.loaded, self.halves = self.s.sem("loaded"), []
        self.s.start()

    def add_half(self):
        self.halves.append(self.s.sb(f"w{len(self.halves)}", [P, DC // 2, IN_W]))
        return self.halves[-1]


def projection_phase(nc, A, K, S, l, xin, w, w_loaded, load_rest):
    hx, hg = 1, KW // 2
    with ExitStack() as x:
        s = Scope(nc, x, f"proj{l}")
        wuq = s.sb("wuq", [QK, 2, 4 * QK])
        wukv = s.sb("wukv", [P, 4 * P])
        gq = s.sb("gq", [P, QR])
        gkv = s.sb("gkv", [P, KVR])
        qkg = s.sb("qkg", [P, 8, QK])
        gg = s.sb("gg", [P, 6, HD])
        xt = [s.sb(f"xt{i}", [P, D]) for i in range(2)]
        rp = s.sb("rp", [P, RT])
        xn = s.sb("xn", [P, D])
        hT = [s.sb(f"hT{i}", [P, DC, P]) for i in range(2)]
        junk = s.sb("junk", [P, D])
        pss, pv, pr, ptmp = (s.sb(n, [P, 1]) for n in ("pss", "pv", "pr", "ptmp"))
        E0 = s.sb("E0", [P, 360])
        ss0, v0, r0, tmp0 = (s.sb(n, [P, 2]) for n in ("ss0", "v0", "r0", "tmp0"))
        krss = s.sb("krss", [P, 1])
        ql = s.sb("ql", [P, QR])
        ck = s.sb("ck", [P, KVR])
        LT = s.sb("LT", [P, 3, P])
        qsq = s.sb("qsq", [P, 4, QK])
        KV = s.sb("KV", [P, 4, P])
        ksq = s.sb("ksq", [P, 4, NOPE])
        ssh, vh, rh, tmph = (s.sb(n, [P, 8]) for n in ("ssh", "vh", "rh", "tmph"))
        QKt = s.sb("QKt", [P, 8, QK])
        E3 = s.sb("E3", [P, 8, HD])
        gsq = s.sb("gsq", [P, 6, HD])
        ssg, vg, rg, tmpg = (s.sb(n, [P, 6]) for n in ("ssg", "vg", "rg", "tmpg"))
        GN = s.sb("GN", [P, 6, HD])
        GR = s.sb("GR", [P, 6, HD])
        t1 = s.sb("t1", [P, 6, HD])
        t2 = s.sb("t2", [P, 6, HD])
        m1 = s.sb("m1", [P, 8, ROPE])
        m2 = s.sb("m2", [P, 8, ROPE])
        TH = [s.sb(f"TH{i}", [P, 512]) for i in range(2)]
        TG = s.sb("TG", [P, 256])
        GT = s.sb("GT", [P, D])
        XW = [s.sb(f"XW{i}", [P, 4, 2 * hx + P]) for i in range(2)]
        GW = [s.sb(f"GW{i}", [P, 2, 2 * hg + P]) for i in range(2)]
        TX = s.sb("TX", [P, 4, 4 * hx + P])
        TW = s.sb("TW", [P, 2, 4 * hg + P])
        XY = s.sb("XY", [P, 4, P + 2 * hx])
        XH = s.sb("XH", [P, 4, P + 2 * hx])
        XZ = s.sb("XZ", [P, 4, P + 2 * hx])
        GY = [s.sb(f"GY{i}", [P, 2, P + 2 * hg]) for i in range(2)]
        cw = s.sb("cw", [P, 4, 3])
        cb = s.sb("cb", [P, 4])
        fw = s.sb("fw", [P, 2, KW])
        fb = s.sb("fb", [P, 2])
        QST = s.sb("QST", [QK, 4, P])
        KST = s.sb("KST", [QK, 4, P])
        GST = s.sb("GST", [P, 3, P])
        b = [s.ps(f"b{i}", [P, 512]) for i in range(8)]
        names = ("small x_loaded rp_loaded gains ss_ready r_ready xn_ready xT_done ht_act ht_dve "
                 "t0_done t1_done t2_done t3_done s1_done s2_done s3_done s5_done f0_done f1_done e0_ready e3_ready "
                 "th1_ready th2_ready th3_ready qlck_ready lt_ready sq_ready qk_ready qkr_ready gn_ready gr_ready "
                 "gate1_ready gates_ready fb_ready fg_ready qst_ready kst_ready gst_ready "
                 "st_dt st_v3 st_v st_q st_k st_g st_gd st_xc st_yc st_out act_steps act_pre dve_steps dve_pre "
                 "taps padded hist_ready xy_ready xh_ready xc_ready conv_ready conv_steps act_hist "
                 "pool_steps").split()
        q = {n: s.sem(n) for n in names}
        block = s.block()

        @block.sync
        def _(sp):
            def walk(tile):
                tile(0, 0, False, False)
                with sp.Fori(0, NLAT // 2 - 1) as j:
                    for u in range(2):
                        tile(j * 2 + (u + 1), 1 - u, False)
                tile(NLAT - 1, 1, False)
                tile(CTX, 0, True)

            sp.dma_start(xt[0][:, :], xin[0:P, :]).then_inc(q["x_loaded"], 16)
            with nc.allow_non_contiguous_dma(reason="broadcast gains"):
                sp.dma_start(wuq[:, :, :], A["mla_w_uq"][l].rearrange("(a p) n -> p a n", a=2)).then_inc(q["small"], 16)
                sp.dma_start(wukv[:, :], A["mla_w_ukv"][l]).then_inc(q["small"], 16)
                sp.dma_start(gq[:, :], A["mla_q_norm_g"][l].partition_broadcast(P)).then_inc(q["small"], 16)
                sp.dma_start(gkv[:, :], A["mla_kv_norm_g"][l].partition_broadcast(P)).then_inc(q["small"], 16)
                for h in range(8):
                    g = A["mla_q_head_g" if h < 4 else "mla_k_head_g"]
                    sp.dma_start(qkg[:, h, :], g[l].partition_broadcast(P)).then_inc(q["small"], 16)
                for h in range(6):
                    g = A["gqa_q_g" if h < 4 else "gqa_k_g"]
                    sp.dma_start(gg[:, h, :], g[l].partition_broadcast(P)).then_inc(q["small"], 16)

            def load_x(m, par):
                sp.wait_ge(q["xn_ready"], m + START)
                sp.wait_ge(q["ht_act"], m + START)
                sp.wait_ge(q["ht_dve"], m + START)
                sp.dma_start(xt[par][:, :], xin[bass.ds(m * P, P), :]).then_inc(q["x_loaded"], 16)

            if load_rest:
                load_input_weights(sp, A, l, w[1], DC // 2, w_loaded)
            sp.dma_start(rp[:, :], A["rope"][0:P, :]).then_inc(q["rp_loaded"], 16)
            with nc.allow_non_contiguous_dma(reason="taps, channels on partitions"):
                for f in range(4):
                    sp.dma_start(cw[:, f, :], A["ssd_conv_w"][l][:, f * P:(f + 1) * P].rearrange("k p -> p k")).then_inc(q["taps"], 16)
                sp.dma_start(cb[:, :], A["ssd_conv_b"][l].rearrange("(f p) -> p f", p=P)).then_inc(q["taps"], 16)
                for f in range(2):
                    sp.dma_start(fw[:, f, :], A["cf_conv_w"][l][:, f * P:(f + 1) * P].rearrange("k p -> p k")).then_inc(q["taps"], 16)
                sp.dma_start(fb[:, :], A["cf_conv_b"][l].rearrange("(f p) -> p f", p=P)).then_inc(q["taps"], 16)

            def store_conv(m, at, width, par):
                sp.wait_ge(q["xc_ready"], m + 1 + START)
                sp.dma_start(S.XC[:, :, bass.ds(at, P + 2 * hx * width)].rearrange("f p t -> p f t"),
                             XZ[:, :, 0:P + 2 * hx * width]).then_inc(q["st_xc"], 16)
                sp.wait_ge(q["conv_ready"], m + 1 + START)
                sp.dma_start(S.YC[:, :, bass.ds(at, P + 2 * hg * width)].rearrange("f p t -> p f t"),
                             GY[par][:, :, 0:P + 2 * hg * width]).then_inc(q["st_yc"], 16)

            def tile(n, par, last, conv=True):
                if not last:
                    load_x(n + 1, 1 - par)
                sp.wait_ge(q["e0_ready"], n + 1 + START)
                sp.dma_start(S.DT[bass.ds(n * P, P), :], E0[:, 352:360]).then_inc(q["st_dt"], 16)
                if last:
                    sp.dma_start(A["new_mla_krope"][0, l], E0[:, A_R:A_R + ROPE]).then_inc(q["st_out"], 16)
                    sp.wait_ge(q["qlck_ready"], n + 1 + START)
                    sp.dma_start(A["new_mla_ckv"][0, l], ck[:, :]).then_inc(q["st_out"], 16)
                sp.wait_ge(q["e3_ready"], n + 1 + START)
                for r in range(2):
                    sp.dma_start(S.V[4 + r:NH:2, :, bass.ds(n + 1, 1), :].rearrange("h p s d -> p h (s d)"),
                                 E3[:, 6:8, :]).then_inc(q["st_v3"], 16)
                if last:
                    sp.dma_start(A["new_gqa_v"][0, l], E3[:, 6:8, :]).then_inc(q["st_out"], 16)
                    sp.wait_ge(q["gn_ready"], n + 1 + START)
                    sp.dma_start(A["new_gqa_k"][0, l], GN[:, 4:6, :]).then_inc(q["st_out"], 16)
                sp.wait_ge(q["gates_ready"], n + 1 + START)
                sp.dma_start(S.G[bass.ds(n * P, P), :], GT[:, :]).then_inc(q["st_gd"], 16)
                if not last:
                    sp.wait_ge(q["qkr_ready"], n + 1 + START)
                    sp.dma_start(rp[:, :], A["rope"][bass.ds((n + 1) * P, P), :]).then_inc(q["rp_loaded"], 16)
                if conv:
                    store_conv(n - 1, n * P - P, 0, 1 - par)

            walk(tile)
            store_conv(CTX, CTX * P, 1, 0)
            for n, per in (("st_dt", 16), ("st_v3", 32), ("st_v", 16), ("st_q", 16), ("st_k", 16), ("st_g", 96),
                           ("st_gd", 16), ("st_xc", 16), ("st_yc", 16)):
                sp.wait_ge(q[n], per * NT + START)
            sp.wait_ge(q["st_out"], 64 + START)

        @block.scalar
        def _(act):
            step = Chain(act, q["act_steps"], 7)

            def pre(m, par):
                act.wait_ge(q["x_loaded"], (m + 1) * 16 + START)
                emit(act.activation(junk[:, :], xt[par][:, :], ACT.Square, accum_out=pss[:, :]), q["ss_ready"], act, m + 1)
                act.wait_ge(q["r_ready"], m + 1 + START)
                act.wait_ge(q["xT_done"], m + START)
                emit(act.activation(xn[:, :], xt[par][:, :], ACT.Copy, scale=pr[:, :]), q["xn_ready"], act, m + 1)

            def evac_hT(m, par):
                md = K.mod[:, l, 1 if is_ctx(m) else 0, :]
                act.wait_ge(q["xT_done"], m + 1 + START)
                pst = Chain(act, q["act_pre"], 3, m)
                for c in range(4):
                    ins = act.activation(hT[par][:, c, :], b[0][:, c * P:(c + 1) * P], ACT.Identity,
                                         scale=md[:, c:c + 1], bias=md[:, DC + c:DC + c + 1])
                    if c < 3:
                        pst(ins)
                    else:
                        emit(ins, q["ht_act"], act, m + 1)

            def tile(n, par, last, conv=True):
                step.tile(n)
                act.wait_ge(q["t1_done"], n + 1 + START)
                emit(act.activation(TH[0][:, :], b[3][:, :], ACT.Tanh, scale=0.5), q["th1_ready"], act, n + 1)
                act.wait_ge(q["t0_done"], n + 1 + START)
                act.wait_ge(q["st_dt"], n * 16 + START)
                step(act.activation(E0[:, :], b[2][:, 0:360], ACT.Copy))
                step(act.activation(junk[:, 0:QR], E0[:, 0:QR], ACT.Square, accum_out=ss0[:, 0:1]))
                step(act.activation(junk[:, 0:KVR], E0[:, A_KV:A_R], ACT.Square, accum_out=ss0[:, 1:2]))
                emit(act.activation(junk[:, 0:ROPE], E0[:, A_R:A_G], ACT.Square, accum_out=krss[:, :]),
                     q["e0_ready"], act, n + 1)
                if not last:
                    pre(n + 1, 1 - par)
                act.wait_ge(q["t3_done"], n + 1 + START)
                act.wait_ge(q["st_v3"], n * 32 + START)
                step(act.activation(E3[:, :, :], b[5][:, :], ACT.Copy))
                emit(act.activation(gsq[:, :, :], E3[:, 0:6, :], ACT.Square), q["e3_ready"], act, n + 1)
                act.wait_ge(q["s1_done"], n + 1 + START)
                step(act.activation(LT[0:QK, 0:2, :], b[7][0:QK, 0:2 * P], ACT.Copy))
                emit(act.activation(LT[:, 2, :], b[7][:, 2 * P:3 * P], ACT.Copy), q["lt_ready"], act, n + 1)
                act.wait_ge(q["t2_done"], n + 1 + START)
                emit(act.activation(TH[1][:, :], b[4][:, :], ACT.Tanh, scale=0.5), q["th2_ready"], act, n + 1)
                act.wait_ge(q["s2_done"], n + 1 + START)
                step(act.activation(qsq[:, :, :], b[2][:, 0:4 * QK], ACT.Square))
                act.wait_ge(q["st_v"], n * 16 + START)
                step(act.activation(KV[:, :, :], b[7][:, :], ACT.Copy))
                emit(act.activation(ksq[:, :, :], KV[:, :, 0:NOPE], ACT.Square), q["sq_ready"], act, n + 1)
                act.dma_start(S.V[0:4, :, bass.ds(n + 1, 1), :].rearrange("h p s d -> p h (s d)"),
                             KV[:, :, NOPE:P]).then_inc(q["st_v"], 16)
                act.wait_ge(q["f0_done"], n + 1 + START)
                if conv:
                    act.wait_ge(q["conv_ready"], n - 1 + START)
                if last:
                    act.wait_ge(q["padded"], 4 + START)
                to = TX[:, :, 3 * hx:3 * hx + P] if last else XW[par][:, :, 2 * hx:]
                emit(act.activation(to, b[6][:, :].rearrange("p (f t) -> p f t", f=4), ACT.Copy), q["fb_ready"], act, n + 1)
                if conv:
                    act.wait_ge(q["fg_ready"], n + START)
                    to, tog = (TX, TW) if last else (XW[par], GW[par])
                    emit(act.activation(to[:, :, 0:2 * hx], XW[1 - par][:, :, P:], ACT.Copy), q["act_hist"], act, n)
                    emit(act.activation(tog[:, :, 0:2 * hg], GW[1 - par][:, :, P:], ACT.Copy), q["hist_ready"], act, n)
                    silu_tanh(n - 1, 0)
                if not last:
                    evac_hT(n + 1, 1 - par)
                act.wait_ge(q["f1_done"], n + 1 + START)
                emit(act.activation(TG[:, :], b[6][:, 256:512], ACT.Tanh, scale=0.5), q["th3_ready"], act, n + 1)
                act.wait_ge(q["s3_done"], n + 1 + START)
                act.wait_ge(q["st_q"], n * 16 + START)
                emit(act.activation(QST[:, :, :], b[2][0:QK, :], ACT.Copy), q["qst_ready"], act, n + 1)
                act.dma_start(S.QT[0:4, :, bass.ds(n * P, P)].rearrange("h r t -> r h t"), QST[:, :, :]).then_inc(q["st_q"], 16)
                act.wait_ge(q["st_k"], n * 16 + START)
                emit(act.activation(KST[:, :, :], b[7][0:QK, :], ACT.Copy), q["kst_ready"], act, n + 1)
                act.dma_start(S.KT[0:4, :, bass.ds((n + 1) * P, P)].rearrange("h r t -> r h t"), KST[:, :, :]).then_inc(q["st_k"], 16)
                act.wait_ge(q["s5_done"], n + 1 + START)
                act.wait_ge(q["st_g"], n * 96 + START)
                emit(act.activation(GST[:, :, :], b[5][:, 0:3 * P], ACT.Copy), q["gst_ready"], act, n + 1)
                for o in range(2):
                    rows = slice(o * HD, (o + 1) * HD)
                    act.dma_start(S.QT[4 + o:NH:2, 0:HD, bass.ds(n * P, P)].rearrange("h r t -> r h t"),
                                 GST[rows, 0:2, :]).then_inc(q["st_g"], 16)
                    for h in (4 + 2 * o, 5 + 2 * o):
                        act.dma_start(S.KT[h, 0:HD, bass.ds((n + 1) * P, P)], GST[rows, 2, :]).then_inc(q["st_g"], 16)
                step.end()

            def silu_tanh(m, width):
                act.wait_ge(q["xy_ready"], m + 1 + START)
                w_ = P + 2 * hx * width
                act.activation(XH[:, :, 0:w_], XY[:, :, 0:w_], ACT.Tanh).then_inc(q["xh_ready"], 1)

            act.wait_ge(q["x_loaded"], 16 + START)
            emit(act.activation(junk[:, :], xt[0][:, :], ACT.Square, accum_out=pss[:, :]), q["ss_ready"], act, 1)
            act.wait_ge(q["r_ready"], 1 + START)
            emit(act.activation(xn[:, :], xt[0][:, :], ACT.Copy, scale=pr[:, :]), q["xn_ready"], act, 1)
            evac_hT(0, 0)
            tile(0, 0, False, False)
            with act.Fori(0, NLAT // 2 - 1) as j:
                for u in range(2):
                    tile(j * 2 + (u + 1), 1 - u, False)
            tile(NLAT - 1, 1, False)
            tile(CTX, 0, True)
            silu_tanh(CTX, 1)

        @block.vector
        def _(dve):
            setup = Chain(dve, q["gains"])
            step = Chain(dve, q["dve_steps"], 3 + RSQRT + 3 + RSQRT + 7 + RSQRT)
            conv = Lagged(dve, q["conv_steps"], 3 * 4 + 2 * KW - 2)

            def halved_taps():
                dve.wait_ge(q["taps"], 16 * 8 + START)
                for t in (cw, fw):
                    setup(dve.tensor_scalar(t[:, :, :], t[:, :, :], 0.5, None, ALU.mult))
                setup(dve.tensor_scalar(cb[:, :], cb[:, :], 0.5, None, ALU.mult))

            def conv_begin(m):
                conv.tile(m)
                dve.wait_ge(q["hist_ready"], m + START)

            def conv_x(m, par, width=0):
                X, w_ = TX if width else XW[par], P + 2 * hx * width
                dve.wait_ge(q["fb_ready"], m + 1 + START)
                for f in range(4):
                    conv(dve.tensor_scalar(XY[:, f, 0:w_], X[:, f, 1:1 + w_], cw[:, f, 1:2], cb[:, f:f + 1], ALU.mult, ALU.add))
                for k in (0, 2):
                    for f in range(4):
                        final = k == 2 and f == 3
                        if final:
                            conv.settle()
                        ins = dve.scalar_tensor_tensor(XY[:, f, 0:w_], X[:, f, k:k + w_], cw[:, f, k:k + 1], XY[:, f, 0:w_],
                                                       ALU.mult, ALU.add)
                        if final:
                            emit(ins, q["xy_ready"], dve, m + 1)
                        else:
                            conv(ins)

            def conv_silu(m, width=0):
                w_ = P + 2 * hx * width
                dve.wait_ge(q["xh_ready"], m + 1 + START)
                dve.wait_ge(q["st_xc"], m * 16 + START)
                emit(dve.scalar_tensor_tensor(XZ[:, :, 0:w_], XH[:, :, 0:w_], 1.0, XY[:, :, 0:w_], ALU.add, ALU.mult),
                     q["xc_ready"], dve, m + 1)

            def conv_g(m, par, taps, width=0):
                X, w_ = TW if width else GW[par], P + 2 * hg * width
                for k in taps:
                    for f in range(2):
                        y = GY[par][:, f, 0:w_]
                        if k == 0:
                            conv(dve.tensor_scalar(y, X[:, f, 0:w_], fw[:, f, 0:1], fb[:, f:f + 1], ALU.mult, ALU.add))
                            continue
                        final = k == KW - 1 and f == 1
                        if final:
                            conv.settle()
                        ins = dve.scalar_tensor_tensor(y, X[:, f, k:k + w_], fw[:, f, k:k + 1], y, ALU.mult, ALU.add)
                        if final:
                            emit(ins, q["conv_ready"], dve, m + 1)
                        else:
                            conv(ins)

            def pre(m, par):
                pst = Chain(dve, q["dve_pre"], RSQRT + 3, m)
                dve.wait_ge(q["ss_ready"], m + 1 + START)
                pst(dve.tensor_scalar(pv[:, :], pss[:, :], 1.0 / D, EPS, ALU.mult, ALU.add))
                rsqrt_steps(dve, lambda i: pst(i) if pst.k < RSQRT else emit(i, q["r_ready"], dve, m + 1),
                            pr[:, :], pv[:, :], ptmp[:, :])
                assert pst.k == RSQRT

            def evac_hT(m, par):
                md = K.mod[:, l, 1 if is_ctx(m) else 0, :]
                pst = Chain(dve, q["dve_pre"], RSQRT + 3, m)
                pst.k = RSQRT
                dve.wait_ge(q["xT_done"], m + 1 + START)
                for c in range(4, 8):
                    ins = dve.tensor_scalar(hT[par][:, c, :], b[1][:, (c - 4) * P:(c - 3) * P],
                                            md[:, c:c + 1], md[:, DC + c:DC + c + 1], ALU.mult, ALU.add)
                    if c < 7:
                        pst(ins)
                    else:
                        emit(ins, q["ht_dve"], dve, m + 1)
                pst.end()

            def tile(n, par, last, with_conv=True):
                step.tile(n)

                def g_taps(a, e):
                    if with_conv:
                        conv_g(n - 1, 1 - par, range(a, e))

                dve.wait_ge(q["th1_ready"], n + 1 + START)
                dve.wait_ge(q["st_gd"], n * 16 + START)
                emit(dve.scalar_tensor_tensor(GT[:, 0:512], TH[0][:, :], 1.0, b[3][:, :], ALU.add, ALU.mult),
                     q["gate1_ready"], dve, n + 1)
                if with_conv:
                    conv_begin(n - 1)
                g_taps(0, 4)
                dve.wait_ge(q["e0_ready"], n + 1 + START)
                step(dve.tensor_scalar(v0[:, 0:1], ss0[:, 0:1], 1.0 / QR, EPS, ALU.mult, ALU.add))
                step(dve.tensor_scalar(v0[:, 1:2], ss0[:, 1:2], 1.0 / KVR, EPS, ALU.mult, ALU.add))
                rsqrt_steps(dve, step, r0[:, :], v0[:, :], tmp0[:, :])
                step(dve.scalar_tensor_tensor(ql[:, :], E0[:, 0:QR], r0[:, 0:1], gq[:, :], ALU.mult, ALU.mult))
                emit(dve.scalar_tensor_tensor(ck[:, :], E0[:, A_KV:A_R], r0[:, 1:2], gkv[:, :], ALU.mult, ALU.mult),
                     q["qlck_ready"], dve, n + 1)
                if not last:
                    pre(n + 1, 1 - par)
                if with_conv:
                    conv_x(n - 1, 1 - par)
                dve.wait_ge(q["e3_ready"], n + 1 + START)
                step(dve.tensor_reduce(ssg[:, :], gsq[:, :, :], AX.X, ALU.add))
                step(dve.tensor_scalar(vg[:, :], ssg[:, :], 1.0 / HD, EPS, ALU.mult, ALU.add))
                rsqrt_steps(dve, step, rg[:, :], vg[:, :], tmpg[:, :])
                step(dve.tensor_tensor(GN[:, :, :], E3[:, 0:6, :], rg[:, :].unsqueeze(2).broadcast_to([P, 6, HD]), ALU.mult))
                emit(dve.tensor_tensor(GN[:, :, :], GN[:, :, :], gg[:, :, :], ALU.mult), q["gn_ready"], dve, n + 1)
                g_taps(4, 8)
                dve.wait_ge(q["th2_ready"], n + 1 + START)
                emit(dve.scalar_tensor_tensor(GT[:, 512:D], TH[1][:, :], 1.0, b[4][:, :], ALU.add, ALU.mult),
                     q["gates_ready"], dve, n + 1)
                g_taps(8, 14)
                dve.wait_ge(q["sq_ready"], n + 1 + START)
                step(dve.tensor_reduce(ssh[:, 0:4], qsq[:, :, :], AX.X, ALU.add))
                step(dve.tensor_reduce(ssh[:, 4:8], ksq[:, :, :], AX.X, ALU.add))
                step(dve.tensor_scalar(ssh[:, 4:8], ssh[:, 4:8], krss[:, 0:1], None, ALU.add))
                step(dve.tensor_scalar(vh[:, :], ssh[:, :], 1.0 / QK, EPS, ALU.mult, ALU.add))
                rsqrt_steps(dve, step, rh[:, :], vh[:, :], tmph[:, :])

                def rows(a, b_, w_):
                    return rh[:, a:b_].unsqueeze(2).broadcast_to([P, b_ - a, w_])

                step(dve.tensor_tensor(QKt[:, 0:4, :], b[2][:, 0:4 * QK].rearrange("p (h d) -> p h d", h=4),
                                       rows(0, 4, QK), ALU.mult))
                step(dve.tensor_tensor(QKt[:, 4:8, 0:NOPE], KV[:, :, 0:NOPE], rows(4, 8, NOPE), ALU.mult))
                step(dve.tensor_tensor(QKt[:, 4:8, NOPE:QK], E0[:, A_R:A_G].unsqueeze(1).broadcast_to([P, 4, ROPE]),
                                       rows(4, 8, ROPE), ALU.mult))
                emit(dve.tensor_tensor(QKt[:, :, :], QKt[:, :, :], qkg[:, :, :], ALU.mult), q["qk_ready"], dve, n + 1)
                g_taps(14, 20)
                if not last:
                    evac_hT(n + 1, 1 - par)
                if with_conv:
                    conv_silu(n - 1)
                g_taps(20, KW)
                dve.wait_ge(q["th3_ready"], n + 1 + START)
                to = TW[:, :, 3 * hg:3 * hg + P] if last else GW[par][:, :, 2 * hg:]
                emit(dve.scalar_tensor_tensor(to, TG[:, :].rearrange("p (f t) -> p f t", f=2), 1.0,
                                              b[6][:, 0:256].rearrange("p (f t) -> p f t", f=2), ALU.add, ALU.mult),
                     q["fg_ready"], dve, n + 1)
                step.end()

            pre(0, 0)
            evac_hT(0, 0)
            dve.wait_ge(q["small"], 16 * 18 + START)
            setup(dve.tensor_scalar(qkg[:, 0:4, :], qkg[:, 0:4, :], float(QK) ** -0.5, None, ALU.mult))
            setup(dve.tensor_scalar(gg[:, 0:4, :], gg[:, 0:4, :], float(HD) ** -0.5, None, ALU.mult))
            tile(0, 0, False, False)
            halved_taps()
            dve.wait_ge(q["padded"], 4 + START)
            with dve.Fori(0, NLAT // 2 - 1) as j:
                for u in range(2):
                    tile(j * 2 + (u + 1), 1 - u, False)
            tile(NLAT - 1, 1, False)
            tile(CTX, 0, True)
            conv_begin(CTX)
            conv_x(CTX, 0, 1)
            conv_silu(CTX, 1)
            conv_g(CTX, 0, range(KW), 1)

        @block.gpsimd
        def _(pool):
            step = Chain(pool, q["pool_steps"], 6)

            def tile(n, par, last):
                step.tile(n)
                pool.wait_ge(q["rp_loaded"], (n + 1) * 16 + START)
                pool.wait_ge(q["gn_ready"], n + 1 + START)
                rope_steps(pool, step, t1[:, :, :], t2[:, :, :], GN[:, :, :], rp[:, 64:128], rp[:, 128:192])
                emit(pool.tensor_tensor(GR[:, :, :], t1[:, :, :], t2[:, :, :], ALU.add), q["gr_ready"], pool, n + 1)
                pool.wait_ge(q["qk_ready"], n + 1 + START)
                rope_steps(pool, step, m1[:, :, :], m2[:, :, :], QKt[:, :, NOPE:QK], rp[:, 0:32], rp[:, 32:64])
                emit(pool.tensor_tensor(QKt[:, :, NOPE:QK], m1[:, :, :], m2[:, :, :], ALU.add), q["qkr_ready"], pool, n + 1)
                step.end()

            pad = Chain(pool, q["padded"])
            for i, t in enumerate((XW[0][:, :, 0:2 * hx], GW[0][:, :, 0:2 * hg], TX[:, :, :], TW[:, :, :])):
                pad(pool.memset(t, 0.0))
            with pool.Fori(0, NLAT // 2) as j:
                for u in range(2):
                    tile(j * 2 + u, u, False)
            tile(CTX, 0, True)

        @block.tensor
        def _(pe):
            def xT(m):
                pe.wait_ge(q["xn_ready"], m + 1 + START)
                pe.wait_ge(q["ht_act"], m + START)
                pe.wait_ge(q["ht_dve"], m + START)
                for c in range(DC):
                    mm = pe.transpose(b[c // 4][:, (c % 4) * P:(c % 4 + 1) * P], xn[:, c * P:(c + 1) * P], K.ident[:, :])
                mm.then_inc(q["xT_done"], 1)

            def w_at(c):
                return w[c // (DC // 2)][:, c % (DC // 2), :]

            def tokens(par, bank, parts):
                at = 0
                for a, e in parts:
                    for c in range(DC):
                        mm = pe.matmul(b[bank][:, at:at + e - a], hT[par][:, c, :], w_at(c)[:, a:e],
                                       start=(c == 0), stop=(c == DC - 1))
                    at += e - a
                return mm

            def channels(par, bank, cols):
                for f, a in enumerate(cols):
                    for c in range(DC):
                        mm = pe.matmul(b[bank][:, f * P:(f + 1) * P], w_at(c)[:, a:a + P], hT[par][:, c, :],
                                       start=(c == 0), stop=(c == DC - 1))
                return mm

            def tile(n, par, last):
                pe.wait_ge(q["ht_act"], n + 1 + START)
                pe.wait_ge(q["ht_dve"], n + 1 + START)
                pe.wait_ge(q["gate1_ready"], n + START)
                tokens(par, 3, [(A_G + NDT, B_XBC + NDT), (B_Z, C_V)]).then_inc(q["t1_done"], 1)
                pe.wait_ge(q["qst_ready"], n + START)
                tokens(par, 2, [(A_Q, A_G + NDT)]).then_inc(q["t0_done"], 1)
                pe.wait_ge(q["gst_ready"], n + START)
                tokens(par, 5, [(D_Q, D_G)]).then_inc(q["t3_done"], 1)
                pe.wait_ge(q["kst_ready"], n + START)
                pe.wait_ge(q["qlck_ready"], n + 1 + START)
                for a in range(2):
                    pe.transpose(b[7][0:QK, a * P:(a + 1) * P], ql[:, a * QK:(a + 1) * QK], K.ident[:, :])
                pe.transpose(b[7][:, 2 * P:3 * P], ck[:, :], K.ident[:, :]).then_inc(q["s1_done"], 1)
                pe.wait_ge(q["gates_ready"], n + START)
                tokens(par, 4, [(C_G, D_Q), (D_G, IN_W)]).then_inc(q["t2_done"], 1)
                pe.wait_ge(q["lt_ready"], n + 1 + START)
                for a in range(2):
                    pe.matmul(b[2][:, 0:4 * QK], LT[0:QK, a, :], wuq[:, a, :], start=(a == 0), stop=(a == 1))
                pe.matmul(b[7][:, :], LT[:, 2, :], wukv[:, :], start=True, stop=True).then_inc(q["s2_done"], 1)
                pe.wait_ge(q["fg_ready"], n + START)
                channels(par, 6, [B_XBC + NDT + P * f for f in range(4)]).then_inc(q["f0_done"], 1)
                if not last:
                    xT(n + 1)
                pe.wait_ge(q["fb_ready"], n + 1 + START)
                channels(par, 6, [C_V, C_V + P, C_GL, C_GL + P]).then_inc(q["f1_done"], 1)
                pe.wait_ge(q["qkr_ready"], n + 1 + START)
                for h in range(8):
                    mm = pe.transpose(b[2 if h < 4 else 7][0:QK, (h % 4) * P:(h % 4 + 1) * P], QKt[:, h, :], K.ident[:, :])
                mm.then_inc(q["s3_done"], 1)
                pe.wait_ge(q["gr_ready"], n + 1 + START)
                for pair in range(3):
                    mm = pe.transpose(b[5][:, pair * P:(pair + 1) * P],
                                      GR[:, 2 * pair:2 * pair + 2, :].rearrange("p h d -> p (h d)"), K.ident[:, :])
                mm.then_inc(q["s5_done"], 1)

            pe.wait_ge(q["xn_ready"], 1 + START)
            xT(0)
            pe.wait_ge(q["small"], 16 * 18 + START)
            pe.wait_ge(w_loaded, 16 * 4 * DC + START)
            with pe.Fori(0, NLAT // 2) as j:
                for u in range(2):
                    tile(j * 2 + u, u, False)
            tile(CTX, 0, True)


def cache_phase(nc, A, K, S, l):
    with ExitStack() as x:
        s = Scope(nc, x, f"cache{l}")
        wukv = s.sb("wukv", [P, 4 * P])
        kg = s.sb("kg", [P, QK])
        ck = s.sb("ck", [P, KVR])
        kr = s.sb("kr", [P, ROPE])
        gk = s.sb("gk", [P, 2, HD])
        gv = s.sb("gv", [P, 2, HD])
        ckT = s.sb("ckT", [P, P])
        KV = s.sb("KV", [P, 4, P])
        sq = s.sb("sq", [P, 4, NOPE])
        sqr = s.sb("sqr", [P, ROPE])
        krss = s.sb("krss", [P, 1])
        ss, v, r, tmp = (s.sb(n, [P, 4]) for n in ("ss", "v", "r", "tmp"))
        KN = s.sb("KN", [P, 4, QK])
        KST = s.sb("KST", [QK, 4, P])
        GST = s.sb("GST", [HD, 2, P])
        pt, pkv, pk, pgk = (s.ps(n, [P, 512]) for n in ("pt", "pkv", "pk", "pgk"))
        loaded, turned, copied, kv_done, sq_ready, kn_ready, kt_done, st_ready, stored, ach, dch = (
            s.sem(n) for n in ("loaded", "turned", "copied", "kv_done", "sq_ready", "kn_ready", "kt_done",
                               "st_ready", "stored", "act_steps", "dve_steps"))
        block = s.block()

        @block.sync
        def _(sp):
            with nc.allow_non_contiguous_dma(reason="broadcast gain"):
                sp.dma_start(ck[:, :], A["cache_mla_ckv"][0, l]).then_inc(loaded, 16)
                sp.dma_start(kr[:, :], A["cache_mla_krope"][0, l]).then_inc(loaded, 16)
                sp.dma_start(gk[:, :, :], A["cache_gqa_k"][0, l]).then_inc(loaded, 16)
                sp.dma_start(gv[:, :, :], A["cache_gqa_v"][0, l]).then_inc(loaded, 16)
                sp.dma_start(wukv[:, :], A["mla_w_ukv"][l]).then_inc(loaded, 16)
                sp.dma_start(kg[:, :], A["mla_k_head_g"][l].partition_broadcast(P)).then_inc(loaded, 16)
            sp.wait_ge(loaded, 96 + START)
            for rep in range(2):
                sp.dma_start(S.V[4 + rep:NH:2, :, 0, :].rearrange("h p d -> p h d"), gv[:, :, :]).then_inc(stored, 16)
            sp.wait_ge(sq_ready, 1 + START)
            sp.dma_start(S.V[0:4, :, 0, :].rearrange("h p d -> p h d"), KV[:, :, NOPE:P]).then_inc(stored, 16)
            sp.wait_ge(st_ready, 1 + START)
            sp.dma_start(S.KT[0:4, :, 0:P].rearrange("h r t -> r h t"), KST[:, :, :]).then_inc(stored, 16)
            for rep in range(2):
                sp.dma_start(S.KT[4 + rep:NH:2, 0:HD, 0:P].rearrange("h r t -> r h t"), GST[:, :, :]).then_inc(stored, 16)
            sp.wait_ge(stored, 96 + START)

        @block.tensor
        def _(pe):
            pe.wait_ge(loaded, 96 + START)
            pe.transpose(pt[:, 0:P], ck[:, :], K.ident[:, :]).then_inc(turned, 1)
            pe.wait_ge(copied, 1 + START)
            pe.matmul(pkv[:, :], ckT[:, :], wukv[:, :], start=True, stop=True).then_inc(kv_done, 1)
            for h in range(2):
                pe.transpose(pgk[0:HD, h * P:(h + 1) * P], gk[:, h, :], K.ident[:, :])
            pe.wait_ge(kn_ready, 1 + START)
            for h in range(4):
                mm = pe.transpose(pk[0:QK, h * P:(h + 1) * P], KN[:, h, :], K.ident[:, :])
            mm.then_inc(kt_done, 1)

        @block.scalar
        def _(act):
            step = Chain(act, ach)
            act.wait_ge(loaded, 96 + START)
            act.wait_ge(turned, 1 + START)
            emit(act.activation(ckT[:, :], pt[:, 0:P], ACT.Copy), copied, act, 1)
            act.wait_ge(kv_done, 1 + START)
            step(act.activation(KV[:, :, :], pkv[:, :], ACT.Copy))
            step(act.activation(sqr[:, :], kr[:, :], ACT.Square, accum_out=krss[:, :]))
            emit(act.activation(sq[:, :, :], KV[:, :, 0:NOPE], ACT.Square), sq_ready, act, 1)
            act.wait_ge(kt_done, 1 + START)
            step(act.activation(KST[:, :, :], pk[0:QK, :], ACT.Copy))
            emit(act.activation(GST[:, :, :], pgk[0:HD, 0:2 * P], ACT.Copy), st_ready, act, 1)

        @block.vector
        def _(dve):
            step = Chain(dve, dch)
            dve.wait_ge(sq_ready, 1 + START)
            step(dve.tensor_reduce(ss[:, :], sq[:, :, :], AX.X, ALU.add))
            step(dve.tensor_scalar(ss[:, :], ss[:, :], krss[:, 0:1], None, ALU.add))
            step(dve.tensor_scalar(v[:, :], ss[:, :], 1.0 / QK, EPS, ALU.mult, ALU.add))
            rsqrt_steps(dve, step, r[:, :], v[:, :], tmp[:, :])
            step(dve.tensor_tensor(KN[:, :, 0:NOPE], KV[:, :, 0:NOPE], r[:, :].unsqueeze(2).broadcast_to([P, 4, NOPE]), ALU.mult))
            step(dve.tensor_tensor(KN[:, :, NOPE:QK], kr[:, :].unsqueeze(1).broadcast_to([P, 4, ROPE]),
                                   r[:, :].unsqueeze(2).broadcast_to([P, 4, ROPE]), ALU.mult))
            emit(dve.tensor_tensor(KN[:, :, :], KN[:, :, :], kg[:, :].unsqueeze(1).broadcast_to([P, 4, QK]), ALU.mult),
                 kn_ready, dve, 1)


def scan_phase(nc, A, K, S, l):
    W4 = 4 * HD
    AFTER, BEFORE, UPTO, FROM = range(4)
    with ExitStack() as xs_:
        s = Scope(nc, xs_, f"scan{l}")
        dt = s.sb("dt", [P, NT, 8])
        dA = s.sb("dA", [P, NT, 8])
        Sb = [s.sb(f"Sb{i}", [P, W4]) for i in range(2)]
        Sp = [s.sb(f"Sp{i}", [P, 2 * W4]) for i in range(2)]
        Sc = s.sb("Sc", [P, W4])
        init = s.sb("init", [P, 2, W4])
        _scan_prepare(nc, A, K, S, l, dt, dA, Sb, Sp, init)
        _scan_backward(nc, A, K, S, l, dt, dA, Sb, Sc, init)
        _scan_forward(nc, A, K, S, l, dt, dA, Sp, Sc, init)


def _scan_prepare(nc, A, K, S, l, dt, dA, Sb, Sp, init):
    with ExitStack() as x:
        s = Scope(nc, x, f"prep{l}")
        n8 = [P, NT, 8]
        bias = s.sb("bias", [P, 8])
        al = s.sb("al", [P, 8])
        t, u, d, e, g = (s.sb(n, n8) for n in ("t", "u", "d", "e", "g"))
        si = s.sb("si", [P, 2, 2, P])
        pt = s.ps("pt", [P, 512])
        loaded, zeroed, s_loaded, t_ready, u_ready, ln_ready, turned, dch = (
            s.sem(n) for n in ("loaded", "zeroed", "s_loaded", "t_ready", "u_ready", "ln_ready", "turned", "dve_steps"))
        block = s.block()

        @block.sync
        def _(sp):
            with nc.allow_non_contiguous_dma(reason="narrow rows"):
                sp.dma_start(dt[:, :, :], S.DT.rearrange("(n p) c -> p n c", p=P)).then_inc(loaded, 16)
                sp.dma_start(bias[:, :], A["ssd_dt_bias"][l].rearrange("d h -> (d h)").partition_broadcast(P)).then_inc(loaded, 16)
                sp.dma_start(al[:, :], A["ssd_a_log"][l].rearrange("d h -> (d h)").partition_broadcast(P)).then_inc(loaded, 16)
                sp.wait_ge(zeroed, 1 + START)
                for dr in range(2):
                    for grp in range(2):
                        sp.dma_start(si[:, dr, grp, grp * HD:(grp + 1) * HD],
                                     A["state_ssd"][0, l, dr, 2 * grp:2 * grp + 2].rearrange("h p n -> (h p) n")).then_inc(s_loaded, 16)

        @block.gpsimd
        def _(pool):
            for i in range(2):
                pool.memset(Sb[i][:, :], 0.0)
                pool.memset(Sp[i][:, :], 0.0)
            pool.memset(si[:, :, :, :], 0.0).then_inc(zeroed, 1)

        @block.tensor
        def _(pe):
            pe.wait_ge(s_loaded, 64 + START)
            for i in range(4):
                mm = pe.transpose(pt[:, i * P:(i + 1) * P], si[:, i // 2, i % 2, :], K.ident[:, :])
            mm.then_inc(turned, 1)

        @block.scalar
        def _(act):
            act.wait_ge(t_ready, 1 + START)
            act.activation(t[:, :, :], t[:, :, :], ACT.Exp)
            act.activation(al[:, :], al[:, :], ACT.Exp).then_inc(u_ready, 1)
            act.wait_ge(t_ready, 2 + START)
            act.activation(g[:, :, :], u[:, :, :], ACT.Ln).then_inc(ln_ready, 1)

        @block.vector
        def _(dve):
            step = Chain(dve, dch)
            dve.wait_ge(loaded, 48 + START)
            step(dve.tensor_tensor(dt[:, :, :], dt[:, :, :], bias[:, :].unsqueeze(1).broadcast_to(n8), ALU.add))
            emit(dve.scalar_tensor_tensor(t[:, :, :], dt[:, :, :], -1.0, dt[:, :, :], ALU.mult, ALU.min), t_ready, dve, 1)
            dve.wait_ge(u_ready, 1 + START)
            emit(dve.tensor_scalar(u[:, :, :], t[:, :, :], 1.0, None, ALU.add), t_ready, dve, 2)
            step(dve.tensor_scalar(d[:, :, :], u[:, :, :], -1.0, None, ALU.add))
            step(dve.tensor_scalar(e[:, :, :], d[:, :, :], 0.0, None, ALU.is_equal))
            step(dve.tensor_tensor(d[:, :, :], d[:, :, :], e[:, :, :], ALU.add))
            step(dve.reciprocal(d[:, :, :], d[:, :, :]))
            dve.wait_ge(ln_ready, 1 + START)
            step(dve.tensor_tensor(g[:, :, :], g[:, :, :], e[:, :, :], ALU.add))
            step(dve.tensor_tensor(g[:, :, :], g[:, :, :], t[:, :, :], ALU.mult))
            step(dve.tensor_tensor(g[:, :, :], g[:, :, :], d[:, :, :], ALU.mult))
            step(dve.scalar_tensor_tensor(dt[:, :, :], dt[:, :, :], 0.0, g[:, :, :], ALU.max, ALU.add))
            step(dve.scalar_tensor_tensor(dA[:, :, :], dt[:, :, :], -1.0, al[:, :].unsqueeze(1).broadcast_to(n8),
                                          ALU.mult, ALU.mult))
            dve.wait_ge(turned, 1 + START)
            step(dve.tensor_copy(init[:, :, :], pt[:, :]))


def conv_at(n, half):
    return LAT + 2 * half if is_ctx(n) else n * P + half


def state_update(dve, step, last, new, old, decay, made):
    def v(ap, g):
        return ap[g * HD:(g + 1) * HD, 2 * g * HD:(2 * g + 2) * HD].rearrange("p (h d) -> p h d", h=2)

    for g, order in ((0, step.go), (1, step)):
        dec = decay[g * HD:(g + 1) * HD, 2 * g:2 * g + 2].unsqueeze(2).broadcast_to([HD, 2, HD])
        order(dve.tensor_tensor(v(new, g), v(old, g), dec, ALU.mult))
    step(dve.tensor_tensor(v(new, 0), v(new, 0), v(made, 0), ALU.add))
    last(dve.tensor_tensor(v(new, 1), v(new, 1), v(made, 1), ALU.add))


def _scan_backward(nc, A, K, S, l, dt, dA, Sb, Sc, init):
    W4 = 4 * HD
    AFTER, BEFORE, UPTO, FROM = range(4)
    with ExitStack() as x:
        s = Scope(nc, x, f"back{l}")
        X = [s.sb(f"X{i}", [P, 3, P]) for i in range(2)]
        XT = [s.sb(f"XT{i}", [P, 3 * P]) for i in range(2)]
        ex = [s.sb(f"ex{i}", [P, 8]) for i in range(2)]
        wt = s.sb("wt", [P, 4])
        xw = [s.sb(f"xw{i}", [P, 4, HD]) for i in range(2)]
        pt = [s.ps(f"pt{i}", [P, 512]) for i in range(2)]
        ps = [s.ps(f"ps{i}", [P, 512]) for i in range(2)]
        x_loaded = [s.sem(f"x_loaded{i}") for i in range(2)]
        stored = [s.sem(f"stored{i}") for i in range(2)]
        turned, xt_ready, xw_ready, st_done, s_ready, dch, uch, ach, first = (
            s.sem(n) for n in ("turned", "xt_ready", "xw_ready", "st_done", "s_ready", "dve_steps", "update_steps",
                               "act_steps", "first"))
        block = s.block()

        def walk(eng, body):
            body(0, 0, 1, CTX, NLAT - 1, 1)
            with eng.Fori(0, NLAT // 2 - 1) as j:
                ns = [j * -2 + (NLAT - 1 - u) for u in range(3)]
                for u in range(2):
                    body(j * 2 + (u + 1), 1 - u, j + (u + 1), ns[u], ns[u + 1], j + 2)
            body(NLAT - 1, 1, NLAT // 2, 1, 0, NLAT // 2 + 1)
            body(NLAT, 0, NLAT // 2 + 1, 0, None, 0)

        @block.sync
        def _(sp):
            def load(n, par):
                sp.dma_start(X[par][:, :, :], S.XC[0:3, :, bass.ds(conv_at(n, 1), P)].rearrange("f p t -> p f t")).then_inc(x_loaded[par], 16)

            def body(k, par, n, n_load):
                if n_load is not None:
                    sp.wait_ge(turned, k + 1 + START)
                    load(n_load, par)
                if not is_ctx(n):
                    sp.wait_ge(s_ready, k + START)
                    sp.dma_start(S.SB[bass.ds(n, 1), :, :].rearrange("n p c -> p (n c)"), Sb[par][:, :]).then_inc(stored[par], 16)

            load(CTX, 0)
            load(NLAT - 1, 1)
            body(0, 0, CTX, NLAT - 2)
            with sp.Fori(0, NLAT // 2 - 1) as j:
                for u in range(2):
                    body(j * 2 + (u + 1), 1 - u, j * -2 + (NLAT - 1 - u), j * -2 + (NLAT - 3 - u))
            body(NLAT - 1, 1, 1, None)
            body(NLAT, 0, 0, None)
            for i in range(2):
                sp.wait_ge(stored[i], 16 * NLAT // 2 + START)

        @block.tensor
        def _(pe):
            def turn(k, par, n, cnt, waits=True):
                pe.wait_ge(x_loaded[par], cnt * 16 + START)
                if waits:
                    pe.wait_ge(xt_ready, k - 1 + START)
                for f in range(3):
                    pe.transpose(pt[par][:, f * P:(f + 1) * P], X[par][:, f, :], K.ident[:, :])
                rhs = dA[:, bass.ds(n, 1), 4:8].rearrange("p n c -> p (n c)")
                pe.matmul(pt[par][:, 384:388], K.tri[:, BEFORE, :], rhs, start=True, stop=True)
                pe.matmul(pt[par][:, 388:392], K.ones[:, :], rhs, start=True, stop=True).then_inc(turned, 1)

            def body(k, par, cnt, n, n_next, cnt_next):
                if n_next is not None:
                    turn(k + 1, 1 - par, n_next, cnt_next, not is_ctx(n))
                pe.wait_ge(xw_ready, k + 1 + START)
                pe.matmul(ps[par][:, 0:W4], XT[par][:, 2 * P:3 * P], xw[par][:, :, :].rearrange("p h d -> p (h d)"),
                          start=True, stop=True).then_inc(st_done, 1)

            turn(0, 0, CTX, 1, False)
            walk(pe, body)

        @block.scalar
        def _(act):
            step = Chain(act, ach, 1)

            def body(k, par, cnt, n, n_next, cnt_next):
                step.tile(k)
                act.wait_ge(turned, k + 1 + START)
                if not is_ctx(n):
                    act.wait_ge(s_ready, k - 1 + START)
                step(act.activation(ex[par][:, :], pt[par][:, 384:392], ACT.Exp))
                emit(act.activation(XT[par][:, :], pt[par][:, 0:384], ACT.Copy), xt_ready, act, k + 1)

            walk(act, body)

        @block.vector
        def _(dve):
            emit(dve.tensor_copy(Sc[:, :], Sb[0][:, :]), first, dve, 1)

            def weigh(k, par, n):
                step.tile(k)
                dve.wait_ge(xt_ready, k + 1 + START)
                step(dve.tensor_tensor(wt[:, :], ex[par][:, 0:4], dt[:, bass.ds(n, 1), 4:8].rearrange("p n c -> p (n c)"), ALU.mult))
                emit(dve.tensor_tensor(xw[par][:, :, :], XT[par][:, 0:W4].rearrange("p (h d) -> p h d", h=4),
                                       wt[:, :].unsqueeze(2).broadcast_to([P, 4, HD]), ALU.mult), xw_ready, dve, k + 1)

            def body(k, par, cnt, n, n_next, cnt_next):
                if n_next is not None:
                    weigh(k + 1, 1 - par, n_next)
                update.tile(k)
                dve.wait_ge(st_done, k + 1 + START)
                if is_ctx(n):
                    state_update(dve, update, lambda ins: emit(ins, first, dve, 2), Sc, Sb[par], ex[par][:, 4:8], ps[par])
                    emit(dve.tensor_copy(Sb[1][:, :], init[:, 1, :]), s_ready, dve, 1)
                else:
                    dve.wait_ge(stored[1 - par], (cnt - 1) * 16 + START)
                    state_update(dve, update, lambda ins: emit(ins, s_ready, dve, k + 1), Sb[1 - par], Sb[par],
                                 ex[par][:, 4:8], ps[par])

            step, update = Chain(dve, dch, 1), Chain(dve, uch, 3)
            weigh(0, 0, CTX)
            walk(dve, body)


def _scan_forward(nc, A, K, S, l, dt, dA, Sp, Sc, init):
    W4 = 4 * HD
    AFTER, BEFORE, UPTO, FROM = range(4)
    with ExitStack() as x:
        s = Scope(nc, x, f"fwd{l}")
        X = [s.sb(f"X{i}", [P, 4, P]) for i in range(2)]
        Z = [s.sb(f"Z{i}", [P, 256]) for i in range(2)]
        XT = [s.sb(f"XT{i}", [P, 3 * P]) for i in range(2)]
        ex = [s.sb(f"ex{i}", [P, 16]) for i in range(2)]
        dts = [s.sb(f"dts{i}", [P, 8]) for i in range(2)]
        dAs = [s.sb(f"dAs{i}", [P, 8]) for i in range(2)]
        R = s.sb("R", [P, 2, 4, P])
        L = [s.sb(f"L{i}", [P, 2, 4, P]) for i in range(2)]
        G = s.sb("G", [P, 2, 2, P])
        wt = s.sb("wt", [P, 4])
        xw = s.sb("xw", [P, 4, HD])
        xdt = s.sb("xdt", [P, 2, 4, HD])
        xd = s.sb("xd", [P, 4, HD])
        T = s.sb("T", [P, 8, HD])
        y = s.sb("y", [P, 256])
        OB = [s.sb(f"OB{i}", [P, 256]) for i in range(2)]
        dsk = s.sb("dsk", [P, 4])
        fin = s.sb("fin", [P, 4, HD])
        pA, pG0, pG1, pF, pR, pY, pO, pT = (s.ps(n, [P, 512]) for n in ("pA", "pG0", "pG1", "pF", "pR", "pY", "pO", "pT"))
        small = s.sem("small")
        loaded = [s.sem(f"loaded{i}") for i in range(2)]
        z_loaded = [s.sem(f"z_loaded{i}") for i in range(2)]
        stored = [s.sem(f"stored{i}") for i in range(2)]
        names = ("turned dts_ready R_ready xt_ready G_done seg_done L_ready M_ready y_done off_done y_ready "
                 "xw_ready st_done s_ready fin_turned fin_ready xd_ready f_stored L_half dve_steps dts_steps act_steps").split()
        q = {n: s.sem(n) for n in names}
        block = s.block()

        def walk(eng, body):
            body(0, 0, CTX, 1, 0)
            with eng.Fori(0, NLAT // 2 - 1) as j:
                for u in range(2):
                    body(j * 2 + (u + 1), 1 - u, j * 2 + u, j + 2, j + u)
            body(NLAT - 1, 1, NLAT - 2, NLAT // 2 + 1, NLAT // 2 - 1)
            body(NLAT, 0, NLAT - 1, 0, NLAT // 2)

        def flat(ap):
            return ap.rearrange("p n c -> p (n c)")

        def h4(ap):
            return ap.rearrange("p (h d) -> p h d", d=HD)

        def per_head(ap, w=HD):
            return ap.unsqueeze(2).broadcast_to([P, ap.shape[-1], w])

        def is_last(k):
            return isinstance(k, int) and k == NLAT

        @block.sync
        def _(sp):
            with nc.allow_non_contiguous_dma(reason="broadcast"):
                sp.dma_start(dsk[:, :], A["ssd_d"][l].partition_broadcast(P)).then_inc(small, 16)

            def load(n, par):
                sp.dma_start(X[par][:, :, :], S.XC[:, :, bass.ds(conv_at(n, 1), P)].rearrange("f p t -> p f t")).then_inc(loaded[par], 16)
                if not is_ctx(n):
                    sp.dma_start(Sp[par][:, W4:2 * W4], S.SB[bass.ds(n, 1), :, :].rearrange("n p c -> p (n c)")).then_inc(loaded[par], 16)

            def load_gates(n, par):
                sp.dma_start(Z[par][:, :], S.G[bass.ds(n * P, P), 256:512]).then_inc(z_loaded[par], 16)

            def body(k, par, n, n_load):
                if n_load is not None:
                    sp.wait_ge(q["off_done"], k + 1 + START)
                    load(n_load, par)
                sp.wait_ge(q["y_ready"], k + 1 + START)
                sp.dma_start(S.O[bass.ds(n * P, P), 512:768], OB[par][:, :]).then_inc(stored[par], 16)
                if n_load is not None:
                    load_gates(n_load, par)

            for par, n in enumerate((CTX, 0)):
                load(n, par)
                load_gates(n, par)
            body(0, 0, CTX, 1)
            with sp.Fori(0, NLAT // 2 - 1) as j:
                for u in range(2):
                    body(j * 2 + (u + 1), 1 - u, j * 2 + u, j * 2 + (u + 2))
            body(NLAT - 1, 1, NLAT - 2, None)
            body(NLAT, 0, NLAT - 1, None)
            sp.wait_ge(q["fin_ready"], 1 + START)
            for dr in range(2):
                for g in range(2):
                    sp.dma_start(A["new_state_ssd"][0, l, dr, 2 * g:2 * g + 2].rearrange("h p n -> (h p) n"),
                                 fin[:, 2 * dr + g, :]).then_inc(q["f_stored"], 16)
            sp.wait_ge(stored[0], 16 * (NT + 1) // 2 + START)
            sp.wait_ge(stored[1], 16 * NLAT // 2 + START)
            sp.wait_ge(q["f_stored"], 64 + START)

        @block.tensor
        def _(pe):
            def turn(k, par, n, count):
                pe.wait_ge(loaded[par], count + START)
                for f in range(3):
                    pe.transpose(pA[:, f * P:(f + 1) * P], X[par][:, f, :], K.ident[:, :])
                f4, b4 = flat(dA[:, bass.ds(n, 1), 0:4]), flat(dA[:, bass.ds(n, 1), 4:8])
                for i, (tri, d4) in enumerate(((K.tri[:, AFTER, :], f4), (K.tri[:, UPTO, :], f4),
                                               (K.tri[:, FROM, :], b4), (K.ones[:, :], f4))):
                    mm = pe.matmul(pA[:, 384 + 4 * i:388 + 4 * i], tri, d4, start=True, stop=True)
                mm.then_inc(q["turned"], 1)

            def score(par):
                for g, bank in enumerate((pG0, pG1)):
                    rows = slice(g * HD, (g + 1) * HD)
                    mm = pe.matmul(bank[:, 0:P], X[par][rows, 2, :], X[par][rows, 3, :], start=True, stop=True)
                mm.then_inc(q["G_done"], 1)

            def carried(par):
                pe.matmul(pO[:, :], X[par][:, 3, :], Sp[par][:, :], start=True, stop=True).then_inc(q["off_done"], 1)

            def segments(k):
                pe.wait_ge(q["R_ready"], 2 * k + 2 + START)
                pe.wait_ge(q["L_ready"], k + START)
                pe.matmul(pF[:, :], K.tri[:, AFTER, :], R[:, 0, :, :].rearrange("p h i -> p (h i)"), start=True, stop=True)
                pe.matmul(pR[:, :], K.tri[:, BEFORE, :], R[:, 1, :, :].rearrange("p h i -> p (h i)"),
                          start=True, stop=True).then_inc(q["seg_done"], 1)

            def body(k, par, n, cnt_next, cnt):
                if not is_last(k):
                    pe.wait_ge(q["xt_ready"], k + 1 + START)
                    turn(k + 1, 1 - par, k, 32 * cnt_next - (16 if par == 1 else 0))
                pe.wait_ge(q["xw_ready"], k + 1 + START)
                pe.wait_ge(q["s_ready"], (0 if is_ctx(n) else k + 1) + START)
                pe.matmul(pT[:, 0:W4], XT[par][:, 2 * P:3 * P], xw[:, :, :].rearrange("p h d -> p (h d)"),
                          start=True, stop=True).then_inc(q["st_done"], 1)
                if not is_last(k):
                    segments(k + 1)
                pe.wait_ge(q["M_ready"], k + 1 + START)
                for h in range(4):
                    cols = slice(h * HD, (h + 1) * HD)
                    pe.matmul(pY[:, cols], L[par][:, 0, h, :], xdt[:, 0, h, :], start=True, stop=False)
                    mm = pe.matmul(pY[:, cols], L[par][:, 1, h, :], xdt[:, 1, h, :], start=False, stop=True)
                mm.then_inc(q["y_done"], 1)
                if is_ctx(n):
                    pe.wait_ge(q["s_ready"], 1 + START)
                    for i in range(4):
                        src = Sp[1][:, :] if i < 2 else Sc[:, :]
                        mm = pe.transpose(pT[:, i * P:(i + 1) * P], src[:, (i % 2) * P:(i % 2 + 1) * P], K.ident[:, :])
                    mm.then_inc(q["fin_turned"], 1)
                    pe.wait_ge(q["fin_ready"], 1 + START)
                if not is_last(k):
                    score(1 - par)
                    pe.wait_ge(q["s_ready"], k + 2 + START)
                    carried(1 - par)

            turn(0, 0, CTX, 16)
            score(0)
            carried(0)
            segments(0)
            walk(pe, body)

        @block.scalar
        def _(act):
            step = Chain(act, q["act_steps"], 1)

            def copy(k, par):
                act.wait_ge(q["turned"], k + 1 + START)
                step.tile(k)
                step(act.activation(ex[par][:, :], pA[:, 384:400], ACT.Exp))
                emit(act.activation(XT[par][:, :], pA[:, 0:384], ACT.Copy), q["xt_ready"], act, k + 1)

            def decays(k, par):
                act.wait_ge(q["seg_done"], k + 1 + START)
                act.wait_ge(q["y_done"], (0 if isinstance(k, int) and k == 0 else k - 1) + START)
                emit(act.activation(L[par][:, 0, :, :], pF[:, :], ACT.Exp), q["L_half"], act, k + 1)
                emit(act.activation(L[par][:, 1, :, :], pR[:, :], ACT.Exp), q["L_ready"], act, k + 1)

            def body(k, par, n, cnt_next, cnt):
                if not is_last(k):
                    act.wait_ge(q["s_ready"], (0 if is_ctx(n) else k + 1) + START)
                    copy(k + 1, 1 - par)
                    decays(k + 1, 1 - par)
                if is_ctx(n):
                    act.wait_ge(q["fin_turned"], 1 + START)
                    for i in range(4):
                        g = i % 2
                        ins = act.activation(fin[:, i, :], pT[:, i * P + g * HD:i * P + (g + 1) * HD], ACT.Copy)
                    emit(ins, q["fin_ready"], act, 1)

            copy(0, 0)
            decays(0, 0)
            walk(act, body)

        @block.gpsimd
        def _(pool):
            def rows(k, par):
                pool.wait_ge(q["dts_ready"], k + 1 + START)
                pool.wait_ge(q["seg_done"], k + START)
                for dr, tri in ((0, UPTO), (1, FROM)):
                    emit(pool.tensor_tensor(R[:, dr, :, :], K.tri[:, tri, :].unsqueeze(1).broadcast_to([P, 4, P]),
                                            per_head(dAs[par][:, 4 * dr:4 * dr + 4], P), ALU.mult),
                         q["R_ready"], pool, 2 * k + 1 + dr)

            def body(k, par, n, cnt_next, cnt):
                if not is_last(k):
                    rows(k + 1, 1 - par)
                pool.wait_ge(q["xt_ready"], k + 1 + START)
                pool.wait_ge(q["y_ready"], k + START)
                emit(pool.tensor_tensor(xd[:, :, :], h4(XT[par][:, 0:W4]), per_head(dsk[:, :]), ALU.mult),
                     q["xd_ready"], pool, k + 1)

            rows(0, 0)
            pool.wait_ge(small, 16 + START)
            walk(pool, body)

        @block.vector
        def _(dve):
            step = Chain(dve, q["dve_steps"], 15)
            ahead = Chain(dve, q["dts_steps"], 1)

            def steps_of(k, par, n):
                ahead.tile(k)
                ahead(dve.tensor_copy(dts[par][:, :], flat(dt[:, bass.ds(n, 1), :])))
                emit(dve.tensor_copy(dAs[par][:, :], flat(dA[:, bass.ds(n, 1), :])), q["dts_ready"], dve, k + 1)

            def body(k, par, n, cnt_next, cnt):
                step.tile(k)
                dve.wait_ge(q["xt_ready"], k + 1 + START)
                xs, e = h4(XT[par][:, 0:W4]), ex[par]
                step.go(dve.tensor_tensor(wt[:, :], dts[par][:, 0:4], e[:, 0:4], ALU.mult))
                for dr, order in ((0, step.go), (1, step)):
                    order(dve.tensor_tensor(xdt[:, dr, :, :], xs, per_head(dts[par][:, 4 * dr:4 * dr + 4]), ALU.mult))
                emit(dve.tensor_tensor(xw[:, :, :], xs, per_head(wt[:, :]), ALU.mult), q["xw_ready"], dve, k + 1)
                if not (isinstance(k, int) and k >= NLAT - 1):
                    dve.wait_ge(q["R_ready"], 2 * k + 2 + START)
                    steps_of(k + 2, par, k + 1)
                dve.wait_ge(q["G_done"], k + 1 + START)
                for g, bank in enumerate((pG0, pG1)):
                    for dr, tri in ((0, UPTO), (1, FROM)):
                        (step if g and dr else step.go)(dve.tensor_tensor(G[:, dr, g, :], bank[:, 0:P], K.tri[:, tri, :], ALU.mult))
                dve.wait_ge(q["L_ready"], k + 1 + START)
                for dr in range(2):
                    Lv = L[par][:, dr, :, :].rearrange("p (g r) i -> p g r i", g=2)
                    ins = dve.tensor_tensor(Lv, Lv, G[:, dr, :, :].unsqueeze(2).broadcast_to([P, 2, 2, P]), ALU.mult)
                    if dr == 0:
                        step(ins)
                    else:
                        emit(ins, q["M_ready"], dve, k + 1)
                dve.wait_ge(q["off_done"], k + 1 + START)
                step(dve.tensor_tensor(T[:, :, :], h4(pO[:, :]), per_head(e[:, 4:12]), ALU.mult))
                step(dve.tensor_tensor(T[:, 0:4, :], T[:, 0:4, :], T[:, 4:8, :], ALU.add))
                dve.wait_ge(q["xd_ready"], k + 1 + START)
                step(dve.tensor_tensor(T[:, 0:4, :], T[:, 0:4, :], xd[:, :, :], ALU.add))
                dve.wait_ge(q["st_done"], k + 1 + START)
                if not is_ctx(n):
                    state_update(dve, step, lambda i: emit(i, q["s_ready"], dve, k + 2), Sp[1 - par], Sp[par], e[:, 12:16], pT)
                else:
                    state_update(dve, step, lambda i: emit(i, q["s_ready"], dve, 1), Sp[1], Sp[0], e[:, 12:16], pT)
                dve.wait_ge(q["y_done"], k + 1 + START)
                step(dve.tensor_tensor(y[:, :], pY[:, 0:256], T[:, 0:4, :].rearrange("p h d -> p (h d)"), ALU.add))
                dve.wait_ge(z_loaded[par], cnt * 16 + 16 + START)
                dve.wait_ge(stored[par], cnt * 16 + START)
                emit(dve.scalar_tensor_tensor(OB[par][:, :], y[:, :], 0.5, Z[par][:, :], ALU.mult, ALU.mult), q["y_ready"], dve, k + 1)
                if is_ctx(n):
                    dve.wait_ge(q["fin_turned"], 1 + START)
                    emit(dve.tensor_copy(Sp[1][:, 0:W4], init[:, 0, :]), q["s_ready"], dve, 2)
                step.end()

            steps_of(0, 0, CTX)
            steps_of(1, 1, 0)
            walk(dve, body)


def attention_phase(nc, A, K, S, l):
    NKT = NLAT + 1
    KEYS = NKT * P
    R1 = QK + 1
    NB = 4
    BODY = 2 * NB
    NPAIR = (NKT + 1) // 2
    CH = [436, 436, 436, 436, 432]
    CA = [0, 436, 872, 1308, 1744]
    NCH = 4 * len(CH)
    CHUNKS_AT = [2, 3, 3, 3, 3, 2, 2, 2, 0]
    POOL_PAIRS = (2, 3)
    DP = [p for p in range(NPAIR) if p not in POOL_PAIRS]
    ND, NPP = len(DP), len(POOL_PAIRS)
    with ExitStack() as x:
        s = Scope(nc, x, f"attn{l}")
        kraw = s.sb("kraw", [QK, KEYS])
        qraw = s.sb("qraw", [QK, LAT])
        Kh = [s.sb(f"Kh{i}", [R1, KEYS], F32R) for i in range(2)]
        Kl = [s.sb(f"Kl{i}", [R1, KEYS], F32R) for i in range(2)]
        Qh = [s.sb(f"Qh{i}", [R1, LAT], F32R) for i in range(2)]
        Ql = [s.sb(f"Ql{i}", [R1, LAT], F32R) for i in range(2)]
        V = [s.sb(f"V{i}", [P, NKT, HD]) for i in range(2)]
        Pb = [s.sb(f"Pb{i}", [P, 1024]) for i in range(3)]
        acc = [s.sb(f"acc{i}", [P, 512]) for i in range(2)]
        pacc = [s.sb(f"pacc{i}", [P, 512]) for i in range(2)]
        OTs = s.sb("OTs", [P, 512])
        mx = s.sb("mx", [P, 4, len(CH)])
        mt = s.sb("mt", [P, 4, R1])
        den = s.sb("den", [P, 4])
        Ost = [s.sb(f"Ost{i}", [P, 4, HD]) for i in range(2)]
        p1 = [s.ps(f"p1{i}", [P, 512]) for i in range(2)]
        ST = [s.ps(f"ST{i}", [P, 1024]) for i in range(2)]
        OT = s.ps("OT", [P, 512])
        misc = s.ps("misc", [P, 512])
        names = ("k_loaded q_loaded v_loaded0 v_loaded1 init hi_ready split_ready st_done exp_done pv_done acc_done pacc_done "
                 "p1_done red_done negm_ready mrow_done mrow_ready ot_copied fin_done o_ready stored0 stored1 "
                 "dve_steps dve_first half_added pool_steps pool_first").split()
        q = {n: s.sem(n) for n in names}
        block = s.block()

        def walk(eng, body):
            with eng.Fori(0, 3) as j:
                body(j, False)
            body(3, True)

        @block.sync
        def _(sp):
            def body(j, final):
                for hb in range(2):
                    for b in range(NB):
                        i = NB * hb + b
                        sp.wait_ge(q["o_ready"], j * BODY + i + 1 + START)
                        sp.dma_start(S.O[b * 512:(b + 1) * 512, bass.ds((j * 2 + hb) * HD, HD)].rearrange("(t p) d -> p t d", p=P),
                                     Ost[b % 2][:, :, :]).then_inc(q[f"stored{b % 2}"], 16)

            walk(sp, body)
            for i in range(2):
                sp.wait_ge(q[f"stored{i}"], 16 * NH * NB // 2 + START)

        @block.gpsimd
        def _(pool):
            init = Chain(pool, q["init"])
            init(pool.memset(mt[:, :, :], 0.0))
            for i in range(2):
                init(pool.memset(Kh[i][QK:R1, :].bitcast(F32), 1.0))
                init(pool.memset(Kl[i][QK:R1, :].bitcast(F32), 0.0))
                init(pool.memset(Ql[i][QK:R1, :].bitcast(F32), 0.0))
            pool.wait_ge(q["hi_ready"], 1 + START)
            first = Chain(pool, q["pool_first"])
            first(pool.tensor_tensor(Kl[0][0:QK, :], kraw[:, :], Kh[0][0:QK, :].bitcast(F32), ALU.subtract))
            emit(pool.tensor_tensor(Ql[0][0:QK, :], qraw[:, :], Qh[0][0:QK, :].bitcast(F32), ALU.subtract), q["split_ready"], pool, 1)
            step = Chain(pool, q["pool_steps"], 3)
            padd = Chain(pool, q["pacc_done"], 2 * NPP - 1)

            def split(h, par, b):
                if b == 0:
                    pool.wait_ge(q["k_loaded"], h * 16 + 16 + START)
                    step(pool.tensor_tensor(Kh[par][0:QK, :], kraw[:, :], K.ones[0:QK, 0:1].broadcast_to([QK, KEYS]), ALU.mult))
                    step(pool.tensor_tensor(Kl[par][0:QK, :], kraw[:, :], Kh[par][0:QK, :].bitcast(F32), ALU.subtract))
                elif b == 1:
                    pool.wait_ge(q["q_loaded"], h * 16 + 16 + START)
                    step(pool.tensor_tensor(Qh[par][0:QK, :], qraw[:, :], K.ones[0:QK, 0:1].broadcast_to([QK, LAT]), ALU.mult))
                else:
                    emit(pool.tensor_tensor(Ql[par][0:QK, :], qraw[:, :], Qh[par][0:QK, :].bitcast(F32), ALU.subtract),
                         q["split_ready"], pool, h + 1)

            def body(j, final):
                for i in range(BODY):
                    B, par, b = j * BODY + i, i // NB, i % NB
                    for k, p in enumerate(POOL_PAIRS):
                        pool.wait_ge(q["exp_done"], B * NPAIR + p + 1 + START)
                        if k == 0:
                            padd.tile(B)
                            if i >= 2:
                                pool.wait_ge(q["acc_done"], (B - 1) * ND + START)
                            padd(pool.tensor_tensor(pacc[i % 2][:, :], Pb[p % 3][:, 0:512], Pb[p % 3][:, 512:1024], ALU.add))
                        else:
                            for half in range(2):
                                padd(pool.tensor_tensor(pacc[i % 2][:, :], pacc[i % 2][:, :],
                                                        Pb[p % 3][:, half * 512:(half + 1) * 512], ALU.add))
                    if b < 3 and not (final and par):
                        if b == 0:
                            step.tile(j * 2 + par)
                            pool.wait_ge(q["pv_done"], B * NPAIR + START)
                        split(j * 2 + par + 1, 1 - par, b)

            walk(pool, body)

        @block.tensor
        def _(pe):
            def first_pass(B, par, b, c):
                t, k = divmod(c, len(CH))
                if c >= 2:
                    pe.wait_ge(q["red_done"], B * NCH + c - 1 + START)
                else:
                    pe.wait_ge(q["red_done"], B * NCH + START)
                q0 = b * 512 + t * P
                pe.matmul(p1[c % 2][:, 0:CH[k]], Qh[par][0:QK, q0:q0 + P], Kh[par][0:QK, CA[k]:CA[k] + CH[k]],
                          start=True, stop=True).then_inc(q["p1_done"], 1)

            def max_row(B):
                pe.wait_ge(q["negm_ready"], B + 1 + START)
                for t in range(4):
                    mm = pe.matmul(misc[0:R1, t * P:(t + 1) * P], mt[:, t, :], K.ident[:, :], start=True, stop=True)
                mm.then_inc(q["mrow_done"], 1)

            def finish(B, i, t):
                if t == 0:
                    pe.wait_ge(q["ot_copied"], B + 1 + START)
                    pe.wait_ge(q["acc_done"], B * ND + ND + START)
                at, cols = t * (HD + 1), slice(t * P, (t + 1) * P)
                pe.matmul(misc[:, at:at + HD], OTs[:, cols], K.ident2[:, :], start=True, stop=True)
                mm = pe.matmul(misc[:, at + HD:at + HD + 1], acc[i % 2][:, cols], K.ones[:, 0:1], start=True, stop=True)
                if t == 3:
                    mm.then_inc(q["fin_done"], 1)

            def scores(B, i, b, par, kt):
                out = ST[(i + kt // 2) % 2][:, (kt % 2) * 512:(kt % 2 + 1) * 512]
                ks, qs = slice(kt * P, (kt + 1) * P), slice(b * 512, (b + 1) * 512)
                pe.matmul(out, Kh[par][:, ks], Qh[par][:, qs], start=True, stop=False)
                pe.matmul(out, Kh[par][:, ks], Ql[par][:, qs], start=False, stop=False)
                mm = pe.matmul(out, Kl[par][:, ks], Qh[par][:, qs], start=False, stop=True)
                if kt % 2 or kt == NKT - 1:
                    mm.then_inc(q["st_done"], 1)

            def pv(B, par, kt):
                p, o = kt // 2, kt % 2
                if o == 0:
                    pe.wait_ge(q["exp_done"], B * NPAIR + p + 1 + START)
                    if p == 0:
                        pe.wait_ge(q["ot_copied"], B + START)
                mm = pe.matmul(OT[o * HD:(o + 1) * HD, :], V[par][:, kt, :], Pb[p % 3][:, o * 512:(o + 1) * 512],
                               start=(kt < 2), stop=(kt >= NKT - 2))
                if o or kt == NKT - 1:
                    mm.then_inc(q["pv_done"], 1)

            pe.wait_ge(q["hi_ready"], 1 + START)
            for c in range(NCH):
                first_pass(0, 0, 0, c)
            max_row(0)
            pe.wait_ge(q["split_ready"], 1 + START)

            def body(j, final):
                for i in range(BODY):
                    B, par, b = j * BODY + i, i // NB, i % NB
                    last = final and i == BODY - 1
                    npar, nb = ((i + 1) % BODY) // NB, (i + 1) % NB
                    pe.wait_ge(q["mrow_ready"], B + 1 + START)
                    if b == 0:
                        pe.wait_ge(q[f"v_loaded{par}"], j * 16 + 16 + START)
                    c = 0
                    for p in range(NPAIR):
                        if p > 0:
                            pe.wait_ge(q["exp_done"], B * NPAIR + p - 1 + START)
                        elif i > 0:
                            pe.wait_ge(q["exp_done"], B * NPAIR - 1 + START)
                        else:
                            pe.wait_ge(q["exp_done"], B * NPAIR + START)
                        chunks = 0 if last else CHUNKS_AT[p]
                        if chunks and p == 0 and nb == 0:
                            pe.wait_ge(q["split_ready"], j * 2 + par + 2 + START)
                        for o in range(2):
                            if 2 * p + o < NKT:
                                scores(B, i, b, par, 2 * p + o)
                            if o < chunks:
                                first_pass(B + 1, npar, nb, c)
                                c += 1
                            if p in (2, 3) and i > 0:
                                finish(B - 1, i - 1, 2 * (p - 2) + o)
                        if p == NPAIR - 1 and not last:
                            pe.wait_ge(q["o_ready"], B + START)
                            max_row(B + 1)
                        if p > 0:
                            pv(B, par, 2 * p - 2)
                            pv(B, par, 2 * p - 1)
                        if chunks > 2:
                            first_pass(B + 1, npar, nb, c)
                            c += 1
                    pv(B, par, NKT - 1)
                if not final:
                    pe.wait_ge(q["mrow_ready"], j * BODY + BODY + 1 + START)
                else:
                    pe.wait_ge(q["o_ready"], j * BODY + BODY - 1 + START)
                for t in range(4):
                    finish(j * BODY + BODY - 1, BODY - 1, t)

            walk(pe, body)

        @block.scalar
        def _(act):
            def row(B, b, par):
                act.wait_ge(q["mrow_done"], B + 1 + START)
                emit(act.activation(Qh[par][QK:R1, b * 512:(b + 1) * 512], misc[QK:R1, :], ACT.Copy), q["mrow_ready"], act, B + 1)

            def load(h, par):
                act.dma_start(kraw[:, :], S.KT[bass.ds(h, 1), :, 0:KEYS].rearrange("h r t -> r (h t)")).then_inc(q["k_loaded"], 16)
                act.dma_start(qraw[:, :], S.QT[bass.ds(h, 1), :, 0:LAT].rearrange("h r t -> r (h t)")).then_inc(q["q_loaded"], 16)
                act.dma_start(V[par][:, :, :], S.V[bass.ds(h, 1), :, 0:NKT, :].rearrange("h p s d -> p (h s d)")).then_inc(q[f"v_loaded{par}"], 16)

            load(0, 0)
            row(0, 0, 0)

            def copy_ot(B):
                act.wait_ge(q["pv_done"], B * NPAIR + NPAIR + START)
                act.wait_ge(q["fin_done"], B + START)
                act.activation(OTs[:, :], OT[:, :], ACT.Copy).then_inc(q["ot_copied"], 1)

            def body(j, final):
                for i in range(BODY):
                    B, par, b = j * BODY + i, i // NB, i % NB
                    last = final and i == BODY - 1
                    for p in range(NPAIR):
                        w = 1024 if p < NPAIR - 1 else 512
                        act.wait_ge(q["st_done"], B * NPAIR + p + 1 + START)
                        if p >= 3:
                            act.wait_ge(q["pv_done"], B * NPAIR + p - 2 + START)
                            if p - 3 in POOL_PAIRS:
                                act.wait_ge(q["pacc_done"], B * (2 * NPP - 1) + 2 * POOL_PAIRS.index(p - 3) + 1 + START)
                            else:
                                act.wait_ge(q["acc_done"], B * ND + DP.index(p - 3) + 1 + START)
                        elif i > 0:
                            act.wait_ge(q["pv_done"], B * NPAIR - 2 + p + START)
                            act.wait_ge(q["acc_done"], B * ND - 2 + p + START)
                        else:
                            act.wait_ge(q["pv_done"], B * NPAIR + START)
                            act.wait_ge(q["acc_done"], B * ND + START)
                        act.activation(Pb[p % 3][:, 0:w], ST[(i + p) % 2][:, 0:w], ACT.Exp).then_inc(q["exp_done"], 1)
                        if p == 0:
                            if i > 0:
                                copy_ot(B - 1)
                            if b == 0 and not (final and par):
                                act.wait_ge(q["split_ready"], j * 2 + par + 1 + START)
                                act.wait_ge(q["pv_done"], B * NPAIR + START)
                                load(j * 2 + par + 1, 1 - par)
                        if p == NPAIR - 1 and not last:
                            row(B + 1, (i + 1) % NB, ((i + 1) % BODY) // NB)
                copy_ot(j * BODY + BODY - 1)

            walk(act, body)

        @block.vector
        def _(dve):
            step = Chain(dve, q["dve_steps"], 0)

            def reduce(B, c):
                t, k = divmod(c, len(CH))
                dve.wait_ge(q["p1_done"], B * NCH + c + 1 + START)
                dve.tensor_reduce(mx[:, t, k:k + 1], p1[c % 2][:, 0:CH[k]], AX.X, ALU.max).then_inc(q["red_done"], 1)

            def maxima(B):
                dve.wait_ge(q["red_done"], B * NCH + NCH + START)
                dve.tensor_reduce(mt[:, :, QK:R1], mx[:, :, :], AX.X, ALU.max, negate=True).then_inc(q["negm_ready"], 1)

            def output(B, i):
                dve.wait_ge(q["fin_done"], B + 1 + START)
                dve.wait_ge(q[f"stored{i % 2}"], out_count(B, i) + START)
                o = misc[:, 0:4 * (HD + 1)].rearrange("p (t d) -> p t d", d=HD + 1)
                emit(dve.reciprocal(den[:, :], o[:, :, HD]), q["dve_steps"], dve, B + 1)
                dve.tensor_tensor(Ost[i % 2][:, :, :], o[:, :, 0:HD], den[:, :].unsqueeze(2).broadcast_to([P, 4, HD]), ALU.mult)\
                    .then_inc(q["o_ready"], 1)

            def out_count(B, i):
                return (B - i) * 8 + (i // 2) * 16

            first = Chain(dve, q["dve_first"])
            dve.wait_ge(q["k_loaded"], 16 + START)
            first(dve.tensor_copy(Kh[0][0:QK, :], kraw[:, :]))
            dve.wait_ge(q["q_loaded"], 16 + START)
            emit(dve.tensor_copy(Qh[0][0:QK, :], qraw[:, :]), q["hi_ready"], dve, 1)
            dve.wait_ge(q["init"], 1 + START)
            for c in range(NCH):
                reduce(0, c)
            maxima(0)

            half_added = Chain(dve, q["half_added"], ND - 1)

            def add(B, i, p):
                sums, pair = acc[i % 2], Pb[p % 3]
                dve.wait_ge(q["exp_done"], B * NPAIR + p + 1 + START)
                if p == 0:
                    if i >= 2:
                        dve.wait_ge(q["fin_done"], B - 1 + START)
                    half_added.tile(B)
                    ins = dve.tensor_tensor(sums[:, :], pair[:, 0:512], pair[:, 512:1024], ALU.add)
                else:
                    if p < NPAIR - 1:
                        half_added(dve.tensor_tensor(sums[:, :], sums[:, :], pair[:, 512:1024], ALU.add))
                    else:
                        dve.wait_ge(q["pacc_done"], (B + 1) * (2 * NPP - 1) + START)
                        half_added(dve.tensor_tensor(sums[:, :], sums[:, :], pacc[i % 2][:, :], ALU.add))
                    ins = dve.tensor_tensor(sums[:, :], sums[:, :], pair[:, 0:512], ALU.add)
                emit(ins, q["acc_done"], dve, B * ND + DP.index(p) + 1)

            def body(j, final):
                for i in range(BODY):
                    B = j * BODY + i
                    last = final and i == BODY - 1
                    c = 0
                    for p in range(NPAIR):
                        chunks = 0 if last else CHUNKS_AT[p]
                        if chunks:
                            reduce(B + 1, c)
                            c += 1
                        if chunks == 2:
                            reduce(B + 1, c)
                            c += 1
                            if p == NPAIR - 2:
                                maxima(B + 1)
                        if p > 0 and p - 1 not in POOL_PAIRS:
                            add(B, i, p - 1)
                        if chunks == 3:
                            for _ in range(2):
                                reduce(B + 1, c)
                                c += 1
                        if p == 4 and i > 0:
                            output(B - 1, i - 1)
                    add(B, i, NPAIR - 1)
                output(j * BODY + BODY - 1, BODY - 1)

            walk(dve, body)


def context_attention_phase(nc, A, K, S, l):
    with ExitStack() as x:
        s = Scope(nc, x, f"cattn{l}")
        Q = s.sb("Q", [QK, NH, P])
        Kt = s.sb("Kt", [QK, NH, P])
        V = s.sb("V", [P, NH, HD])
        mx = s.sb("mx", [P, NH])
        sums = s.sb("sums", [P, NH])
        Pr = s.sb("Pr", [P, NH, P])
        PT = s.sb("PT", [P, NH, P])
        O = s.sb("O", [P, NH, HD])
        pS, pT = s.ps("pS", [P, NH * P]), s.ps("pT", [P, NH * P])
        pO = s.ps("pO", [P, NH * HD])
        loaded, s_done, mx_ready, e_ready, t_done, t_ready, pv_done, r_ready, o_ready, stored = (
            s.sem(n) for n in ("loaded", "s_done", "mx_ready", "e_ready", "t_done", "t_ready", "pv_done", "r_ready",
                               "o_ready", "stored"))
        block = s.block()

        @block.sync
        def _(sp):
            sp.dma_start(Q[:, :, :], S.QT[:, :, CTX * P:].rearrange("h r t -> r h t")).then_inc(loaded, 16)
            sp.dma_start(Kt[:, :, :], S.KT[:, :, (CTX + 1) * P:].rearrange("h r t -> r h t")).then_inc(loaded, 16)
            sp.dma_start(V[:, :, :], S.V[:, :, CTX + 1, :].rearrange("h p d -> p h d")).then_inc(loaded, 16)
            sp.wait_ge(o_ready, 1 + START)
            sp.dma_start(S.O[CTX * P:, 0:NH * HD], O[:, :, :].rearrange("p h d -> p (h d)")).then_inc(stored, 16)
            sp.wait_ge(stored, 16 + START)

        @block.tensor
        def _(pe):
            pe.wait_ge(loaded, 48 + START)
            for h in range(NH):
                mm = pe.matmul(pS[:, h * P:(h + 1) * P], Q[:, h, :], Kt[:, h, :], start=True, stop=True)
            mm.then_inc(s_done, 1)
            pe.wait_ge(e_ready, NH + START)
            for h in range(NH):
                mm = pe.transpose(pT[:, h * P:(h + 1) * P], Pr[:, h, :], K.ident[:, :])
            mm.then_inc(t_done, 1)
            pe.wait_ge(t_ready, 1 + START)
            for h in range(NH):
                mm = pe.matmul(pO[:, h * HD:(h + 1) * HD], PT[:, h, :], V[:, h, :], start=True, stop=True)
            mm.then_inc(pv_done, 1)

        @block.scalar
        def _(act):
            act.wait_ge(mx_ready, 1 + START)
            for h in range(NH):
                act.activation(Pr[:, h, :], pS[:, h * P:(h + 1) * P], ACT.Exp, bias=mx[:, h:h + 1],
                               accum_out=sums[:, h:h + 1]).then_inc(e_ready, 1)
            act.wait_ge(t_done, 1 + START)
            act.activation(PT[:, :, :], pT[:, :], ACT.Copy).then_inc(t_ready, 1)

        @block.vector
        def _(dve):
            dve.wait_ge(s_done, 1 + START)
            dve.tensor_reduce(mx[:, :], pS[:, :].rearrange("p (h k) -> p h k", k=P), AX.X, ALU.max, negate=True).then_inc(mx_ready, 1)
            dve.wait_ge(e_ready, NH + START)
            dve.reciprocal(sums[:, :], sums[:, :]).then_inc(r_ready, 1)
            dve.wait_ge(r_ready, 1 + START)
            dve.wait_ge(pv_done, 1 + START)
            dve.tensor_tensor(O[:, :, :], pO[:, :].rearrange("p (h d) -> p h d", d=HD),
                              sums[:, :].unsqueeze(2).broadcast_to([P, NH, HD]), ALU.mult).then_inc(o_ready, 1)


def output_phase(nc, A, K, S, l, xin, xout, w_in=None, w_in_loaded=None):
    with ExitStack() as x:
        s = Scope(nc, x, f"out{l}")
        wr = [s.sb(f"wr{i}", [P, D]) for i in range(2)]
        wh, wl = s.sb("wh", [P, DC, D], F32R), s.sb("wl", [P, DC, D], F32R)
        O = [s.sb(f"O{i}", [P, 768]) for i in range(2)]
        C = [s.sb(f"C{i}", [P, 2, P]) for i in range(2)]
        cst = s.sb("cst", [P, 6])
        mv = s.sb("mv", [P, 2])
        md = s.sb("md", [P, 1])
        vv, rr, tt = (s.sb(n, [P, 2]) for n in ("vv", "rr", "tt"))
        ct, cth, c1, sq = (s.sb(n, [P, 256]) for n in ("ct", "cth", "c1", "sq"))
        ng, lg, lb = (s.sb(n, [P, 256]) for n in ("ng", "lg", "lb"))
        G = [s.sb(f"G{i}", [P, D]) for i in range(2)]
        X = [s.sb(f"X{i}", [P, D]) for i in range(2)]
        og = [s.sb(f"og{i}", [P, D]) for i in range(2)]
        oTh = [s.sb(f"oTh{i}", [P, DC, P], F32R) for i in range(2)]
        oTl = [s.sb(f"oTl{i}", [P, DC, P], F32R) for i in range(2)]
        Y = [s.sb(f"Y{i}", [P, D]) for i in range(2)]
        pT = [s.ps(f"pT{i}", [P, D]) for i in range(2)]
        pY = [s.ps(f"pY{i}", [P, D]) for i in range(2)]
        raw = wr + Y
        w_loaded = [s.sem(f"w_loaded{i}") for i in range(len(raw))]
        w_high, w_low, pg_ready, lo_ready = (s.sem(n) for n in ("w_high", "w_low", "pg_ready", "lo_ready"))
        loaded = [s.sem(f"loaded{i}") for i in range(2)]
        x_loaded = [s.sem(f"x_loaded{i}") for i in range(2)]
        stored = [s.sem(f"stored{i}") for i in range(2)]
        og_ready, t_done, ot_ready, y_done, y_ready, dch, tch, gains, halved, ct_done, sq_ready, c_ready, cth_ready = (
            s.sem(n) for n in ("og_ready", "t_done", "ot_ready", "y_done", "y_ready", "dve_steps", "scaled", "gains",
                               "halved", "ct_done", "sq_ready", "c_ready", "cth_ready"))
        block = s.block()

        def walk(eng, body):
            for n in range(2):
                body(n, n, 0, False)
            with eng.Fori(0, NLAT // 2 - 1) as j:
                for u in range(2):
                    body(j * 2 + (u + 2), u, j + 1, False)
            body(CTX, 0, NLAT // 2, True)

        @block.sync
        def _(sp):
            def load(n, par):
                rows = bass.ds(n * P, P)
                sp.dma_start(C[par][:, :, :], S.YC[:, :, bass.ds(conv_at(n, KW // 2), P)].rearrange("f p t -> p f t")).then_inc(loaded[par], 16)
                sp.dma_start(O[par][:, :], S.O[rows, :]).then_inc(loaded[par], 16)
                sp.dma_start(G[par][:, :], S.G[rows, :]).then_inc(loaded[par], 16)

            def load_x(n, par):
                sp.dma_start(X[par][:, :], xin[bass.ds(n * P, P), :]).then_inc(x_loaded[par], 16)

            load(0, 0)
            load_x(0, 0)
            load(1, 1)
            with nc.allow_non_contiguous_dma(reason="broadcast gains"):
                for t_, src in ((ng, "ssd_norm_g"), (lg, "cf_ln_g"), (lb, "cf_ln_b")):
                    sp.dma_start(t_[:, :], A[src][l].partition_broadcast(P)).then_inc(gains, 16)
            for c in range(DC):
                if c >= len(raw):
                    sp.wait_ge(w_low, c - len(raw) + 1 + START)
                sp.dma_start(raw[c % len(raw)][:, :], A["w_out"][l, c * P:(c + 1) * P, :]).then_inc(w_loaded[c % len(raw)], 16)

            def body(n, par, load_b, load_xt):
                if load_b:
                    sp.wait_ge(og_ready, n + 1 + START)
                    sp.wait_ge(pg_ready, 2 * n + 2 + START)
                    load(n + 2, par)
                if load_xt:
                    sp.wait_ge(y_ready, n + START)
                    load_x(n + 1, 1 - par)
                sp.wait_ge(y_ready, n + 1 + START)
                sp.dma_start(xout[bass.ds(n * P, P), :], Y[par][:, :]).then_inc(stored[par], 16)

            body(0, 0, True, True)
            body(1, 1, True, True)
            if w_in is not None:
                load_input_weights(sp, A, l + 1, w_in, 0, w_in_loaded)
            with sp.Fori(0, NLAT // 2 - 2) as j:
                for u in range(2):
                    body(j * 2 + (u + 2), u, True, True)
            body(NLAT - 2, 0, True, True)
            body(NLAT - 1, 1, False, True)
            body(CTX, 0, False, False)
            sp.wait_ge(stored[0], 16 * (NT + 1) // 2 + START)
            sp.wait_ge(stored[1], 16 * NLAT // 2 + START)

        @block.tensor
        def _(pe):
            def turn_conv(n, par, cnt):
                pe.wait_ge(loaded[par], cnt * 48 + 48 + START)
                pe.wait_ge(lo_ready, (0 if isinstance(n, int) and n < 2 else n - 1) + START)
                for f in range(2):
                    mm = pe.transpose(pT[par][:, f * P:(f + 1) * P], C[par][:, f, :], K.ident[:, :])
                mm.then_inc(ct_done, 1)

            def turn(n, par):
                pe.wait_ge(og_ready, n + 1 + START)
                pe.wait_ge(pg_ready, 2 * n + 2 + START)
                for c in range(DC):
                    mm = pe.transpose(pT[par][:, c * P:(c + 1) * P], og[par][:, c * P:(c + 1) * P], K.ident[:, :])
                mm.then_inc(t_done, 1)

            def body(n, par, cnt, turn_next=True, conv_next=True):
                pe.wait_ge(lo_ready, n + 1 + START)
                pe.wait_ge(tch, (0 if isinstance(n, int) and n < 2 else n - 1) + START)
                for half in range(2):
                    cols = slice(half * 512, (half + 1) * 512)
                    for c in range(DC):
                        if half and c == DC // 2 and turn_next:
                            turn(n + 1, 1 - par)
                        pe.matmul(pY[par][:, cols], oTh[par][:, c, :], wh[:, c, cols], start=(c == 0), stop=False)
                        pe.matmul(pY[par][:, cols], oTh[par][:, c, :], wl[:, c, cols], start=False, stop=False)
                        mm = pe.matmul(pY[par][:, cols], oTl[par][:, c, :], wh[:, c, cols], start=False, stop=(c == DC - 1))
                mm.then_inc(y_done, 1)
                if conv_next:
                    turn_conv(n + 2, par, cnt + 1)

            turn_conv(0, 0, 0)
            turn(0, 0)
            turn_conv(1, 1, 0)
            pe.wait_ge(w_low, DC + START)
            body(0, 0, 0)
            body(1, 1, 0)
            with pe.Fori(0, NLAT // 2 - 2) as j:
                for u in range(2):
                    body(j * 2 + (u + 2), u, j + 1)
            body(NLAT - 2, 0, NLAT // 2 - 1)
            body(NLAT - 1, 1, NLAT // 2 - 1, True, False)
            body(CTX, 0, NLAT // 2, False, False)

        @block.scalar
        def _(act):
            def square(n, par, cnt):
                act.wait_ge(loaded[par], cnt * 48 + 48 + START)
                emit(act.activation(sq[:, :], O[par][:, 512:768], ACT.Square, accum_out=vv[:, 0:1]), sq_ready, act, n + 1)
                act.wait_ge(c_ready, n + 1 + START)
                emit(act.activation(cth[:, :], ct[:, :], ACT.Tanh), cth_ready, act, n + 1)

            square(0, 0, 0)
            for c in range(DC):
                act.wait_ge(w_loaded[c % len(raw)], 16 * (c // len(raw)) + 16 + START)
                act.activation(wh[:, c, :], raw[c % len(raw)][:, :], ACT.Copy).then_inc(w_high, 1)

            def body(n, par, j, last):
                act.wait_ge(t_done, n + 1 + START)
                act.wait_ge(y_done, (0 if isinstance(n, int) and n < 2 else n - 1) + START)
                act.activation(oTh[par][:, :, :], pT[par][:, :], ACT.Copy).then_inc(ot_ready, 1)
                if not last:
                    square(n + 1, 1 - par, j + par)

            walk(act, body)

        @block.vector
        def _(dve):
            step = Chain(dve, dch, 22)
            setup = Chain(dve, halved)
            dve.wait_ge(gains, 48 + START)
            setup(dve.tensor_scalar(lg[:, :], lg[:, :], 0.5, None, ALU.mult))
            setup(dve.tensor_scalar(lb[:, :], lb[:, :], 0.5, None, ALU.mult))
            setup(dve.tensor_scalar(ng[:, :], ng[:, :], 2.0, None, ALU.mult))

            def gates(n, par, cnt):
                step.tile(n)
                dve.wait_ge(ct_done, n + 1 + START)
                conv = pT[par][:, 0:256]
                step(dve.bn_stats(cst[:, :], conv))
                halves_ = cst[:, :].rearrange("p (o c) -> p o c", o=2)
                step.go(dve.tensor_tensor(mv[:, :], halves_[:, 0, 1:3], halves_[:, 1, 1:3], ALU.add))
                step(dve.tensor_tensor(md[:, 0:1], cst[:, 1:2], cst[:, 4:5], ALU.subtract))
                step(dve.scalar_tensor_tensor(md[:, 0:1], md[:, 0:1], 0.25, md[:, 0:1], ALU.mult, ALU.mult))
                step(dve.scalar_tensor_tensor(md[:, 0:1], mv[:, 1:2], 1.0 / 256, md[:, 0:1], ALU.mult, ALU.add))
                step.go(dve.tensor_scalar(vv[:, 1:2], md[:, 0:1], EPS, None, ALU.add))
                step.go(dve.tensor_scalar(mv[:, 0:1], mv[:, 0:1], 0.5, None, ALU.mult))
                dve.wait_ge(sq_ready, n + 1 + START)
                step(dve.tensor_scalar(vv[:, 0:1], vv[:, 0:1], 1.0 / 256, EPS, ALU.mult, ALU.add))
                rsqrt_steps(dve, step, rr[:, :], vv[:, :], tt[:, :])
                step(dve.tensor_scalar(ct[:, :], conv, mv[:, 0:1], rr[:, 1:2], ALU.subtract, ALU.mult))
                step(dve.tensor_tensor(ct[:, :], ct[:, :], lg[:, :], ALU.mult))
                emit(dve.tensor_tensor(ct[:, :], ct[:, :], lb[:, :], ALU.add), c_ready, dve, n + 1)
                dve.wait_ge(loaded[par], cnt * 48 + 48 + START)
                g, o, out = G[par], O[par], og[par]
                step.go(dve.scalar_tensor_tensor(out[:, 256:512], o[:, 512:768], rr[:, 0:1], ng[:, :], ALU.mult, ALU.mult))
                dve.wait_ge(cth_ready, n + 1 + START)
                step(dve.scalar_tensor_tensor(c1[:, :], cth[:, :], 1.0, ct[:, :], ALU.add, ALU.mult))
                emit(dve.tensor_tensor(out[:, 512:768], g[:, 512:768], c1[:, :], ALU.mult), og_ready, dve, n + 1)

            def low(n, par):
                dve.wait_ge(ot_ready, n + 1 + START)
                emit(dve.tensor_tensor(oTl[par][:, :, :].rearrange("p c t -> p (c t)"), pT[par][:, :],
                                       oTh[par][:, :, :].rearrange("p c t -> p (c t)").bitcast(F32), ALU.subtract),
                     lo_ready, dve, n + 1)

            gates(0, 0, 0)
            for c in range(DC):
                dve.wait_ge(w_high, c + 1 + START)
                emit(dve.tensor_tensor(wl[:, c, :], raw[c % len(raw)][:, :], wh[:, c, :].bitcast(F32), ALU.subtract), w_low, dve, c + 1)
            low(0, 0)

            def body(n, par, j, last):
                if not last:
                    gates(n + 1, 1 - par, j + par)
                    low(n + 1, 1 - par)
                dve.wait_ge(y_done, n + 1 + START)
                dve.wait_ge(stored[par], j * 16 + START)
                emit(dve.tensor_tensor(Y[par][:, :], pY[par][:, :], K.gate[:, 2 * l + (1 if last else 0), :], ALU.mult), tch, dve, n + 1)

            walk(dve, body)

        @block.gpsimd
        def _(pool):
            gated = Chain(pool, pg_ready, 2)

            def gates(n, par, cnt):
                pool.wait_ge(loaded[par], cnt * 48 + 48 + START)
                pool.wait_ge(t_done, (0 if isinstance(n, int) and n < 2 else n - 1) + START)
                gated.tile(n)
                for g0, o0 in ((0, 0), (768, 256)):
                    gated(pool.tensor_tensor(og[par][:, g0:g0 + 256], G[par][:, g0:g0 + 256], O[par][:, o0:o0 + 256], ALU.mult))

            gates(0, 0, 0)

            def body(n, par, j, last):
                if not last:
                    gates(n + 1, 1 - par, j + par)
                pool.wait_ge(tch, n + 1 + START)
                pool.wait_ge(x_loaded[par], j * 16 + 16 + START)
                emit(pool.tensor_tensor(Y[par][:, :], X[par][:, :], Y[par][:, :], ALU.add), y_ready, pool, n + 1)

            walk(pool, body)


INPUTS = {
    "x": (NT * P, D), "cache_mla_ckv": (1, DEPTH, P, KVR), "cache_mla_krope": (1, DEPTH, P, ROPE),
    "cache_gqa_k": (1, DEPTH, P, 2, HD), "cache_gqa_v": (1, DEPTH, P, 2, HD),
    "state_ssd": (1, DEPTH, 2, 4, HD, HD), "c": (1, D), "c_ctx": (D,), "w_mod": (DEPTH, D, 3 * D),
    "b_mod": (DEPTH, 3 * D), "norm_g": (DEPTH, D), "w_in": (DEPTH, D, IN_W), "w_out": (DEPTH, D, D),
    "mla_q_norm_g": (DEPTH, QR), "mla_w_uq": (DEPTH, QR, 4 * QK), "mla_kv_norm_g": (DEPTH, KVR),
    "mla_w_ukv": (DEPTH, KVR, 4 * P), "mla_q_head_g": (DEPTH, QK), "mla_k_head_g": (DEPTH, QK),
    "ssd_conv_w": (DEPTH, 3, 512), "ssd_conv_b": (DEPTH, 512), "ssd_dt_bias": (DEPTH, 2, 4),
    "ssd_a_log": (DEPTH, 2, 4), "ssd_d": (DEPTH, 4), "ssd_norm_g": (DEPTH, 256),
    "cf_conv_w": (DEPTH, KW, 256), "cf_conv_b": (DEPTH, 256), "cf_ln_g": (DEPTH, 256),
    "cf_ln_b": (DEPTH, 256), "gqa_q_g": (DEPTH, HD), "gqa_k_g": (DEPTH, HD), "rope": (NT * P, RT),
}
OUTPUTS = {
    "y": (NT * P, D), "new_mla_ckv": (1, DEPTH, P, KVR), "new_mla_krope": (1, DEPTH, P, ROPE),
    "new_gqa_k": (1, DEPTH, P, 2, HD), "new_gqa_v": (1, DEPTH, P, 2, HD),
    "new_state_ssd": (1, DEPTH, 2, 4, HD, HD),
}


class Scratch:

    def __init__(self, nc):
        def dram(name, *shape):
            return nc.dram_tensor(f"scratch_{name}", shape, F32, kind="Internal").ap()

        self.QT = dram("QT", NH, QK, NT * P)
        self.KT = dram("KT", NH, QK, NSLOT * P)
        self.V = dram("V", NH, P, NSLOT, HD)
        self.G = dram("G", NT * P, D)
        self.DT = dram("DT", NT * P, 8)
        self.XC = dram("XC", 4, P, NT * P + 2)
        self.YC = dram("YC", 2, P, NT * P + 2 * (KW // 2))
        self.SB = dram("SB", NT, P, 256)
        self.O = dram("O", NT * P, 768)
        self.X1 = dram("X1", NT * P, D)


class Persistent:

    def __init__(self, nc, x):
        def sb(name, shape):
            return x.enter_context(nc.sbuf_tensor(name, shape, F32))

        self.ident = sb("ident", [P, P])
        self.ident2 = sb("ident2", [P, HD])
        self.ones = sb("ones", [P, P])
        self.tri = sb("tri", [P, 4, P])
        self.mod = sb("mod", [P, DEPTH, 2, 2 * DC])
        self.gate = sb("gate", [P, 2 * DEPTH, D])


def build(nc, A):
    S = Scratch(nc)
    with ExitStack() as x:
        K = Persistent(nc, x)
        constants_phase(nc, K, S)
        weights = ExitStack()
        w_in = InputWeights(nc, weights, 0)
        for half in range(2):
            w_in.add_half()
        modulation_phase(nc, A, K, S, w_in.halves, w_in.loaded)
        for l in range(DEPTH):
            xin = A["x"] if l == 0 else S.X1
            xout = A["y"] if l == DEPTH - 1 else S.X1
            if l:
                w_in.add_half()
            projection_phase(nc, A, K, S, l, xin, w_in.halves, w_in.loaded, l > 0)
            weights.close()
            cache_phase(nc, A, K, S, l)
            scan_phase(nc, A, K, S, l)
            attention_phase(nc, A, K, S, l)
            context_attention_phase(nc, A, K, S, l)
            if l + 1 < DEPTH:
                w_in = InputWeights(nc, weights, l + 1)
                output_phase(nc, A, K, S, l, xin, xout, w_in.add_half(), w_in.loaded)
            else:
                output_phase(nc, A, K, S, l, xin, xout)
        weights.close()


def kernel(**inputs):
    import concourse.bacc as bacc
    from concourse.bass_utils import run_bass_kernel_spmd

    arrays = {n: np.asarray(inputs[n]) for n in INPUTS if n not in ("x", "rope")}
    arrays["x"] = np.concatenate([np.asarray(inputs["x_sample"])[0], np.asarray(inputs["x_prompt"])[0]], 0)
    arrays["rope"] = rope_table()
    nc = bacc.Bacc("TRN2", target_bir_lowering=False, num_devices=1)
    A, feeds = {}, {}
    for n, shape in INPUTS.items():
        A[n] = nc.dram_tensor(f"in_{n}", shape, F32, kind="ExternalInput").ap()
        feeds[f"in_{n}"] = np.ascontiguousarray(arrays[n])
    for n, shape in OUTPUTS.items():
        A[n] = nc.dram_tensor(f"out_{n}", shape, F32, kind="ExternalOutput").ap()
    build(nc, A)
    r = run_bass_kernel_spmd(nc, [feeds], core_ids=[0]).results[0]
    y = r["out_y"]
    return (y[LAT:][None], y[:LAT][None]) + tuple(r[f"out_{n}"] for n in OUTPUTS if n != "y")
```
